# Optimizing a Trainium2 kernel written in Bass

```python
import math
import jax, jax.numpy as jnp
from jax import lax
import numpy as np

D_MODEL = 1024
BATCH = 1
SEQ = 256
DEPTH = 2

HEAD_DIM = 64
D_MIX = D_MODEL
SSM_WIDTH = D_MIX // 4
SSM_CH = 16
SSM_GROUPS = SSM_WIDTH // SSM_CH
SSM_STATE = 64
ATTN_HEADS = (D_MIX - SSM_WIDTH) // (2 * HEAD_DIM)
MLA_HEADS = ATTN_HEADS
MLA_NOPE = HEAD_DIM
MLA_ROPE = HEAD_DIM // 2
MLA_V = HEAD_DIM
MLA_Q_RANK = 192
MLA_KV_RANK = 128
NSA_HEADS = ATTN_HEADS
NSA_KV_HEADS = 2
NSA_REP = NSA_HEADS // NSA_KV_HEADS
NSA_DIM = HEAD_DIM
CMP_BLOCK = 32
CMP_STRIDE = 16
SEL_BLOCK = 64
SEL_TOPN = 8
WINDOW = 256
REL_BUCKETS = 32
REL_MAX_DIST = 128
XATTN_HEADS = 4
XATTN_DIM = D_MODEL // XATTN_HEADS
MEM_TOKENS = 256
FF_DENSE = 2816
N_EXPERTS = 8
TOP_K = 2
FF_EXPERT = 3584
Q_BLOCK = 128
ROPE_THETA = 10000.0
EPS = 1e-6
NEG_INF = -1e30
FORCE = 1e9
N_DENSE = (DEPTH + 1) // 2
N_MOE = DEPTH // 2
MLA_WIDTH = MLA_HEADS * MLA_V
NSA_WIDTH = NSA_HEADS * NSA_DIM
IN_SPLITS = (SSM_WIDTH, MLA_Q_RANK, MLA_KV_RANK, MLA_ROPE, NSA_HEADS * NSA_DIM,
             6 * NSA_KV_HEADS * NSA_DIM, 3 * NSA_HEADS)
IN_COLS = sum(IN_SPLITS)

kernel_name = "hymba_s5_mla_nsa_moe_trunk"

def rmsnorm(x, g):
    xf = x.astype(jnp.float32)
    y = xf * lax.rsqrt(jnp.mean(xf * xf, axis=-1, keepdims=True) + EPS)
    return (y * g.astype(jnp.float32)).astype(x.dtype)

def softmax32(s):
    return jax.nn.softmax(s.astype(jnp.float32), axis=-1)

def t5_bucket(dist):
    n = jnp.maximum(dist, 0)
    exact = REL_BUCKETS // 2
    nf = jnp.maximum(n, exact).astype(jnp.float32)
    large = exact + (jnp.log(nf / exact) / math.log(REL_MAX_DIST / exact)
                     * (REL_BUCKETS - exact)).astype(jnp.int32)
    return jnp.where(n < exact, n, jnp.minimum(large, REL_BUCKETS - 1))

def rope_tables(seq, dim):
    pos = jnp.arange(seq, dtype=jnp.float32)
    inv = 1.0 / (ROPE_THETA ** (jnp.arange(0, dim, 2, dtype=jnp.float32) / dim))
    ang = pos[:, None] * inv[None, :]
    return jnp.cos(ang), jnp.sin(ang)

def apply_rope(x, cos, sin):
    half = x.shape[-1] // 2
    xf = x.astype(jnp.float32)
    x1, x2 = xf[..., :half], xf[..., half:]
    return jnp.concatenate([x1 * cos - x2 * sin, x2 * cos + x1 * sin], axis=-1).astype(x.dtype)

def _cplx_combine(e1, e2):
    a1r, a1i, b1r, b1i = e1
    a2r, a2i, b2r, b2i = e2
    ar = a2r * a1r - a2i * a1i
    ai = a2r * a1i + a2i * a1r
    br = a2r * b1r - a2i * b1i + b2r
    bi = a2r * b1i + a2i * b1r + b2i
    return (ar, ai, br, bi)

def ssm_mixer(u, a_re, a_im, b_re, b_im, c_re, c_im, d, log_dt, w_glu):
    f32 = jnp.float32
    bsz, seq, _ = u.shape
    ug = u.astype(f32).reshape(bsz, seq, SSM_GROUPS, SSM_CH)
    dt = jnp.exp(log_dt.astype(f32))[:, None]
    lr, li = a_re.astype(f32), a_im.astype(f32)
    mag = jnp.exp(lr * dt)
    ab_r, ab_i = mag * jnp.cos(li * dt), mag * jnp.sin(li * dt)
    den = lr * lr + li * li
    nr = ab_r - 1.0
    f_r = (nr * lr + ab_i * li) / den
    f_i = (ab_i * lr - nr * li) / den
    br, bi = b_re.astype(f32), b_im.astype(f32)
    bb_r = f_r[..., None] * br - f_i[..., None] * bi
    bb_i = f_r[..., None] * bi + f_i[..., None] * br
    bu_r = jnp.einsum('bsgc,gpc->bsgp', ug, bb_r)
    bu_i = jnp.einsum('bsgc,gpc->bsgp', ug, bb_i)
    a_r = jnp.broadcast_to(ab_r, bu_r.shape)
    a_i = jnp.broadcast_to(ab_i, bu_r.shape)
    _, _, h_r, h_i = lax.associative_scan(_cplx_combine, (a_r, a_i, bu_r, bu_i), axis=1)
    y = (jnp.einsum('bsgp,gcp->bsgc', h_r, c_re.astype(f32))
         - jnp.einsum('bsgp,gcp->bsgc', h_i, c_im.astype(f32))
         + d.astype(f32).reshape(SSM_GROUPS, SSM_CH) * ug)
    y = jax.nn.gelu(y.reshape(bsz, seq, SSM_WIDTH)).astype(u.dtype)
    return y * jax.nn.sigmoid(y @ w_glu)

def mla_mixer(cq, ckv, kr, q_norm, w_uq, kv_norm, w_ukv, cos, sin):
    bsz, seq, _ = cq.shape
    q = (rmsnorm(cq, q_norm) @ w_uq).reshape(bsz, seq, MLA_HEADS, MLA_NOPE + MLA_ROPE)
    q_nope = q[..., :MLA_NOPE]
    q_rope = apply_rope(q[..., MLA_NOPE:], cos[:, None, :], sin[:, None, :])
    kv = (rmsnorm(ckv, kv_norm) @ w_ukv).reshape(bsz, seq, MLA_HEADS, MLA_NOPE + MLA_V)
    k_nope, v = kv[..., :MLA_NOPE], kv[..., MLA_NOPE:]
    k_rope = apply_rope(kr, cos, sin)
    scale = (MLA_NOPE + MLA_ROPE) ** -0.5
    kpos = jnp.arange(seq)

    def block(i):
        qs = i * Q_BLOCK
        qn = lax.dynamic_slice_in_dim(q_nope, qs, Q_BLOCK, axis=1)
        qr = lax.dynamic_slice_in_dim(q_rope, qs, Q_BLOCK, axis=1)
        s = (jnp.einsum('bqhd,bkhd->bhqk', qn, k_nope)
             + jnp.einsum('bqhr,bkr->bhqk', qr, k_rope)).astype(jnp.float32) * scale
        t = qs + jnp.arange(Q_BLOCK)
        s = jnp.where(kpos[None, :] <= t[:, None], s, NEG_INF)
        p = softmax32(s).astype(v.dtype)
        return jnp.einsum('bhqk,bkhd->bqhd', p, v)

    o = lax.map(block, jnp.arange(seq // Q_BLOCK))
    return o.transpose(1, 0, 2, 3, 4).reshape(bsz, seq, MLA_WIDTH)

def nsa_compress(k, pe, w1, w2):
    bsz, seq, g, dh = k.shape
    ratio = CMP_BLOCK // CMP_STRIDE
    n_chunk = seq // CMP_STRIDE
    nbc = n_chunk - ratio + 1
    ch = k.reshape(bsz, n_chunk, CMP_STRIDE, g, dh)
    blocks = jnp.concatenate([ch[:, j:j + nbc] for j in range(ratio)], axis=2)
    blocks = blocks + pe[None, None, :, None, :]
    flat = blocks.transpose(0, 1, 3, 2, 4).reshape(bsz, nbc, g, CMP_BLOCK * dh)
    return jax.nn.gelu(flat @ w1) @ w2

def nsa_mixer(q, kv, gate_logits, cmp_pe, cmp_w1, cmp_w2, rel_bias):
    f32 = jnp.float32
    bsz, seq, _ = q.shape
    G, R, dh = NSA_KV_HEADS, NSA_REP, NSA_DIM
    dt = q.dtype
    q = q.reshape(bsz, seq, G, R, dh)
    kv = kv.reshape(bsz, seq, 6, G, dh)
    k_cr, v_cr, k_sl, v_sl, k_wn, v_wn = [kv[:, :, j] for j in range(6)]
    gates = jax.nn.sigmoid(gate_logits.astype(f32)).reshape(bsz, seq, 3, G, R).astype(dt)
    k_c = nsa_compress(k_cr, cmp_pe[0], cmp_w1[0], cmp_w2[0])
    v_c = nsa_compress(v_cr, cmp_pe[1], cmp_w1[1], cmp_w2[1])
    nbc = k_c.shape[1]
    nbs = seq // SEL_BLOCK
    n_sel = min(SEL_TOPN, nbs)
    c_end = jnp.arange(nbc) * CMP_STRIDE + CMP_BLOCK - 1
    ci = jnp.arange(nbc)[:, None]
    sj = jnp.arange(nbs)[None, :]
    overlap = ((ci * CMP_STRIDE <= sj * SEL_BLOCK + SEL_BLOCK - 1)
               & (ci * CMP_STRIDE + CMP_BLOCK - 1 >= sj * SEL_BLOCK)).astype(f32)
    k_sb = k_sl.reshape(bsz, nbs, SEL_BLOCK, G, dh).transpose(0, 3, 1, 2, 4)
    v_sb = v_sl.reshape(bsz, nbs, SEL_BLOCK, G, dh).transpose(0, 3, 1, 2, 4)
    pad = ((0, 0), (WINDOW, 0), (0, 0), (0, 0))
    k_wp = jnp.pad(k_wn, pad)
    v_wp = jnp.pad(v_wn, pad)
    rb_h = rel_bias.astype(f32)
    rb_grn = rb_h.reshape(REL_BUCKETS, G, R).transpose(1, 2, 0)
    b_ix = jnp.arange(bsz)[:, None, None, None]
    g_ix = jnp.arange(G)[None, :, None, None]
    gi5 = jnp.arange(G)[None, :, None, None, None]
    ri5 = jnp.arange(R)[None, None, :, None, None]
    scale = dh ** -0.5
    span = Q_BLOCK + WINDOW

    def head_bias(dist):
        return rb_h[t5_bucket(dist)].reshape(*dist.shape, G, R).transpose(2, 3, 0, 1)

    def block(i):
        qs = i * Q_BLOCK
        t = qs + jnp.arange(Q_BLOCK)
        qb = lax.dynamic_slice_in_dim(q, qs, Q_BLOCK, axis=1)
        gb = lax.dynamic_slice_in_dim(gates, qs, Q_BLOCK, axis=1)
        dist_c = t[:, None] - c_end[None, :]
        ok_c = dist_c >= 0
        s_c = jnp.einsum('bqgrd,bngd->bgrqn', qb, k_c).astype(f32) * scale + head_bias(dist_c)
        p_c = softmax32(jnp.where(ok_c, s_c, NEG_INF)) * ok_c.any(-1)[:, None].astype(f32)
        o_c = jnp.einsum('bgrqn,bngd->bqgrd', p_c.astype(dt), v_c)
        imp = jnp.einsum('bgrqn,nm->bgqm', p_c, overlap)
        cur = t // SEL_BLOCK
        forced = (sj == 0) | (sj == cur[:, None]) | (sj == cur[:, None] - 1)
        future = sj * SEL_BLOCK > t[:, None]
        imp = jnp.where(forced, FORCE, jnp.where(future, -FORCE, imp))
        _, idx = lax.top_k(imp, n_sel)
        k_g = k_sb[b_ix, g_ix, idx].reshape(bsz, G, Q_BLOCK, n_sel * SEL_BLOCK, dh)
        v_g = v_sb[b_ix, g_ix, idx].reshape(bsz, G, Q_BLOCK, n_sel * SEL_BLOCK, dh)
        kpos = (idx[..., None] * SEL_BLOCK + jnp.arange(SEL_BLOCK)).reshape(bsz, G, Q_BLOCK, n_sel * SEL_BLOCK)
        dist_s = t[:, None] - kpos
        bias_s = rb_grn[gi5, ri5, t5_bucket(dist_s)[:, :, None]]
        s_s = jnp.einsum('bqgrd,bgqmd->bgrqm', qb, k_g).astype(f32) * scale + bias_s
        p_s = softmax32(jnp.where((dist_s >= 0)[:, :, None], s_s, NEG_INF))
        o_s = jnp.einsum('bgrqm,bgqmd->bqgrd', p_s.astype(dt), v_g)
        k_w = lax.dynamic_slice_in_dim(k_wp, qs, span, axis=1)
        v_w = lax.dynamic_slice_in_dim(v_wp, qs, span, axis=1)
        kpos_w = qs - WINDOW + jnp.arange(span)
        dist_w = t[:, None] - kpos_w[None, :]
        ok_w = (dist_w >= 0) & (dist_w < WINDOW) & (kpos_w >= 0)[None, :]
        s_w = jnp.einsum('bqgrd,blgd->bgrql', qb, k_w).astype(f32) * scale + head_bias(dist_w)
        p_w = softmax32(jnp.where(ok_w, s_w, NEG_INF))
        o_w = jnp.einsum('bgrql,blgd->bqgrd', p_w.astype(dt), v_w)
        o = (gb[:, :, 0][..., None] * o_c + gb[:, :, 1][..., None] * o_s
             + gb[:, :, 2][..., None] * o_w)
        return o.reshape(bsz, Q_BLOCK, G * R * dh)

    o = lax.map(block, jnp.arange(seq // Q_BLOCK))
    return o.transpose(1, 0, 2, 3).reshape(bsz, seq, NSA_WIDTH)

def cross_attn(h, mem, g_x, g_mem, wq, wkv, wo):
    bsz, seq, _ = h.shape
    m = mem.shape[1]
    q = (rmsnorm(h, g_x) @ wq).reshape(bsz, seq, XATTN_HEADS, XATTN_DIM)
    kv = (rmsnorm(mem, g_mem) @ wkv).reshape(bsz, m, 2, XATTN_HEADS, XATTN_DIM)
    k, v = kv[:, :, 0], kv[:, :, 1]
    s = jnp.einsum('bshd,bmhd->bhsm', q, k).astype(jnp.float32) * XATTN_DIM ** -0.5
    p = softmax32(s).astype(v.dtype)
    o = jnp.einsum('bhsm,bmhd->bshd', p, v).reshape(bsz, seq, XATTN_HEADS * XATTN_DIM)
    return o @ wo

def swiglu(x, wg, wu, wd):
    return (jax.nn.silu(x @ wg) * (x @ wu)) @ wd

def moe_swiglu(x, router, wg, wu, wd):
    bsz, seq, d = x.shape
    xt = x.reshape(-1, d)
    logits = (xt @ router).astype(jnp.float32)
    top_v, top_i = lax.top_k(logits, TOP_K)
    w = jax.nn.softmax(top_v, axis=-1)
    comb = jnp.sum(jax.nn.one_hot(top_i, N_EXPERTS, dtype=jnp.float32) * w[..., None], axis=1)
    comb = comb.astype(xt.dtype)
    out = jnp.zeros_like(xt)
    for e in range(N_EXPERTS):
        out = out + comb[:, e:e + 1] * swiglu(xt, wg[e], wu[e], wd[e])
    return out.reshape(bsz, seq, d)

def setup_inputs(seed: int = 0) -> dict:
    key = jax.random.key(seed)
    ks = iter(jax.random.split(key, 48))
    f32 = jnp.float32
    L, G, P, C = DEPTH, SSM_GROUPS, SSM_STATE, SSM_CH

    def nrm(shape, scale):
        return jax.random.normal(next(ks), shape, f32) * scale

    def gain(shape):
        return 1.0 + nrm(shape, 0.02)

    return {
        "x": nrm((BATCH, SEQ, D_MODEL), 1.0),
        "mem": nrm((BATCH, MEM_TOKENS, D_MODEL), 1.0),
        "w_in": nrm((L, D_MODEL, IN_COLS), D_MODEL ** -0.5),
        "w_out": nrm((L, D_MIX, D_MODEL), D_MIX ** -0.5),
        "mix_norm": gain((L, D_MODEL)),
        "out_norm": gain((L, D_MIX)),
        "ssm_a_re": -0.5 + nrm((L, G, P), 0.01),
        "ssm_a_im": jnp.pi * jnp.arange(P, dtype=f32) + nrm((L, G, P), 0.01),
        "ssm_b_re": nrm((L, G, P, C), C ** -0.5),
        "ssm_b_im": nrm((L, G, P, C), C ** -0.5),
        "ssm_c_re": nrm((L, G, C, P), P ** -0.5),
        "ssm_c_im": nrm((L, G, C, P), P ** -0.5),
        "ssm_d": nrm((L, SSM_WIDTH), 1.0),
        "ssm_log_dt": jax.random.uniform(next(ks), (L, G), f32, math.log(1e-3), math.log(1e-1)),
        "ssm_w_glu": nrm((L, SSM_WIDTH, SSM_WIDTH), SSM_WIDTH ** -0.5),
        "mla_q_norm": gain((L, MLA_Q_RANK)),
        "mla_w_uq": nrm((L, MLA_Q_RANK, MLA_HEADS * (MLA_NOPE + MLA_ROPE)), MLA_Q_RANK ** -0.5),
        "mla_kv_norm": gain((L, MLA_KV_RANK)),
        "mla_w_ukv": nrm((L, MLA_KV_RANK, MLA_HEADS * (MLA_NOPE + MLA_V)), MLA_KV_RANK ** -0.5),
        "nsa_cmp_pe": nrm((L, 2, CMP_BLOCK, NSA_DIM), 0.1),
        "nsa_cmp_w1": nrm((L, 2, CMP_BLOCK * NSA_DIM, NSA_DIM), (CMP_BLOCK * NSA_DIM) ** -0.5),
        "nsa_cmp_w2": nrm((L, 2, NSA_DIM, NSA_DIM), NSA_DIM ** -0.5),
        "rel_bias": nrm((REL_BUCKETS, NSA_HEADS), 0.5),
        "xattn_norm": gain((L, D_MODEL)),
        "mem_norm": gain((L, D_MODEL)),
        "xattn_wq": nrm((L, D_MODEL, XATTN_HEADS * XATTN_DIM), D_MODEL ** -0.5),
        "xattn_wkv": nrm((L, D_MODEL, 2 * XATTN_HEADS * XATTN_DIM), D_MODEL ** -0.5),
        "xattn_wo": nrm((L, XATTN_HEADS * XATTN_DIM, D_MODEL), D_MODEL ** -0.5),
        "ffn_norm": gain((L, D_MODEL)),
        "dense_w_gate": nrm((N_DENSE, D_MODEL, FF_DENSE), D_MODEL ** -0.5),
        "dense_w_up": nrm((N_DENSE, D_MODEL, FF_DENSE), D_MODEL ** -0.5),
        "dense_w_down": nrm((N_DENSE, FF_DENSE, D_MODEL), FF_DENSE ** -0.5),
        "moe_router": nrm((N_MOE, D_MODEL, N_EXPERTS), D_MODEL ** -0.5),
        "moe_w_gate": nrm((N_MOE, N_EXPERTS, D_MODEL, FF_EXPERT), D_MODEL ** -0.5),
        "moe_w_up": nrm((N_MOE, N_EXPERTS, D_MODEL, FF_EXPERT), D_MODEL ** -0.5),
        "moe_w_down": nrm((N_MOE, N_EXPERTS, FF_EXPERT, D_MODEL), FF_EXPERT ** -0.5),
        "final_norm": gain((D_MODEL,)),
    }

def reference(x, mem, w_in, w_out, mix_norm, out_norm, ssm_a_re, ssm_a_im, ssm_b_re, ssm_b_im,
              ssm_c_re, ssm_c_im, ssm_d, ssm_log_dt, ssm_w_glu, mla_q_norm, mla_w_uq, mla_kv_norm,
              mla_w_ukv, nsa_cmp_pe, nsa_cmp_w1, nsa_cmp_w2, rel_bias, xattn_norm, mem_norm, xattn_wq,
              xattn_wkv, xattn_wo, ffn_norm, dense_w_gate, dense_w_up, dense_w_down, moe_router,
              moe_w_gate, moe_w_up, moe_w_down, final_norm):
    seq = x.shape[1]
    cos, sin = rope_tables(seq, MLA_ROPE)
    offsets = np.cumsum(IN_SPLITS)[:-1].tolist()
    o1 = SSM_WIDTH
    o2 = SSM_WIDTH + MLA_WIDTH
    h = x
    for l in range(DEPTH):
        proj = rmsnorm(h, mix_norm[l]) @ w_in[l]
        u, cq, ckv, kr, nq, nkv, ngate = jnp.split(proj, offsets, axis=-1)
        y_ssm = ssm_mixer(u, ssm_a_re[l], ssm_a_im[l], ssm_b_re[l], ssm_b_im[l], ssm_c_re[l],
                          ssm_c_im[l], ssm_d[l], ssm_log_dt[l], ssm_w_glu[l])
        y_mla = mla_mixer(cq, ckv, kr, mla_q_norm[l], mla_w_uq[l], mla_kv_norm[l], mla_w_ukv[l], cos, sin)
        y_nsa = nsa_mixer(nq, nkv, ngate, nsa_cmp_pe[l], nsa_cmp_w1[l], nsa_cmp_w2[l], rel_bias)
        g = out_norm[l]
        y = jnp.concatenate([rmsnorm(y_ssm, g[:o1]), rmsnorm(y_mla, g[o1:o2]),
                             rmsnorm(y_nsa, g[o2:])], axis=-1)
        h = h + y @ w_out[l]
        h = h + cross_attn(h, mem, xattn_norm[l], mem_norm[l], xattn_wq[l], xattn_wkv[l], xattn_wo[l])
        hn = rmsnorm(h, ffn_norm[l])
        if l % 2 == 0:
            h = h + swiglu(hn, dense_w_gate[l // 2], dense_w_up[l // 2], dense_w_down[l // 2])
        else:
            h = h + moe_swiglu(hn, moe_router[l // 2], moe_w_gate[l // 2], moe_w_up[l // 2],
                               moe_w_down[l // 2])
    return rmsnorm(h, final_norm)


_drawn_inputs = setup_inputs


def setup_inputs(seed=0):
    import zlib

    import numpy as np

    out = dict(_drawn_inputs(seed))
    spreads = {}
    factors = {'ssm_a_re': 23.238,
     'mla_q_norm': 3.098,
     'xattn_norm': 8.0,
     'mem_norm': 8.0,
     'final_norm': 7.202,
     'ffn_norm': 3.914}
    for name, (base, spread) in spreads.items():
        noise = np.random.default_rng([zlib.crc32(name.encode()), seed]).standard_normal(out[name].shape)
        drawn = base * np.exp(spread * noise) if base else spread * noise
        out[name] = __import__('jax').numpy.asarray(drawn.astype(out[name].dtype))
    for name, factor in factors.items():
        out[name] = (out[name] * factor).astype(out[name].dtype)
    return out
```

```python
import math
from contextlib import ExitStack

import concourse.bass as bass
from concourse import mybir
import numpy as np

ALU = mybir.AluOpType
ACT = mybir.ActivationFunctionType
AX = mybir.AxisListType
F32 = mybir.dt.float32
U32 = mybir.dt.uint32
I32 = mybir.dt.int32

P = 128
D = 1024
KD = D // P
T = 256
TT = T // P
L = 2
NH = 6
HD = 64
NOPE, ROPE = 64, 32
QK = NOPE + ROPE
NCMP = 15
CSTRIDE = 16
NPAIR = 16
XH = 4
FD, FE = 2816, 3584
NE = 8
PIECE = 256
DENSE_PIECES, MOE_PIECES = FD // PIECE, FE // PIECE
EPS = 1e-6
NEG = -1e30
BUCKETS, MAX_DIST = 32, 128

RING = 6
SLOT = 2048
COMMON = 27
DENSE_CHUNKS = 3 * DENSE_PIECES
MOE_CHUNKS = 3 * MOE_PIECES
LAYER_CHUNKS = COMMON + DENSE_CHUNKS
assert LAYER_CHUNKS % RING == 0 and MOE_CHUNKS % RING == 0
CHUNKS = LAYER_CHUNKS + COMMON + NE * MOE_CHUNKS
MOE_FIRST = LAYER_CHUNKS + COMMON

LP = {}
_at = 0
for _n, _w in (("cols", 101), ("glu", 2 * 256), ("uq", 2 * 576), ("ukv", 768), ("w1", 2 * NPAIR * 64), ("w2", 2 * 64),
               ("bt", 2048), ("ct", 2 * 8 * 32)):
    LP[_n] = (_at, _w)
    _at += _w
LPW = _at
C_MIX, C_OUT, C_XN, C_MEM, C_FFN = 0, 8, 16, 24, 32
C_ARE, C_AIM, C_LDT, C_D, C_KVN, C_QN, C_PE = 40, 48, 56, 64, 66, 67, 69
assert C_PE + 2 * NPAIR == LP["cols"][1]
CS = {}
_at = 0
for _n, _w in (("ident", 128), ("cmask", 256), ("rope", 64), ("before", 128), ("ones", 128), ("iota", 256), ("iota8", 8),
               ("okc", 2), ("vcm", 6), ("half", 4), ("router", 64)):
    CS[_n] = (_at, _w)
    _at += _w
CSW = _at

ROT = 5
JOBS = []


def _job(name, eng, chunk=None):
    JOBS.append((name, eng, chunk))


for _i in range(4):
    _job(f"hT{_i}", "act")
for _i, (_n, _e) in enumerate((("u", "act"), ("zA", "act"), ("zB", "act"), ("q0", "dve"), ("q1", "dve"))):
    _job(_n, _e, _i)
_job("ck", "act")
_job("cv", "dve", 5)
_job("vs", "dve", 6)
for _n, _e in (("cqT", "act"), ("ckvT", "act"), ("hid", "dve"), ("qn0", "act"), ("qr0", "dve"), ("qn1", "act"),
               ("qr1", "dve"), ("kn0", "act"), ("kn1", "act"), ("kn2", "act"), ("vm0", "act"), ("vm1", "act"),
               ("kcv", "dve"), ("qT0", "act"), ("qT1", "act"), ("qT2", "act"), ("sc", "dve"), ("pcT", "act"),
               ("oc0", "dve"), ("oc1", "dve")):
    _job(_n, _e)
HEADS = 18
LEAD = 3
MEMK = {0: 0, 2: 1, 4: 2, 6: 3}
MEMV = {8: 0, 11: 1}
STATES = {1 + 2 * _i: _i for _i in range(8)}
for _i in range(LEAD):
    _job(f"s{_i}", "dve")
for _i in range(HEADS):
    if _i + LEAD < HEADS:
        _job(f"s{_i + LEAD}", "dve")
    if _i in MEMK:
        _job(f"mk{MEMK[_i]}", "act", 7 + MEMK[_i])
    if _i in MEMV:
        _job(f"mv{MEMV[_i]}_0", "act")
        _job(f"mv{MEMV[_i]}_1", "act", 12 + 2 * MEMV[_i])
    if _i in STATES:
        _job(f"bu{STATES[_i]}", "dve")
    _job(f"pT{_i}", "act")
_job("yr", "dve")
_job("gl", "act")
for _i in range(4):
    _job(f"yT{_i}", "act")
for _i in range(2):
    _job(f"wo{_i}_0", "dve")
    _job(f"wo{_i}_1", "dve", 16 + 2 * _i)
for _i in range(4):
    _job(f"xT{_i}", "act")
for _i in range(4):
    _job(f"xq{_i}", "act", 19 + _i)
for _i in range(XH):
    _job(f"xs{_i}", "act")
for _i in range(XH):
    _job(f"xp{_i}", "dve")
    _job(f"xo{_i}", "act")
for _i in range(2):
    _job(f"xw{_i}_0", "dve")
    _job(f"xw{_i}_1", "dve", 24 + 2 * _i)
for _i in range(4):
    _job(f"fT{_i}", "act")
NAMES = [j[0] for j in JOBS]
assert len(set(NAMES)) == len(NAMES)
DRAINS = {e: [j[0] for j in JOBS if j[1] == e] for e in ("act", "dve")}
PLAIN = [j[0] for j in JOBS if j[2] is None]


def trunk(nc, x, mem, weights, lparams, consts, onehot, relb, fgain, out, scratch):
    with ExitStack() as ctx:
        def sb(name, shape, dt=F32):
            return ctx.enter_context(nc.sbuf_tensor(name, shape, dt))

        def sem(name):
            return ctx.enter_context(nc.semaphore(name))

        ring = sb("ring", [P, RING, SLOT])
        h = sb("h", [P, TT, D])
        row = sb("row", [P, TT, D])
        col = sb("col", [P, KD, T])
        memraw = sb("memraw", [P, KD, T])
        btab = sb("btab", [P, NH, T])
        cst = sb("cst", [P, CSW])
        lp = sb("lp", [P, LPW])
        big = sb("big", [P, 2, 8, T])
        g = sb("g", [P, 2, 2, T])
        ql = sb("ql", [P, 2, T])
        ckvT = sb("ckvT", [P, T])
        qT = sb("qT", [QK, NH, T])
        kT = sb("kT", [QK, NH, T])
        vm = sb("vm", [P, TT, 384])
        uT = sb("uT", [P, 2, T])
        qz = sb("qz", [P, NH, T])
        kslT = sb("kslT", [P, T])
        kwnT = sb("kwnT", [P, T])
        vs = sb("vs", [P, TT, T])
        kc = sb("kc", [P, 2, 3, T])
        pt = sb("pt", [P, 2, 512])
        xk = sb("xk", [P, KD, T])
        xv = sb("xv", [P, TT, D])
        small = sb("small", [P, 512])
        cp = sb("cp", [P, 2, 8, 32])
        rt = sb("rt", [P, 2, 96])
        kcT = sb("kcT", [P, 16])
        pcs = sb("pcs", [96, T])
        hid = sb("hid", [HD, 2, 32])
        hidr = sb("hidr", [HD, 96])
        vbd = sb("vbd", [96, 384])
        xc = sb("xc", [P, TT, NH, 16])
        pc = sb("pc", [P, TT, NH, 16])
        eight = sb("eight", [P, 16])
        idx = sb("idx", [P, 8], U32)
        flag = sb("flag", [1, 1], I32)

        def cs(name):
            a, w = CS[name]
            return cst[:, a:a + w]

        def lpv(name):
            a, w = LP[name]
            return lp[:, a:a + w]

        ident = cs("ident")
        cmask = cs("cmask")
        cos2 = cs("rope")[:, 0:32].rearrange("p (t c) -> p t c", t=2)
        sin2 = cs("rope")[:, 32:64].rearrange("p (t c) -> p t c", t=2)
        half = cs("half")
        cols = lpv("cols")
        glu = lpv("glu").rearrange("p (k n) -> p k n", k=2)
        uq = lpv("uq").rearrange("p (k n) -> p k n", k=2)
        ukv = lpv("ukv")
        w1 = lpv("w1").rearrange("p (v m n) -> p v m n", v=2, m=NPAIR)
        w2 = lpv("w2").rearrange("p (v n) -> p v n", v=2)
        bt = lpv("bt").rearrange("p (j c n) -> p j c n", j=8, c=2)
        ct = lpv("ct").rearrange("p (c j n) -> p c j n", c=2, j=8)
        rowf = row[:, :, :].rearrange("p t n -> p (t n)")
        z = rowf[:, 0:704].rearrange("p (t n) -> p t n", t=2)
        krp = rowf[:, 704:896].rearrange("p (t n) -> p t n", t=2)
        qrow = rowf[:, 896:2048].rearrange("p (t h n) -> p t h n", t=2, h=NH)
        prob = kc[:, :, :, :].rearrange("p a b n -> p (a b n)")[:, 0:1536].rearrange("p (b n) -> p b n", b=4)
        ftab = big
        bigf = big[:, :, :, :].rearrange("p a b n -> p (a b n)")
        memT = col
        w1f = lpv("w1")
        tmpd = w1f[:, 0:1024].rearrange("p (a n) -> p a n", a=4)
        tmpdf = w1f[:, 0:1024]
        tmpp = w1f[:, 1024:2048].rearrange("p (a n) -> p a n", a=4)
        kcf = kc[:, :, :, :].rearrange("p a b n -> p (a b n)")
        xprob = kcf.rearrange("p (b n) -> p b n", b=3)
        xkf = xk[:, :, :].rearrange("p k n -> p (k n)")
        xvf = xv[:, :, :].rearrange("p k n -> p (k n)")
        xq = big[:, 0, :, :]
        xo = big[:, 1, :, :]
        ss = small[:, 0:8]
        rstd = small[:, 8:16]
        gates = small[:, 16:52].rearrange("p (t n) -> p t n", t=2)
        mx = small[:, 52:92]
        sums = small[:, 92:132]
        nmx = small[:, 132:172]
        rinv = small[:, 172:212]
        wgt = small[:, 212:248].rearrange("p (t n) -> p t n", t=2)
        par = small[:, 248:376].rearrange("p (k n) -> p k n", k=16)
        cmx = small[:, 376:388]
        csum = small[:, 388:400]
        crow = small[:, 400:401]
        xmx = small[:, 404:412]
        xsum = small[:, 412:420]
        xnm = small[:, 420:428]
        xri = small[:, 428:436]

        banks = [ctx.enter_context(nc.psum_tensor(f"bank{i}", [P, 512], F32)) for i in range(8)]
        ob = [banks[5], banks[6]]
        yb = banks[7]

        landed = [sem(f"landed{i}") for i in range(RING)]
        weights_used = sem("weights_used")
        s_const = sem("s_const")
        lp_landed = sem("lp_landed")
        s_pro = sem("s_pro")
        s_scr = sem("s_scr")
        s_out = sem("s_out")
        arrived = sem("arrived")
        go = sem("go")
        per_layer = []

        def lsem(name):
            s = sem(name)
            per_layer.append(s)
            return s

        mm_done = lsem("mm_done")
        act_drained = lsem("act_drained")
        dve_drained = lsem("dve_drained")
        act_seq = lsem("act_seq")
        dve_seq = lsem("dve_seq")
        pool_seq = lsem("pool_seq")
        pe_note = lsem("pe_note")
        ss_ready = lsem("ss_ready")
        rstd_ready = lsem("rstd_ready")
        z_ready = lsem("z_ready")
        scan_ready = lsem("scan_ready")
        ar1 = lsem("ar1")
        pool_note = lsem("pool_note")
        row_ready = lsem("row_ready")
        memT_ready = lsem("memT_ready")
        rope_ready = lsem("rope_ready")
        par_ready = lsem("par_ready")
        trig_ready = lsem("trig_ready")
        ftab_ready = lsem("ftab_ready")
        ct_ready = lsem("ct_ready")
        state_ready = lsem("state_ready")
        g_free = lsem("g_free")
        hid_ready = lsem("hid_ready")
        cmp_ready = lsem("cmp_ready")
        cexp_ready = lsem("cexp_ready")
        cprob_ready = lsem("cprob_ready")
        score_ready = lsem("score_ready")
        prob_ready = lsem("prob_ready")
        pT_read = lsem("pT_read")
        o_read = lsem("o_read")
        gate_ready = lsem("gate_ready")
        ys_pre = lsem("ys_pre")
        ys_ready = lsem("ys_ready")
        glu_ready = lsem("glu_ready")
        y_ready = lsem("y_ready")
        xmax_ready = lsem("xmax_ready")
        xexp_ready = lsem("xexp_ready")
        xprob_ready = lsem("xprob_ready")
        h_ready = lsem("h_ready")
        gu_done = lsem("gu_done")
        silu_done = lsem("silu_done")
        hid_done = lsem("hid_done")
        hT_tr = lsem("hT_tr")
        hT_done = lsem("hT_done")
        down_done = lsem("down_done")
        y_taken = lsem("y_taken")
        ffn_added = lsem("ffn_added")
        route = lsem("route")
        route_pe = lsem("route_pe")
        flag_ready = lsem("flag_ready")
        clear_range = range(min(s.num for s in per_layer), max(s.num for s in per_layer) + 1)
        assert len(clear_range) == len(per_layer)

        moe = []
        for i in range(2):
            moe.append({n: sem(f"moe{i}_{n}") for n in (
                "onehot", "gathered", "xe", "oh_t", "oh", "gu", "silu", "hid", "htr", "ht", "down", "y", "scat", "added", "used")})
        flag_again = sem("flag_again")
        final_ready = sem("final_ready")
        p_dve, p_act, p_pool, p_pe = sem("p_dve"), sem("p_act"), sem("p_pool"), sem("p_pe")
        f_dve, f_act, f_pool = sem("f_dve"), sem("f_act"), sem("f_pool")
        fg_landed = sem("fg_landed")
        landed2 = [sem(f"landed_again{i}") for i in range(RING)]

        def index(name):
            return NAMES.index(name)

        def bank(name):
            return banks[index(name) % ROT]

        def wait_free(eng, name):
            n = index(name) - ROT
            if n < 0:
                return
            old, by, _ = JOBS[n]
            eng.wait_ge(act_drained if by == "act" else dve_drained, DRAINS[by].index(old) + 1)

        def wait_tile(eng, l, name):
            c = JOBS[index(name)][2]
            if c is None:
                eng.wait_ge(mm_done, PLAIN.index(name) + 1)
            else:
                eng.wait_ge(weights_used, l * LAYER_CHUNKS + RING + c + 1)

        def wait_drained(eng, name):
            by = JOBS[index(name)][1]
            eng.wait_ge(act_drained if by == "act" else dve_drained, DRAINS[by].index(name) + 1)

        def kv_group(i):
            return (i % NH) // 3

        hr = bigf[:, 0:1024].rearrange("p (b t n) -> p b t n", b=2, t=TT)
        ht = bigf[:, 1024:2048].rearrange("p (b n) -> p b n", b=2)
        gs = bigf[:, 2048:3072].rearrange("p (b t n) -> p b t n", b=2, t=TT)

        def ffn_slots(i, first):
            if i == 0:
                return (first) % RING, (first + 1) % RING, (first + 4) % RING
            return (first + 3 * i - 1) % RING, (first + 3 * i) % RING, (first + 3 * i + 4) % RING

        def dense_pe(pe):
            f0 = COMMON % RING

            def landed_wait(at):
                n, slot = at
                pe.wait_ge(landed[slot], 16 * n)

            def nth(c):
                return c // RING + 1, c % RING

            def part(i, half, r, even):
                c = COMMON + (half if i == 0 else 3 * i - 1 + half)
                n, slot = nth(c)
                landed_wait((n + r, slot))
                w = ring[:, slot, :]
                for t in range(TT):
                    if half == 0 and even is not None:
                        pe.wait_ge(hid_done, TT * (even - 1) + t + 1)
                    for k in range(4):
                        ins = pe.matmul(banks[t][:, :], col[:, 4 * half + k, t * P:(t + 1) * P], w[:, k * 512:(k + 1) * 512],
                                        start=(half == 0 and k == 0), stop=(half == 1 and k == 3))
                    if half == 1 and t == 0:
                        ins.then_inc(gu_done, 1)
                ins.then_inc(weights_used, 1)

            def turn(i, n):
                pe.wait_ge(hid_done, TT * n + TT)
                for f in range(2):
                    for t in range(TT):
                        c = f * T + t * P
                        ins = pe.transpose(banks[2][:, c:c + P], hr[:, i % 2, t, f * P:(f + 1) * P], ident)
                ins.then_inc(hT_tr, 1)

            def down(i, n, r, last=False):
                c = COMMON + (3 * i + 4 if not last else 3 * i + 2)
                m, slot = nth(c)
                landed_wait((m + r, slot))
                pe.wait_ge(hT_done, n + 1)
                w = ring[:, slot, :]
                for f in range(2):
                    for t in range(TT):
                        for nn in range(2):
                            ins = pe.matmul(banks[3 + 2 * t + nn][:, :], ht[:, i % 2, f * T + t * P:f * T + (t + 1) * P],
                                            w[:, f * 1024 + nn * 512:f * 1024 + (nn + 1) * 512],
                                            start=(i == 0 and f == 0), stop=(last and f == 1), skip_group_check=True)
                ins.then_inc(weights_used, 1)

            def step(i, n, r):
                part(i + 1, 0, r, n + 1)
                turn(i, n)
                part(i + 1, 1, r, None)
                down(i, n, r)

            pe.wait_ge(act_drained, len(DRAINS["act"]))
            part(0, 0, 0, None)
            part(0, 1, 0, None)
            step(0, 0, 0)
            step(1, 1, 0)
            with pe.Fori(1, (DENSE_PIECES - 1) // 2) as r:
                step_in_loop = ((0, 2 * r), (1, 2 * r + 1))
                for i, n in step_in_loop:
                    part(i + 1, 0, r, n + 1)
                    turn(i, n)
                    part(i + 1, 1, r, None)
                    c = COMMON + 3 * i + 4
                    m, slot = nth(c)
                    landed_wait((m + r, slot))
                    pe.wait_ge(hT_done, n + 1)
                    w = ring[:, slot, :]
                    for f in range(2):
                        for t in range(TT):
                            for nn in range(2):
                                ins = pe.matmul(banks[3 + 2 * t + nn][:, :], ht[:, i % 2, f * T + t * P:f * T + (t + 1) * P],
                                                w[:, f * 1024 + nn * 512:f * 1024 + (nn + 1) * 512],
                                                start=False, stop=False, skip_group_check=True)
                    ins.then_inc(weights_used, 1)
            n = DENSE_PIECES - 1
            turn(n, n)
            down(n, n, 0, last=True)
            pe.wait_ge(weights_used, RING + LAYER_CHUNKS)

        lg = bigf[:, 3072:3088].rearrange("p (t e) -> p t e", t=TT)
        sel = bigf[:, 3088:3104].rearrange("p (t e) -> p t e", t=TT)
        comb = bigf[:, 3104:3120].rearrange("p (t e) -> p t e", t=TT)
        rank = bigf[:, 3120:3136].rearrange("p (t e) -> p t e", t=TT)
        oh1 = bigf[:, 3136:3152].rearrange("p (t e) -> p t e", t=TT)
        cnt = bigf[:, 3152:3160]
        idf = bigf[:, 3160:3168]
        wd = bigf[:, 3168:3176]
        router = cs("router")
        iota8 = cs("iota8")
        before = cs("before")
        ones = cs("ones")

        def route_on_pe(pe):
            for t in range(TT):
                for k in range(KD):
                    ins = pe.matmul(banks[7][:, t * 8:(t + 1) * 8], col[:, k, t * P:(t + 1) * P], router[:, k * 8:(k + 1) * 8],
                                    start=(k == 0), stop=(k == KD - 1))
            ins.then_inc(route_pe, 1)
            pe.wait_ge(route, 1)
            pe.matmul(banks[6][:, 0:8], before, sel[:, 0, :], start=True, stop=True)
            pe.matmul(banks[6][:, 8:16], before, sel[:, 1, :], start=True, stop=False)
            pe.matmul(banks[6][:, 8:16], ones, sel[:, 0, :], start=False, stop=True)
            pe.matmul(banks[6][:, 16:24], ones, sel[:, 0, :], start=True, stop=False)
            pe.matmul(banks[6][:, 16:24], ones, sel[:, 1, :], start=False, stop=True).then_inc(route_pe, 1)
            pe.wait_ge(route, 2)

        oh = xvf[:, 0:256].rearrange("p (t j) -> p t j", t=TT)
        ohT = xvf[:, 256:512]
        xe = xkf[:, 0:1024].rearrange("p (k j) -> p k j", k=KD)
        ye = xkf[:, 1024:2048]
        N = MOE_PIECES

        def moe_pe(pe, m, used, base, land, first):

            def slot_of(c, e, r=0):
                q = first + c
                s = q % RING
                pe.wait_ge(land[s], 16 * (q // RING + 1 + e * (MOE_CHUNKS // RING) + r))
                return ring[:, s, :]

            def part(i, half, e, r=0, n=None):
                w = slot_of(half if i == 0 else 3 * i - 1 + half, e, r)
                if half == 0 and n is not None:
                    pe.wait_ge(m["hid"], N * e + n - 1)
                for k in range(4):
                    ins = pe.matmul(banks[i % 2][:, :], xe[:, 4 * half + k, :], w[:, k * 512:(k + 1) * 512],
                                    start=(half == 0 and k == 0), stop=(half == 1 and k == 3))
                ins.then_inc(used, 1)

            def turn(i, e, n):
                pe.wait_ge(m["hid"], N * e + n + 1)
                for f in range(2):
                    ins = pe.transpose(banks[2][:, f * P:(f + 1) * P], hr[:, i % 2, 0, f * P:(f + 1) * P], ident)
                ins.then_inc(m["htr"], 1)

            def down(i, e, n, r=0, start=False, last=False):
                w = slot_of(3 * i + 2 if last else 3 * i + 4, e, r)
                pe.wait_ge(m["ht"], N * e + n + 1)
                for f in range(2):
                    for nn in range(2):
                        ins = pe.matmul(banks[3 + nn][:, :], ht[:, i % 2, f * P:(f + 1) * P],
                                        w[:, f * 1024 + nn * 512:f * 1024 + (nn + 1) * 512],
                                        start=(start and f == 0), stop=(last and f == 1), skip_group_check=True)
                ins.then_inc(used, 1)

            def gather(e):
                pe.wait_ge(m["onehot"], e + 1)
                for k in range(KD):
                    for t in range(TT):
                        ins = pe.matmul(banks[5 + k // 4][:, (k % 4) * P:(k % 4 + 1) * P], row[:, t, k * P:(k + 1) * P], oh[:, t, :],
                                        start=(t == 0), stop=(t == TT - 1))
                ins.then_inc(m["gathered"], 1)

            def turn_onehot():
                for t in range(TT):
                    ins = pe.transpose(banks[7][:, t * P:(t + 1) * P], oh[:, t, :], ident)
                ins.then_inc(m["oh_t"], 1)

            def scatter(e):
                pe.wait_ge(m["y"], e + 1)
                pe.wait_ge(m["oh"], e + 1)
                for t in range(TT):
                    for nn in range(2):
                        q = 2 * t + nn
                        if q == 3:
                            pe.wait_ge(m["added"], 4 * e + 1)
                        pe.matmul(banks[(5, 6, 7, 5)[q]][:, :], ohT[:, t * P:(t + 1) * P], ye[:, nn * 512:(nn + 1) * 512],
                                  start=True, stop=True).then_inc(m["scat"], 1)

            def pieces(e, boundary):
                for i in range(2):
                    part(i + 1, 0, e, 0, None if i == 0 else i + 1)
                    turn(i, e, i)
                    part(i + 1, 1, e)
                    down(i, e, i, start=(i == 0))
                with pe.Fori(1, N // 2 - 1) as r:
                    for i in range(2):
                        part(i + 1, 0, e, r, 2 * r + i + 1)
                        turn(i, e, 2 * r + i)
                        part(i + 1, 1, e, r)
                        down(i, e, 2 * r + i, r)
                part(N - 1, 0, e, 0, N - 1)
                turn(N - 2, e, N - 2)
                part(N - 1, 1, e)
                down(N - 2, e, N - 2)
                if boundary:
                    gather(e + 1)
                turn(N - 1, e, N - 1)
                down(N - 1, e, N - 1, last=True)

            gather(0)
            turn_onehot()
            pe.wait_ge(m["xe"], 1)
            part(0, 0, 0)
            part(0, 1, 0)
            with pe.Fori(0, NE - 1) as e:
                pieces(e, True)
                pe.wait_ge(m["xe"], e + 2)
                part(0, 0, e + 1)
                part(0, 1, e + 1)
                scatter(e)
                pe.wait_ge(m["added"], 4 * e + 4)
                turn_onehot()
            pieces(NE - 1, False)
            scatter(NE - 1)
            pe.wait_ge(m["added"], 4 * NE)

        def dense_act(act):
            def silu(i, n, buf_free):
                for t in range(TT):
                    if t == 0:
                        act.wait_ge(gu_done, n + 1)
                    else:
                        act.wait_ge(weights_used, RING + COMMON + (2 if i == 0 and buf_free is None else 3 * n + 1))
                    if buf_free is not None:
                        act.wait_ge(hid_done, TT * buf_free + t + 1)
                    act.activation(gs[:, i % 2, t, :], banks[t][:, 0:256], ACT.Silu).then_inc(silu_done, 1)

            def copy_units(i, n, wait):
                act.wait_ge(hT_tr, n + 1)
                if wait:
                    act.wait_ge(weights_used, RING + COMMON + 3 * n - 1)
                act.activation(ht[:, i % 2, :], banks[2][:, :], ACT.Copy).then_inc(hT_done, 1)

            silu(0, 0, None)
            copy_units(0, 0, False)
            silu(1, 1, 0)
            copy_units(1, 1, False)
            silu(0, 2, 1)
            with act.Fori(1, (DENSE_PIECES - 1) // 2) as r:
                copy_units(0, 2 * r, True)
                silu(1, 2 * r + 1, 2 * r)
                copy_units(1, 2 * r + 1, True)
                silu(0, 2 * r + 2, 2 * r + 1)
            copy_units(0, DENSE_PIECES - 1, True)

        def moe_act(act, m, used, base):
            def silu(i, e, n, wait=True):
                act.wait_ge(used, base + e * MOE_CHUNKS + (2 if i == 0 and not wait else 3 * n + 1))
                if wait and not (i == 1 and isinstance(n, int) and n < 2):
                    act.wait_ge(m["hid"], N * e + n - 1)
                act.activation(gs[:, i % 2, 0, :], banks[i % 2][:, 0:256], ACT.Silu).then_inc(m["silu"], 1)

            def copy_units(i, e, n, wait):
                act.wait_ge(m["htr"], N * e + n + 1)
                if wait:
                    act.wait_ge(used, base + e * MOE_CHUNKS + 3 * n - 1)
                act.activation(ht[:, i % 2, 0:256], banks[2][:, 0:256], ACT.Copy).then_inc(m["ht"], 1)

            def copy_onehot(e):
                act.wait_ge(m["oh_t"], e + 1)
                act.activation(ohT, banks[7][:, 0:256], ACT.Copy).then_inc(m["oh"], 1)

            def pieces(e):
                copy_units(0, e, 0, False)
                silu(1, e, 1)
                copy_units(1, e, 1, False)
                silu(0, e, 2)
                with act.Fori(1, N // 2 - 1) as r:
                    copy_units(0, e, 2 * r, True)
                    silu(1, e, 2 * r + 1)
                    copy_units(1, e, 2 * r + 1, True)
                    silu(0, e, 2 * r + 2)
                copy_units(0, e, N - 2, True)
                silu(1, e, N - 1)
                copy_units(1, e, N - 1, True)
                act.wait_ge(used, base + e * MOE_CHUNKS + MOE_CHUNKS)
                for nn in range(2):
                    ins = act.activation(ye[:, nn * 512:(nn + 1) * 512], banks[3 + nn][:, :], ACT.Copy)
                ins.then_inc(m["y"], 1)

            copy_onehot(0)
            silu(0, 0, 0, False)
            with act.Fori(0, NE - 1) as e:
                pieces(e)
                silu(0, e + 1, 0, False)
                copy_onehot(e + 1)
            pieces(NE - 1)

        def dense_dve(dve):
            def product(i, n, wait):
                for t in range(TT):
                    dve.wait_ge(silu_done, TT * n + t + 1)
                    if wait and t == 0:
                        dve.wait_ge(hT_tr, n - 1)
                    dve.tensor_tensor(hr[:, i % 2, t, :], gs[:, i % 2, t, :], banks[t][:, 256:512], ALU.mult).then_inc(hid_done, 1)

            product(0, 0, False)
            product(1, 1, False)
            product(0, 2, True)
            with dve.Fori(1, (DENSE_PIECES - 1) // 2) as r:
                product(1, 2 * r + 1, True)
                product(0, 2 * r + 2, True)
            dve.wait_ge(weights_used, RING + LAYER_CHUNKS)
            for t in range(TT):
                for n in range(2):
                    hs = h[:, t, n * 512:(n + 1) * 512]
                    dve.tensor_tensor(hs, hs, banks[3 + 2 * t + n][:, :], ALU.add).then_inc(ffn_added, 1)

        def route_on_dve(dve):
            n = [0]

            def link(ins):
                n[0] += 1
                ins.then_inc(ar1, 1)
                dve.wait_ge(ar1, n[0])

            dve.wait_ge(route_pe, 1)
            link(dve.tensor_copy(lg, banks[7][:, 0:16].rearrange("p (t e) -> p t e", t=TT)))
            for t in range(TT):
                for choice in (oh1, sel):
                    link(dve.max(eight[:, 0:8], lg[:, t, :]))
                    link(dve.max_index(idx[:, :], eight[:, 0:8], lg[:, t, :]))
                    if choice is oh1:
                        dve.tensor_copy(wd[:, 4 + t:5 + t], eight[:, 0:1])
                    else:
                        dve.tensor_tensor(wd[:, t:t + 1], eight[:, 0:1], wd[:, 4 + t:5 + t], ALU.subtract)
                    link(dve.tensor_copy(idf, idx[:, :]))
                    link(dve.tensor_scalar(choice[:, t, :], iota8, idf[:, 0:1], None, ALU.is_equal))
                    if choice is oh1:
                        link(dve.scalar_tensor_tensor(lg[:, t, :], oh1[:, t, :], NEG, lg[:, t, :], ALU.mult, ALU.add))
            link(dve.tensor_copy(comb, sel))
            link(dve.tensor_tensor(sel, sel, oh1, ALU.add))
            dve.tensor_copy(eight[:, 8:9], eight[:, 0:1]).then_inc(route, 1)
            dve.wait_ge(route_pe, 2)
            dve.tensor_copy(rank, banks[6][:, 0:16].rearrange("p (t e) -> p t e", t=TT))
            link(dve.tensor_copy(cnt, banks[6][:, 16:24]))
            dve.tensor_copy(eight[:, 9:10], cnt[:, 0:1]).then_inc(route, 1)
            link(dve.tensor_reduce(eight[:, 10:11], cnt, AX.X, ALU.max))
            dve.tensor_scalar(flag[0:1, 0:1], eight[0:1, 10:11], float(P) + 0.5, None, ALU.is_gt).then_inc(flag_ready, 1)
            dve.wait_ge(flag_ready, 1)
            dve.tensor_copy(eight[:, 11:12], eight[:, 10:11]).then_inc(route, 1)
            dve.wait_ge(route, 4)
            link(dve.tensor_scalar(wd[:, 2:4], wd[:, 0:2], 1.0, None, ALU.add))
            link(dve.reciprocal(wd[:, 2:4], wd[:, 2:4]))
            link(dve.tensor_tensor(wd[:, 0:2], wd[:, 0:2], wd[:, 2:4], ALU.mult))
            for t in range(TT):
                link(dve.tensor_scalar(comb[:, t, :], comb[:, t, :], wd[:, t:t + 1], None, ALU.mult))
                link(dve.scalar_tensor_tensor(comb[:, t, :], oh1[:, t, :], wd[:, 2 + t:3 + t], comb[:, t, :], ALU.mult, ALU.add))

        def moe_dve(dve, m, tile):
            places = cs("iota")[:, tile * P:(tile + 1) * P]

            def onehot(e):
                for t in range(TT):
                    ins = dve.tensor_scalar(oh[:, t, :], places, rank[:, t, bass.ds(e, 1)], sel[:, t, bass.ds(e, 1)],
                                            ALU.is_equal, ALU.mult)
                ins.then_inc(m["onehot"], 1)

            def gathered(e):
                dve.wait_ge(m["gathered"], e + 1)
                for k in range(KD):
                    ins = dve.tensor_scalar(xe[:, k, :], banks[5 + k // 4][:, (k % 4) * P:(k % 4 + 1) * P],
                                            cols[:, C_FFN + k:C_FFN + k + 1], None, ALU.mult)
                ins.then_inc(m["xe"], 1)

            def product(i, e, n, wait=True):
                dve.wait_ge(m["silu"], N * e + n + 1)
                if wait:
                    dve.wait_ge(m["htr"], N * e + n - 1)
                dve.tensor_tensor(hr[:, i % 2, 0, :], gs[:, i % 2, 0, :], banks[i % 2][:, 256:512], ALU.mult).then_inc(m["hid"], 1)

            def pieces(e, more):
                product(1, e, 1, False)
                if more:
                    dve.wait_ge(m["oh_t"], e + 1)
                    onehot(e + 1)
                product(0, e, 2)
                with dve.Fori(1, N // 2 - 1) as r:
                    product(1, e, 2 * r + 1)
                    product(0, e, 2 * r + 2)
                product(1, e, N - 1)
                if more:
                    gathered(e + 1)

            def add(e):
                for t in range(TT):
                    for nn in range(2):
                        q = 2 * t + nn
                        dve.wait_ge(m["scat"], 4 * e + q + 1)
                        hs = h[:, t, nn * 512:(nn + 1) * 512]
                        dve.scalar_tensor_tensor(hs, banks[(5, 6, 7, 5)[q]][:, :], comb[:, t, bass.ds(e, 1)], hs,
                                                 ALU.mult, ALU.add).then_inc(m["added"], 1)

            onehot(0)
            gathered(0)
            product(0, 0, 0, False)
            with dve.Fori(0, NE - 1) as e:
                pieces(e, True)
                add(e)
                product(0, e + 1, 0, False)
            pieces(NE - 1, False)
            add(NE - 1)
            dve.wait_ge(m["added"], 4 * NE)

        block = ctx.enter_context(nc.Block())

        @block.sync
        def _(sp):
            sp.dma_start(cst[:, :], consts).then_inc(s_const, 16)
            sp.dma_start(h[:, :, :], x.rearrange("(t p) n -> p t n", p=P)).then_inc(s_const, 16)
            sp.dma_start(row[:, :, :], mem.rearrange("(t p) n -> p t n", p=P)).then_inc(s_const, 16)
            sp.dma_start(bigf[0:33, 0:512], onehot).then_inc(s_const, 16)
            sp.dma_start(bigf[0:33, 512:518], relb).then_inc(s_const, 16)

            def stream(first, count, used, land):
                rounds, rest = divmod(count, RING)
                with sp.Fori(0, rounds) as r:
                    for s in range(RING):
                        sp.wait_ge(used, r * RING + (s + 1))
                        sp.dma_start(ring[:, s, :], weights[first + r * RING + s]).then_inc(land[s], 16)
                for s in range(rest):
                    sp.wait_ge(used, rounds * RING + s + 1)
                    sp.dma_start(ring[:, s, :], weights[first + rounds * RING + s]).then_inc(land[s], 16)

            stream(0, CHUNKS, weights_used, landed)
            sp.wait_ge(flag_again, 1)
            v = sp.value_load(flag[0:1, 0:1], min_val=0, max_val=1)
            with sp.If(v == 1):
                stream(MOE_FIRST, NE * MOE_CHUNKS, moe[1]["used"], landed2)
            with sp.Else():
                sp.nop()
            sp.wait_ge(final_ready, 2)
            sp.dma_start(out.rearrange("(t p) n -> p t n", p=P), row[:, :, :]).then_inc(s_out, 16)
            sp.wait_ge(s_out, 16)
        @block.tensor
        def _(pe):
            mm = pe.matmul

            def finish(name, ins):
                ins.then_inc(mm_done if JOBS[index(name)][2] is None else weights_used, 1)

            def chunk(l, c):
                pe.wait_ge(landed[c % RING], 16 * (LAYER_CHUNKS // RING * l + c // RING + 1))
                return ring[:, c % RING, :]

            def transpose_rows(stage):
                for i in range(4):
                    wait_free(pe, f"{stage}T{i}")
                    b = bank(f"{stage}T{i}")
                    for k in range(2):
                        for t in range(TT):
                            f = (2 * i + k) * P
                            ins = pe.transpose(b[:, (k * TT + t) * P:(k * TT + t + 1) * P], row[:, t, f:f + P], ident)
                    finish(f"{stage}T{i}", ins)

            def features_out(name, l, c, width=2, at=0):
                w = chunk(l, c)
                wait_free(pe, name)
                b = bank(name)
                for m in range(width):
                    for k in range(KD):
                        ins = mm(b[:, m * T:(m + 1) * T], w[:, k * 256 + m * P:k * 256 + (m + 1) * P], col[:, k, :],
                                 start=(k == 0), stop=(k == KD - 1))
                finish(name, ins)

            def tokens_out(stage, l, c0, src):
                for part in range(2):
                    w = chunk(l, c0 + part)
                    for t in range(TT):
                        name = f"{stage}_{t}"
                        if part == 0:
                            wait_free(pe, name)
                        for k in range(4):
                            ins = mm(bank(name)[:, :], src[:, 4 * part + k, t * P:(t + 1) * P], w[:, k * 512:(k + 1) * 512],
                                     start=(part == 0 and k == 0), stop=(part == 1 and k == 3))
                        if part == 1:
                            finish(name, ins)
                        elif t == TT - 1:
                            ins.then_inc(weights_used, 1)

            pe.sem_inc(weights_used, RING)
            pe.sem_inc(moe[1]["used"], RING)
            pe.wait_ge(p_act, 2)
            for i in range(4):
                for k in range(2):
                    for t in range(TT):
                        f = (2 * i + k) * P
                        ins = pe.transpose(banks[i][:, (k * TT + t) * P:(k * TT + t + 1) * P], row[:, t, f:f + P], ident)
                ins.then_inc(p_pe, 1)
            pe.wait_ge(p_dve, 4)
            for hh in range(NH):
                b = banks[4 + hh % 4]
                if hh >= 4:
                    pe.wait_ge(p_dve, 4 + hh - 3)
                mm(b[:, 0:384], bigf[0:33, 640 + hh * P:640 + (hh + 1) * P], bigf[0:33, 0:384],
                   start=True, stop=True).then_inc(p_pe, 1)
            pe.wait_ge(p_act, 6)
            pe.wait_ge(p_dve, 4 + NH)

            with pe.Fori(0, L) as l:
                pe.wait_ge(row_ready, 2)
                transpose_rows("h")
                wait_drained(pe, "hT3")
                features_out("u", l, 0)
                w = chunk(l, 1)
                wait_free(pe, "zA")
                for t in range(TT):
                    for k in range(KD):
                        ins = mm(bank("zA")[:, t * 256:(t + 1) * 256], col[:, k, t * P:(t + 1) * P], w[:, k * 256:(k + 1) * 256],
                                 start=(k == 0), stop=(k == KD - 1))
                finish("zA", ins)
                w = chunk(l, 2)
                wait_free(pe, "zB")
                for t in range(TT):
                    for k in range(KD):
                        mm(bank("zB")[:, t * 114:(t + 1) * 114], col[:, k, t * P:(t + 1) * P], w[:, k * 256:k * 256 + 114],
                           start=(k == 0), stop=(k == KD - 1))
                for k in range(KD):
                    ins = mm(bank("zB")[:, 228:484], w[:, k * 256 + 114:k * 256 + 242], col[:, k, :],
                             start=(k == 0), stop=(k == KD - 1))
                finish("zB", ins)
                features_out("q0", l, 3)
                features_out("q1", l, 4)
                w = chunk(l, 5)
                for v, name in enumerate(("ck", "cv")):
                    wait_free(pe, name)
                    for k in range(KD):
                        ins = mm(bank(name)[:, 0:T], w[:, k * 256 + v * P:k * 256 + (v + 1) * P], col[:, k, :],
                                 start=(k == 0), stop=(k == KD - 1))
                    finish(name, ins)
                w = chunk(l, 6)
                wait_free(pe, "vs")
                for t in range(TT):
                    for k in range(KD):
                        ins = mm(bank("vs")[:, t * 256:(t + 1) * 256], col[:, k, t * P:(t + 1) * P], w[:, k * 256:(k + 1) * 256],
                                 start=(k == 0), stop=(k == KD - 1))
                finish("vs", ins)

                pe.wait_ge(z_ready, 1)
                wait_free(pe, "cqT")
                b = bank("cqT")
                for t in range(TT):
                    pe.transpose(b[:, t * P:(t + 1) * P], z[:, t, 0:128], ident)
                    ins = pe.transpose(b[0:64, T + t * P:T + (t + 1) * P], z[:, t, 128:192], ident)
                finish("cqT", ins)
                pe.wait_ge(rope_ready, 1)
                wait_free(pe, "ckvT")
                b = bank("ckvT")
                for t in range(TT):
                    pe.transpose(b[:, t * P:(t + 1) * P], z[:, t, 192:320], ident)
                    ins = pe.transpose(b[0:96, T + t * P:T + (t + 1) * P], krp[:, t, :], ident)
                finish("ckvT", ins)
                wait_drained(pe, "ck")
                wait_drained(pe, "cv")
                wait_free(pe, "hid")
                b = bank("hid")
                for v in range(2):
                    for m in range(NPAIR):
                        ins = mm(b[0:HD, v * 45:(v + 1) * 45], w1[:, v, m, :], kc[:, v, :, 2 * m:2 * m + 225:CSTRIDE],
                                 start=(m == 0), stop=(m == NPAIR - 1))
                finish("hid", ins)
                wait_drained(pe, "cqT")
                for t in range(TT):
                    for name, a, n in ((f"qn{t}", 0, 384), (f"qr{t}", 384, 192)):
                        wait_free(pe, name)
                        for k in range(2):
                            ins = mm(bank(name)[:, 0:n], ql[:, k, t * P:(t + 1) * P], uq[:, k, a:a + n],
                                     start=(k == 0), stop=(k == 1))
                        finish(name, ins)
                wait_drained(pe, "ckvT")
                for i in range(3):
                    wait_free(pe, f"kn{i}")
                    for hh in range(2):
                        c = (2 * i + hh) * 64
                        ins = mm(bank(f"kn{i}")[0:HD, hh * T:(hh + 1) * T], ukv[:, c:c + 64], ckvT[:, :], start=True, stop=True)
                    finish(f"kn{i}", ins)
                for t in range(TT):
                    wait_free(pe, f"vm{t}")
                    ins = mm(bank(f"vm{t}")[:, 0:384], ckvT[:, t * P:(t + 1) * P], ukv[:, 384:768], start=True, stop=True)
                    finish(f"vm{t}", ins)
                pe.wait_ge(hid_ready, 1)
                wait_free(pe, "kcv")
                b = bank("kcv")
                mm(b[0:64, 0:16], w2[0:HD, 0, :], hid[:, 0, 0:16], start=True, stop=True)
                mm(b[64:128, 0:16], w2[0:HD, 0, :], hid[:, 0, 16:32], start=True, stop=True)
                ins = mm(b[0:96, 16:80], hidr[:, :], w2[0:HD, 1, :], start=True, stop=True)
                finish("kcv", ins)
                wait_drained(pe, "qn1")
                wait_drained(pe, "qr1")
                for i in range(3):
                    wait_free(pe, f"qT{i}")
                    for hh in range(2):
                        for t in range(TT):
                            c = (hh * TT + t) * P
                            ins = pe.transpose(bank(f"qT{i}")[0:QK, c:c + P], qrow[:, t, 2 * i + hh, :], ident)
                    finish(f"qT{i}", ins)
                wait_drained(pe, "kcv")
                wait_free(pe, "sc")
                for t in range(TT):
                    for hh in range(NH):
                        c = (t * NH + hh) * 16
                        ins = mm(bank("sc")[:, c:c + 16], qz[:, hh, t * P:(t + 1) * P], kcT[:, :], start=True, stop=True)
                finish("sc", ins)
                pe.wait_ge(cexp_ready, 1)
                wait_free(pe, "pcT")
                for t in range(TT):
                    ins = pe.transpose(bank("pcT")[0:96, t * P:(t + 1) * P], pc[:, t, :, :].rearrange("p h n -> p (h n)"), ident)
                finish("pcT", ins)
                wait_drained(pe, "pcT")
                for t in range(TT):
                    wait_free(pe, f"oc{t}")
                    ins = mm(bank(f"oc{t}")[:, 0:384], pcs[:, t * P:(t + 1) * P], vbd[:, :], start=True, stop=True)
                    finish(f"oc{t}", ins)

                def scores(i):
                    name = f"s{i}"
                    if i == 0:
                        wait_drained(pe, "qT2")
                        wait_drained(pe, "kn2")
                    if i < NH:
                        q, k = qT[:, i, :], kT[:, i, :]
                    else:
                        q, k = qz[:, i % NH, :], (kslT if i < 2 * NH else kwnT)[:, :]
                    wait_free(pe, name)
                    mm(bank(name)[:, 0:128], q[:, 0:128], k[:, 0:128], start=True, stop=True)
                    finish(name, mm(bank(name)[:, 128:384], q[:, 128:256], k, start=True, stop=True))

                def outputs(i):
                    hh, gi = i % NH, kv_group(i)
                    wait_drained(pe, f"pT{i}")
                    if hh == 0 and i > 0:
                        pe.wait_ge(o_read, TT * (i // NH))
                    if i < NH:
                        v = [vm[:, t, hh * 64:(hh + 1) * 64] for t in range(TT)]
                    else:
                        a = (i // NH - 1) * 128 + gi * 64
                        v = [vs[:, t, a:a + 64] for t in range(TT)]
                    p = pt[:, i % 2, :]
                    mm(ob[0][:, hh * 64:(hh + 1) * 64], p[:, 0:128], v[0], start=True, stop=True)
                    mm(ob[1][:, hh * 64:(hh + 1) * 64], p[:, 128:256], v[0], start=True, stop=False)
                    mm(ob[1][:, hh * 64:(hh + 1) * 64], p[:, 256:384], v[1], start=False, stop=True).then_inc(pe_note, 1)

                def state_inputs(j):
                    name = f"bu{j}"
                    wait_free(pe, name)
                    for c in range(2):
                        ins = mm(bank(name)[:, c * T:(c + 1) * T], bt[:, j, c, :], uT[:, j // 4, :], start=True, stop=True)
                    finish(name, ins)

                def state_outputs(j):
                    pe.wait_ge(state_ready, j + 1)
                    y = yb[32 * (j % 4):32 * (j % 4) + 32, (j // 4) * T:(j // 4 + 1) * T]
                    mm(y, cp[:, 0, j, :], g[:, j % 2, 0, :], start=True, stop=False)
                    mm(y, cp[:, 1, j, :], g[:, j % 2, 1, :], start=False, stop=True).then_inc(g_free, 1)

                for i in range(LEAD):
                    scores(i)
                pe.wait_ge(ct_ready, 1)
                pe.wait_ge(memT_ready, KD)
                for i in range(HEADS):
                    if i + LEAD < HEADS:
                        scores(i + LEAD)
                    if i in MEMK:
                        features_out(f"mk{MEMK[i]}", l, 7 + MEMK[i])
                    if i in MEMV:
                        tokens_out(f"mv{MEMV[i]}", l, 11 + 2 * MEMV[i], memT)
                    if i in STATES:
                        state_inputs(STATES[i])
                    pe.wait_ge(prob_ready, i + 1)
                    wait_free(pe, f"pT{i}")
                    for c in range(3):
                        ins = pe.transpose(bank(f"pT{i}")[:, c * P:(c + 1) * P], prob[:, i % 4, c * P:(c + 1) * P], ident)
                    finish(f"pT{i}", ins)
                    if i > 0:
                        outputs(i - 1)
                    if i in STATES and STATES[i] > 0:
                        state_outputs(STATES[i] - 1)
                outputs(HEADS - 1)
                state_outputs(7)

                pe.wait_ge(ys_ready, 1)
                wait_free(pe, "yr")
                for t in range(TT):
                    for k in range(2):
                        ins = pe.transpose(bank("yr")[:, t * T + k * P:t * T + (k + 1) * P], uT[:, k, t * P:(t + 1) * P], ident)
                finish("yr", ins)
                wait_free(pe, "gl")
                for t in range(TT):
                    for k in range(2):
                        ins = mm(bank("gl")[:, t * T:(t + 1) * T], uT[:, k, t * P:(t + 1) * P], glu[:, k, :],
                                 start=(k == 0), stop=(k == 1))
                finish("gl", ins)
                pe.wait_ge(row_ready, 4)
                transpose_rows("y")
                wait_drained(pe, "yT3")
                tokens_out("wo0", l, 15, col)
                tokens_out("wo1", l, 17, col)

                pe.wait_ge(row_ready, 6)
                transpose_rows("x")
                wait_drained(pe, "xT3")
                for i in range(XH):
                    features_out(f"xq{i}", l, 19 + i)
                for i in range(XH):
                    wait_drained(pe, f"xq{i}")
                    wait_free(pe, f"xs{i}")
                    for t in range(TT):
                        for m in range(2):
                            ins = mm(bank(f"xs{i}")[:, t * T:(t + 1) * T], xq[:, 2 * i + m, t * P:(t + 1) * P], xk[:, 2 * i + m, :],
                                     start=(m == 0), stop=(m == 1))
                    finish(f"xs{i}", ins)
                for i in range(XH):
                    pe.wait_ge(xprob_ready, i + 1)
                    wait_free(pe, f"xp{i}")
                    for kt in range(2):
                        for t in range(TT):
                            c = kt * T + t * P
                            ins = pe.transpose(bank(f"xp{i}")[:, c:c + P], xprob[:, i % 3, t * T + kt * P:t * T + (kt + 1) * P], ident)
                    finish(f"xp{i}", ins)
                    wait_drained(pe, f"xp{i}")
                    wait_free(pe, f"xo{i}")
                    for m in range(2):
                        for kt in range(2):
                            a = i * 256 + m * P
                            ins = mm(bank(f"xo{i}")[:, m * T:(m + 1) * T], xv[:, kt, a:a + P], pt[:, i % 2, kt * T:(kt + 1) * T],
                                     start=(kt == 0), stop=(kt == 1))
                    finish(f"xo{i}", ins)
                wait_drained(pe, "xo3")
                tokens_out("xw0", l, 23, xo)
                tokens_out("xw1", l, 25, xo)

                pe.wait_ge(row_ready, 8)
                transpose_rows("f")
                pe.wait_ge(act_drained, len(DRAINS["act"]))
                pe.wait_ge(dve_drained, len(DRAINS["dve"]))
                with pe.If(l == 0):
                    dense_pe(pe)
                with pe.Else():
                    route_on_pe(pe)
                    moe_pe(pe, moe[0], weights_used, RING + MOE_FIRST, landed, MOE_FIRST)
                pe.drain().then_inc(arrived, 1)
                pe.wait_ge(go, l + 1)

            pe.wait_ge(flag_again, 1)
            v = pe.value_load(flag[0:1, 0:1], min_val=0, max_val=1)
            with pe.If(v == 1):
                moe_pe(pe, moe[1], moe[1]["used"], RING, landed2, 0)
            with pe.Else():
                pe.nop()

        @block.scalar
        def _(act):
            A = act.activation
            seq = [0]

            def link(ins):
                seq[0] += 1
                ins.then_inc(act_seq, 1)
                act.wait_ge(act_seq, seq[0])

            def drained(ins):
                ins.then_inc(act_drained, 1)

            def scale_rows(n):
                act.wait_ge(rstd_ready, n)
                for t in range(TT):
                    A(row[:, t, :], h[:, t, :], ACT.Copy, scale=rstd[:, t:t + 1]).then_inc(row_ready, 1)

            def drain_transposes(l, stage, gain):
                for i in range(4):
                    wait_tile(act, l, f"{stage}T{i}")
                    b = bank(f"{stage}T{i}")
                    for k in range(2):
                        kk = 2 * i + k
                        ins = A(col[:, kk, :], b[:, k * T:(k + 1) * T], ACT.Copy, scale=cols[:, gain + kk:gain + kk + 1])
                    drained(ins)

            act.wait_ge(p_pool, 1)
            for t in range(TT):
                A(row[:, t, :], row[:, t, :], ACT.Copy, scale=rstd[:, t:t + 1]).then_inc(p_act, 1)
            for i in range(4):
                act.wait_ge(p_pe, i + 1)
                A(memraw[:, 2 * i:2 * i + 2, :], banks[i][:, :], ACT.Copy).then_inc(p_act, 1)

            with act.Fori(0, L) as l:
                seq[0] = 0
                act.wait_ge(lp_landed, 16 * l + 16)
                A(par[:, 0, :], cols[:, C_LDT:C_LDT + 8], ACT.Exp).then_inc(trig_ready, 1)
                scale_rows(1)
                drain_transposes(l, "h", C_MIX)
                act.wait_ge(par_ready, 1)
                A(par[:, 6, :], par[:, 1, :], ACT.Exp).then_inc(trig_ready, 1)
                A(par[:, 7, :], par[:, 4, :], ACT.Sin).then_inc(trig_ready, 1)
                A(par[:, 8, :], par[:, 5, :], ACT.Sin).then_inc(trig_ready, 1)
                wait_tile(act, l, "u")
                drained(A(uT[:, :, :], bank("u")[:, :], ACT.Copy))
                wait_tile(act, l, "zA")
                drained(A(z[:, :, 0:256], bank("zA")[:, :].rearrange("p (t n) -> p t n", t=2), ACT.Copy))
                wait_tile(act, l, "zB")
                b = bank("zB")[:, 0:228].rearrange("p (t n) -> p t n", t=2)
                A(z[:, :, 256:352], b[:, :, 0:96], ACT.Copy)
                A(gates, b[:, :, 96:114], ACT.Tanh, scale=0.5)
                drained(A(kwnT[:, :], bank("zB")[:, 228:484], ACT.Copy))
                wait_tile(act, l, "ck")
                for gi in range(2):
                    b = bank("ck")[gi * 64:(gi + 1) * 64, 0:T]
                    A(kc[0:64, 0, gi, :], b, ACT.Copy)
                    ins = A(kc[64:128, 0, gi, 0:255], b[:, 1:256], ACT.Copy)
                drained(ins)
                act.wait_ge(rstd_ready, 2)
                for t in range(TT):
                    A(z[:, t, 0:192], z[:, t, 0:192], ACT.Copy, scale=rstd[:, 2 + t:3 + t])
                A(z[:, 0, 192:320], z[:, 0, 192:320], ACT.Copy, scale=rstd[:, 4:5])
                A(z[:, 1, 192:320], z[:, 1, 192:320], ACT.Copy, scale=rstd[:, 5:6]).then_inc(z_ready, 1)
                wait_tile(act, l, "cqT")
                A(ql[:, 0, :], bank("cqT")[:, 0:256], ACT.Copy, scale=cols[:, C_QN:C_QN + 1])
                drained(A(ql[0:64, 1, :], bank("cqT")[0:64, 256:512], ACT.Copy, scale=cols[0:64, C_QN + 1:C_QN + 2]))
                wait_tile(act, l, "ckvT")
                A(ckvT[:, :], bank("ckvT")[:, 0:256], ACT.Copy, scale=cols[:, C_KVN:C_KVN + 1])
                drained(A(kT[64:96, :, :], bank("ckvT")[64:96, 256:512].unsqueeze(1).broadcast_to([32, NH, T]), ACT.Copy))
                for t in range(TT):
                    wait_tile(act, l, f"qn{t}")
                    drained(A(qrow[:, t, :, 0:64], bank(f"qn{t}")[:, 0:384].rearrange("p (h n) -> p h n", h=NH), ACT.Copy))
                for i in range(3):
                    wait_tile(act, l, f"kn{i}")
                    drained(A(kT[0:64, 2 * i:2 * i + 2, :], bank(f"kn{i}")[0:64, :].rearrange("p (h n) -> p h n", h=2), ACT.Copy))
                for t in range(TT):
                    wait_tile(act, l, f"vm{t}")
                    drained(A(vm[:, t, :], bank(f"vm{t}")[:, 0:384], ACT.Copy))
                wait_drained(act, "hid")
                link(A(hid[:, :, :], hid[:, :, :], ACT.Gelu_apprx_tanh))
                A(hidr[:, :].rearrange("p (g r n) -> p g r n", g=2, r=3),
                  hid[:, 1, :].rearrange("p (g n) -> p g n", g=2).unsqueeze(2).broadcast_to([HD, 2, 3, 16]),
                  ACT.Copy).then_inc(hid_ready, 1)
                for i in range(3):
                    wait_tile(act, l, f"qT{i}")
                    drained(A(qT[:, 2 * i:2 * i + 2, :], bank(f"qT{i}")[0:QK, :].rearrange("p (h n) -> p h n", h=2), ACT.Copy))
                act.wait_ge(cmp_ready, 1)
                A(pc[:, :, :, 0:NCMP], pc[:, :, :, 0:NCMP], ACT.Exp, scale=0.125).then_inc(cexp_ready, 1)
                wait_tile(act, l, "pcT")
                drained(A(pcs[:, :], bank("pcT")[0:96, 0:256], ACT.Copy))

                def exponentials(i):
                    wait_drained(act, f"s{i}")
                    p = prob[:, i % 4, :]
                    A(p[:, 0:128], p[:, 0:128], ACT.Exp, bias=mx[:, 2 * i:2 * i + 1], scale=-1.0,
                      accum_out=sums[:, 2 * i:2 * i + 1])
                    A(p[:, 128:384], p[:, 128:384], ACT.Exp, bias=mx[:, 2 * i + 1:2 * i + 2], scale=-1.0,
                      accum_out=sums[:, 2 * i + 1:2 * i + 2]).then_inc(prob_ready, 1)

                for i in range(LEAD):
                    exponentials(i)
                for i in range(HEADS):
                    if i in MEMK:
                        m = MEMK[i]
                        wait_tile(act, l, f"mk{m}")
                        drained(A(xk[:, 2 * m:2 * m + 2, :], bank(f"mk{m}")[:, :], ACT.Copy))
                    if i in MEMV:
                        m = MEMV[i]
                        for t in range(TT):
                            wait_tile(act, l, f"mv{m}_{t}")
                            drained(A(xv[:, t, m * 512:(m + 1) * 512], bank(f"mv{m}_{t}")[:, :], ACT.Copy))
                    wait_tile(act, l, f"pT{i}")
                    if i >= 2:
                        act.wait_ge(pe_note, i - 1)
                    drained(A(pt[:, i % 2, 0:384], bank(f"pT{i}")[:, 0:384], ACT.Copy))
                    if i + LEAD < HEADS:
                        exponentials(i + LEAD)

                act.wait_ge(ys_pre, 2)
                A(uT[:, :, :], uT[:, :, :], ACT.Gelu_apprx_tanh).then_inc(ys_ready, 1)
                wait_tile(act, l, "gl")
                colf = col[:, 0:2, :].rearrange("p k n -> p (k n)")
                drained(A(colf, bank("gl")[:, :], ACT.Tanh, scale=0.5))
                act.wait_ge(rstd_ready, 3)
                for t in range(TT):
                    for s, (a, n) in enumerate(((0, 256), (256, 384), (640, 384))):
                        ins = A(row[:, t, a:a + n], row[:, t, a:a + n], ACT.Copy, scale=rstd[:, 2 * s + t:2 * s + t + 1])
                    ins.then_inc(row_ready, 1)
                drain_transposes(l, "y", C_OUT)
                scale_rows(4)
                drain_transposes(l, "x", C_XN)
                for i in range(XH):
                    wait_tile(act, l, f"xq{i}")
                    drained(A(xq[:, 2 * i:2 * i + 2, :], bank(f"xq{i}")[:, :], ACT.Copy))
                for i in range(XH):
                    act.wait_ge(xmax_ready, i + 1)
                    if i == 3:
                        wait_tile(act, l, "xp0")
                    for t in range(TT):
                        ins = A(xprob[:, i % 3, t * T:(t + 1) * T], bank(f"xs{i}")[:, t * T:(t + 1) * T], ACT.Exp,
                                bias=xnm[:, 2 * i + t:2 * i + t + 1], scale=0.0625, accum_out=xsum[:, 2 * i + t:2 * i + t + 1])
                    drained(ins)
                for i in range(XH):
                    wait_tile(act, l, f"xo{i}")
                    drained(A(xo[:, 2 * i:2 * i + 2, :], bank(f"xo{i}")[:, :], ACT.Copy))
                scale_rows(5)
                drain_transposes(l, "f", C_FFN)
                with act.If(l == 0):
                    dense_act(act)
                with act.Else():
                    act.wait_ge(route, 3)
                    A(wd[:, 0:2], wd[:, 0:2], ACT.Exp).then_inc(route, 1)
                    moe_act(act, moe[0], weights_used, RING + MOE_FIRST)
                act.drain().then_inc(arrived, 1)
                act.wait_ge(go, l + 1)

            act.wait_ge(flag_again, 1)
            v = act.value_load(flag[0:1, 0:1], min_val=0, max_val=1)
            with act.If(v == 1):
                moe_act(act, moe[1], moe[1]["used"], RING)
            with act.Else():
                act.nop()
            act.wait_ge(f_pool, 1)
            for t in range(TT):
                A(row[:, t, :], h[:, t, :], ACT.Copy, scale=rstd[:, t:t + 1]).then_inc(f_act, 1)

        @block.vector
        def _(dve):
            seq = [0]

            def link(ins):
                seq[0] += 1
                ins.then_inc(dve_seq, 1)
                dve.wait_ge(dve_seq, seq[0])

            def drained(ins):
                ins.then_inc(dve_drained, 1)

            def settled(name):
                dve.wait_ge(dve_drained, DRAINS["dve"].index(name) + 1)

            def tt(out, a, b, op):
                return dve.tensor_tensor(out, a, b, op)

            def squares(src, junk, to):
                return dve.tensor_tensor_reduce(junk, src, src, 1.0, 0.0, ALU.mult, ALU.add, to)

            def mean_eps(a, n, width):
                return dve.tensor_scalar(ss[:, a:a + n], ss[:, a:a + n], 1.0 / width, EPS, ALU.mult, ALU.add)

            def norm_h(junk):
                for t in range(TT):
                    ins = squares(h[:, t, :], junk[:, t * D:(t + 1) * D], ss[:, t:t + 1])
                link(ins)
                mean_eps(0, 2, D).then_inc(ss_ready, 1)

            for ap, v in ((ql[64:128, 1, :], 0.0), (qz[:, :, :], 0.0), (hid[:, :, :], 0.0), (pc[:, :, :, :], 0.0),
                          (xc[:, :, :, :], NEG)):
                dve.memset(ap, v)
            dve.wait_ge(s_const, 80)
            for t in range(TT):
                ins = squares(row[:, t, :], xvf[:, t * D:(t + 1) * D], ss[:, t:t + 1])
            ins.then_inc(p_dve, 1)
            dve.wait_ge(p_dve, 1)
            mean_eps(0, 2, D).then_inc(p_dve, 1)
            dve.tensor_scalar(bigf[0:33, 512:518], bigf[0:33, 512:518], 8.0, None, ALU.mult).then_inc(p_dve, 1)
            dve.wait_ge(p_dve, 3)
            dve.tensor_copy(bigf[0:33, 640:1408].rearrange("p (h n) -> p h n", h=NH),
                            bigf[0:33, 512:518].unsqueeze(2).broadcast_to([33, NH, P])).then_inc(p_dve, 1)
            for hh in range(NH):
                dve.wait_ge(p_pe, 4 + hh + 1)
                dve.tensor_copy(bigf[:, 1408 + hh * 384:1408 + (hh + 1) * 384], banks[4 + hh % 4][:, 0:384]).then_inc(p_dve, 1)
            dve.wait_ge(p_pool, 2 + 0)

            with dve.Fori(0, L) as l:
                seq[0] = 0
                norm_h(xvf)
                q = [par[:, i, :] for i in range(16)]
                dt_, x1, th, kk, red, ab, mag, sn, cn, abr, abi, den, nr, fr, fi, tmp = q
                lr, li = cols[:, C_ARE:C_ARE + 8], cols[:, C_AIM:C_AIM + 8]
                dve.wait_ge(trig_ready, 1)
                tt(x1, lr, dt_, ALU.mult)
                link(tt(th, li, dt_, ALU.mult))
                magic = 12582912.0
                link(dve.tensor_scalar(kk, th, 1.0 / (2 * math.pi), magic, ALU.mult, ALU.add))
                link(dve.tensor_scalar(kk, kk, -magic, None, ALU.add))
                c1 = 6.28125
                c2 = float(np.float32(np.round((2 * math.pi - c1) * 2 ** 20) / 2 ** 20))
                c3 = 2 * math.pi - c1 - c2
                link(dve.scalar_tensor_tensor(red, kk, -c1, th, ALU.mult, ALU.add))
                link(dve.scalar_tensor_tensor(red, kk, -c2, red, ALU.mult, ALU.add))
                link(dve.scalar_tensor_tensor(red, kk, -c3, red, ALU.mult, ALU.add))
                link(dve.tensor_scalar(red, red, 3.1415925, -3.1415925, ALU.min, ALU.max))
                link(dve.tensor_scalar(ab, red, -1.0, None, ALU.mult))
                link(tt(ab, ab, red, ALU.min))
                dve.tensor_scalar(ab, ab, 1.0, math.pi / 2, ALU.mult, ALU.add).then_inc(par_ready, 1)
                tt(den, lr, lr, ALU.mult)
                link(tt(tmp, li, li, ALU.mult))
                link(tt(den, den, tmp, ALU.add))
                link(dve.reciprocal(den, den))
                dve.wait_ge(trig_ready, 4)
                tt(abr, mag, cn, ALU.mult)
                link(tt(abi, mag, sn, ALU.mult))
                link(dve.tensor_scalar(nr, abr, -1.0, None, ALU.add))
                tt(fr, nr, lr, ALU.mult)
                link(tt(tmp, abi, li, ALU.mult))
                link(tt(fr, fr, tmp, ALU.add))
                link(tt(fr, fr, den, ALU.mult))
                tt(fi, abi, lr, ALU.mult)
                link(tt(tmp, nr, li, ALU.mult))
                link(tt(fi, fi, tmp, ALU.subtract))
                link(tt(fi, fi, den, ALU.mult))
                frb, fib = (f.unsqueeze(2).broadcast_to([P, 8, 32]) for f in (fr, fi))
                t0 = pt[:, 0, 0:256].rearrange("p (j n) -> p j n", j=8)
                t1 = pt[:, 1, 0:256].rearrange("p (j n) -> p j n", j=8)
                tt(cp[:, 0], ct[:, 0], frb, ALU.mult)
                tt(t0, ct[:, 1], fib, ALU.mult)
                tt(cp[:, 1], ct[:, 0], fib, ALU.mult)
                link(tt(t1, ct[:, 1], frb, ALU.mult))
                tt(cp[:, 0], cp[:, 0], t0, ALU.subtract)
                dve.scalar_tensor_tensor(cp[:, 1], cp[:, 1], -1.0, t1, ALU.mult, ALU.subtract).then_inc(ct_ready, 1)
                link(dve.memset(kc[:, :, 2, :], 0.0))
                dve.tensor_copy(kc[:, :, 2, 0:32:2], cols[:, C_PE:C_PE + 32].rearrange("p (v m) -> p v m", v=2))

                wait_drained(dve, "zB")
                for t in range(TT):
                    squares(z[:, t, 0:192], pt[:, 0, t * 192:(t + 1) * 192], ss[:, 2 + t:3 + t])
                for t in range(TT):
                    ins = squares(z[:, t, 192:320], pt[:, 1, t * 128:(t + 1) * 128], ss[:, 4 + t:5 + t])
                link(ins)
                mean_eps(2, 2, 192)
                mean_eps(4, 2, 128).then_inc(ss_ready, 1)
                link(dve.tensor_scalar(gates, gates, 1.0, 0.5, ALU.add, ALU.mult))
                dve.memset(krp[:, :, 0:64], 0.0)

                def rotate(out, x1, x2, c, s, shape):
                    n = shape[1]
                    a, b = (rt[:, i, 0:n * 16].rearrange("p (h n) -> p h n", h=n) for i in range(2))
                    tt(a, x1, c, ALU.mult)
                    link(tt(b, x2, s, ALU.mult))
                    link(tt(out[0], a, b, ALU.subtract))
                    tt(a, x2, c, ALU.mult)
                    link(tt(b, x1, s, ALU.mult))
                    return tt(out[1], a, b, ALU.add)

                rotate((krp[:, :, 64:80], krp[:, :, 80:96]), z[:, :, 320:336], z[:, :, 336:352], cos2, sin2,
                       [P, 2, 16]).then_inc(rope_ready, 1)

                wait_tile(dve, l, "q0")
                b = bank("q0")[:, :].rearrange("p (m n) -> p m n", m=2)
                dve.tensor_copy(qz[0:64, 0:2, :], b[0:64])
                drained(dve.tensor_copy(qz[64:128, 3:5, :], b[64:128]))
                wait_tile(dve, l, "q1")
                dve.tensor_copy(qz[0:64, 2, :], bank("q1")[0:64, 0:256])
                dve.tensor_copy(qz[64:128, 5, :], bank("q1")[64:128, 0:256])
                drained(dve.tensor_copy(kslT[:, :], bank("q1")[:, 256:512]))
                wait_tile(dve, l, "cv")
                for gi in range(2):
                    b = bank("cv")[gi * 64:(gi + 1) * 64, 0:T]
                    dve.tensor_copy(kc[0:64, 1, gi, :], b)
                    ins = dve.tensor_copy(kc[64:128, 1, gi, 0:255], b[:, 1:256])
                drained(ins)
                wait_tile(dve, l, "vs")
                drained(dve.tensor_copy(vs[:, :, :], bank("vs")[:, :].rearrange("p (t n) -> p t n", t=2)))
                wait_tile(dve, l, "hid")
                b = bank("hid")
                for v in range(2):
                    ins = dve.tensor_copy(rt[0:64, 0, v:v + 1], b[0:64, v * 45 + 30:v * 45 + 31])
                link(ins)
                for v in range(2):
                    ins = dve.tensor_scalar(hid[:, v, :].rearrange("p (g n) -> p g n", g=2)[:, :, 0:NCMP],
                                            b[0:64, v * 45:v * 45 + 30].rearrange("p (g n) -> p g n", g=2),
                                            rt[0:64, 0, v:v + 1], None, ALU.add)
                drained(ins)
                for t in range(TT):
                    settled(("hid", "qr0")[t])
                    wait_tile(dve, l, f"qr{t}")
                    b = bank(f"qr{t}")[:, 0:192].rearrange("p (h n) -> p h n", h=NH)
                    c, s = (x[:, t, :].unsqueeze(1).broadcast_to([P, NH, 16]) for x in (cos2, sin2))
                    drained(rotate((qrow[:, t, :, 64:80], qrow[:, t, :, 80:96]), b[:, :, 0:16], b[:, :, 16:32], c, s, [P, NH, 16]))
                wait_tile(dve, l, "kcv")
                b = bank("kcv")
                dve.tensor_copy(kcT[:, :], b[:, 0:16])
                drained(tt(vbd[:, :].rearrange("p (h n) -> p h n", h=NH), b[0:96, 16:80].unsqueeze(1).broadcast_to([96, NH, 64]),
                           cs("vcm")[0:96, :].unsqueeze(2).broadcast_to([96, NH, 64]), ALU.mult))
                wait_tile(dve, l, "sc")
                b = bank("sc")[:, 0:192].rearrange("p (t h n) -> p t h n", t=2, h=NH)
                tt(xc[:, 0, :, 0:7], b[:, 0, :, 0:7], btab[:, :, 159:256:CSTRIDE], ALU.add)
                ins = tt(xc[:, 1, :, 0:NCMP], b[:, 1, :, 0:NCMP], btab[:, :, 31:256:CSTRIDE], ALU.add)
                drained(ins)
                settled("sc")
                cmx3 = cmx.rearrange("p (t h) -> p t h", t=2)
                csum3 = csum.rearrange("p (t h) -> p t h", t=2)
                link(dve.tensor_reduce(cmx3, xc[:, :, :, 0:NCMP], AX.X, ALU.max))
                tt(pc[:, :, :, 0:NCMP], xc[:, :, :, 0:NCMP], cmx3.unsqueeze(3).broadcast_to([P, TT, NH, NCMP]),
                   ALU.subtract).then_inc(cmp_ready, 1)
                dve.wait_ge(cexp_ready, 1)
                link(dve.tensor_reduce(csum3, pc[:, :, :, 0:NCMP], AX.X, ALU.add))
                link(dve.reciprocal(csum, csum))
                link(tt(csum3, csum3, gates[:, :, 0:NH], ALU.mult))
                link(tt(csum3, csum3, cs("okc").unsqueeze(2).broadcast_to([P, TT, NH]), ALU.mult))
                wait_tile(dve, l, "qT2")
                for t in range(TT):
                    wait_tile(dve, l, f"oc{t}")
                    drained(tt(row[:, t, 640:1024].rearrange("p (h n) -> p h n", h=NH),
                               bank(f"oc{t}")[:, 0:384].rearrange("p (h n) -> p h n", h=NH),
                               csum3[:, t, :].unsqueeze(2).broadcast_to([P, NH, 64]), ALU.mult))

                def masked_scores(i):
                    wait_tile(dve, l, f"s{i}")
                    if i >= 4:
                        wait_tile(dve, l, f"pT{i - 4}")
                    b, p = bank(f"s{i}"), prob[:, i % 4, :]
                    m = cmask if i < NH else btab[:, i % NH, :]
                    sc = -float(QK) ** -0.5 if i < NH else -float(HD) ** -0.5
                    dve.tensor_tensor_reduce(p[:, 0:128], b[:, 0:128], m[:, 128:256], sc, 3.0e38, ALU.add, ALU.min,
                                             mx[:, 2 * i:2 * i + 1])
                    drained(dve.tensor_tensor_reduce(p[:, 128:384], b[:, 128:384], m, sc, 3.0e38, ALU.add, ALU.min,
                                                     mx[:, 2 * i + 1:2 * i + 2]))

                def states(j):
                    wait_tile(dve, l, f"bu{j}")
                    if j == 0:
                        dve.wait_ge(ftab_ready, 1)
                    b = bank(f"bu{j}")[:, :].rearrange("p (c n) -> p c n", c=2)
                    f0, f1 = (ftab[:, c, j, :].unsqueeze(1).broadcast_to([P, 2, T]) for c in range(2))
                    if j >= 2:
                        dve.wait_ge(g_free, j - 1)
                    gg = g[:, j % 2]
                    tt(tmpd[:, 0:2, :], b, f0, ALU.mult)
                    drained(tt(tmpd[:, 2:4, :], b, f1, ALU.mult))
                    settled(f"bu{j}")
                    tt(gg[:, 0, :], tmpd[:, 0, :], tmpd[:, 3, :], ALU.add)
                    link(tt(gg[:, 1, :], tmpd[:, 1, :], tmpd[:, 2, :], ALU.subtract))
                    for c in range(2):
                        ins = dve.tensor_tensor_scan(gg[:, c, :], mag[:, j:j + 1].broadcast_to([P, T]), gg[:, c, :], 0.0,
                                                     ALU.mult, ALU.add)
                    ins.then_inc(scan_ready, 1)

                def group_outputs(n):
                    dve.wait_ge(prob_ready, NH * (n + 1))
                    s3 = sums[:, 12 * n:12 * n + 12].rearrange("p (h t) -> p t h", t=2)
                    r3 = rinv[:, 12 * n:12 * n + 12].rearrange("p (t h) -> p t h", t=2)
                    link(dve.reciprocal(r3, s3))
                    if n:
                        link(tt(r3, r3, gates[:, :, n * NH:(n + 1) * NH], ALU.mult))
                    dve.wait_ge(pe_note, NH * (n + 1))
                    for t in range(TT):
                        o = ob[t][:, 0:384].rearrange("p (h n) -> p h n", h=NH)
                        w = r3[:, t, :].unsqueeze(2).broadcast_to([P, NH, 64])
                        a = (256, 640, 640)[n]
                        to = row[:, t, a:a + 384]
                        if n == 0:
                            tt(to.rearrange("p (h n) -> p h n", h=NH), o, w, ALU.mult).then_inc(o_read, 1)
                        else:
                            x = tmpdf[:, t * 512:t * 512 + 384]
                            tt(x.rearrange("p (h n) -> p h n", h=NH), o, w, ALU.mult).then_inc(o_read, 1)
                            dve.wait_ge(o_read, TT * n + t + 1)
                            link(tt(to, to, x, ALU.add))

                for i in range(LEAD):
                    masked_scores(i)
                for i in range(HEADS):
                    if i + LEAD < HEADS:
                        masked_scores(i + LEAD)
                    if i in STATES:
                        states(STATES[i])
                    if i in (NH, 2 * NH):
                        group_outputs(i // NH - 1)
                group_outputs(2)

                dve.wait_ge(g_free, 8)
                for c in range(2):
                    dve.scalar_tensor_tensor(uT[:, c, :], uT[:, c, :], cols[:, C_D + c:C_D + c + 1], yb[:, c * T:(c + 1) * T],
                                             ALU.mult, ALU.add).then_inc(ys_pre, 1)
                wait_tile(dve, l, "yr")
                wait_drained(dve, "gl")
                y3 = row[:, :, 0:256]
                drained(dve.scalar_tensor_tensor(y3, col[:, 0:2, :], 1.0, bank("yr")[:, :].rearrange("p (t n) -> p t n", t=2),
                                                 ALU.add, ALU.mult))
                settled("yr")
                link(dve.tensor_scalar(y3, y3, 0.5, None, ALU.mult))
                for s, (a, n) in enumerate(((0, 256), (256, 384), (640, 384))):
                    for t in range(TT):
                        ins = squares(row[:, t, a:a + n], w1f[:, t * D + a:t * D + a + n], ss[:, 2 * s + t:2 * s + t + 1])
                link(ins)
                mean_eps(0, 2, 256)
                mean_eps(2, 4, 384).then_inc(ss_ready, 1)

                def add_to_h(stage):
                    for n in range(2):
                        for t in range(TT):
                            wait_tile(dve, l, f"{stage}{n}_{t}")
                            hs = h[:, t, n * 512:(n + 1) * 512]
                            drained(tt(hs, hs, bank(f"{stage}{n}_{t}")[:, :], ALU.add))
                    settled(f"{stage}1_1")

                add_to_h("wo")
                norm_h(w1f)
                for i in range(XH):
                    wait_tile(dve, l, f"xs{i}")
                    link(dve.tensor_reduce(xmx[:, 2 * i:2 * i + 2], bank(f"xs{i}")[:, :].rearrange("p (t n) -> p t n", t=2),
                                           AX.X, ALU.max))
                    dve.tensor_scalar(xnm[:, 2 * i:2 * i + 2], xmx[:, 2 * i:2 * i + 2], -0.0625, None,
                                      ALU.mult).then_inc(xmax_ready, 1)
                for i in range(XH):
                    wait_drained(dve, f"xs{i}")
                    link(dve.reciprocal(xri[:, 2 * i:2 * i + 2], xsum[:, 2 * i:2 * i + 2]))
                    for t in range(TT):
                        p = xprob[:, i % 3, t * T:(t + 1) * T]
                        ins = dve.tensor_scalar(p, p, xri[:, 2 * i + t:2 * i + t + 1], None, ALU.mult)
                    ins.then_inc(xprob_ready, 1)
                    wait_tile(dve, l, f"xp{i}")
                    if i >= 2:
                        wait_tile(dve, l, f"xo{i - 2}")
                    drained(dve.tensor_copy(pt[:, i % 2, :], bank(f"xp{i}")[:, :]))
                add_to_h("xw")
                norm_h(w1f)

                with dve.If(l == 0):
                    dense_dve(dve)
                with dve.Else():
                    route_on_dve(dve)
                    moe_dve(dve, moe[0], 0)
                dve.drain().then_inc(arrived, 1)
                dve.wait_ge(go, l + 1)

            dve.sem_inc(flag_again, 1)
            v = dve.value_load(flag[0:1, 0:1], min_val=0, max_val=1)
            with dve.If(v == 1):
                moe_dve(dve, moe[1], 1)
            with dve.Else():
                dve.nop()
            for t in range(TT):
                squares(h[:, t, :], bigf[:, t * D:(t + 1) * D], ss[:, t:t + 1]).then_inc(f_dve, 1)
            dve.wait_ge(f_dve, 2)
            mean_eps(0, 2, D).then_inc(f_dve, 1)
            dve.wait_ge(fg_landed, 16)
            fg = memraw[:, 0:4, :].rearrange("p k n -> p (k n)")
            for t in range(TT):
                dve.wait_ge(f_act, t + 1)
                tt(row[:, t, :], row[:, t, :], fg, ALU.mult).then_inc(final_ready, 1)

        @block.gpsimd
        def _(pool):
            seq = [0]

            def link(ins):
                seq[0] += 1
                ins.then_inc(pool_seq, 1)
                pool.wait_ge(pool_seq, seq[0])

            def tt(out, a, b, op):
                return pool.tensor_tensor(out, a, b, op)

            def power(a, n, counter):
                tt(rstd[:, a:a + n], ss[:, a:a + n], half[:, 0:1].broadcast_to([P, n]), ALU.pow).then_inc(counter, 1)

            pool.dma_start(lp[:, :], lparams[0]).then_inc(lp_landed, 16)
            pool.wait_ge(s_const, 80)
            pool.wait_ge(p_dve, 2)
            power(0, 2, p_pool)
            pool.wait_ge(p_dve, 4 + NH)
            pool.dma_start(scratch[:, :, :].rearrange("h p n -> p h n"),
                           bigf[:, 1408:1408 + NH * 384].rearrange("p (h n) -> p h n", h=NH)).then_inc(s_scr, 16)
            pool.wait_ge(s_scr, 16)
            skew = bass.AP(scratch.tensor, 127, [[383, P], [P * 384, NH], [1, T]])
            pool.dma_start(btab[:, :, :], skew).then_inc(s_scr, 16)
            pool.wait_ge(s_scr, 32)
            pool.sem_inc(p_pool, 1)

            with pool.Fori(0, L) as l:
                seq[0] = 0
                pool.wait_ge(ss_ready, 1)
                power(0, 2, rstd_ready)
                pool.wait_ge(trig_ready, 4)
                re, im = ftab[:, 0], ftab[:, 1]
                pool.tensor_copy(re[:, :, 0:1], par[:, 8, :].unsqueeze(2))
                link(pool.tensor_copy(im[:, :, 0:1], par[:, 7, :].unsqueeze(2)))

                def double(m):
                    a, b = (f[:, :, m - 1:m].broadcast_to([P, 8, m]) for f in (re, im))
                    x = xkf[:, 0:8 * m].rearrange("p (j n) -> p j n", j=8)
                    y = xkf[:, 1024:1024 + 8 * m].rearrange("p (j n) -> p j n", j=8)
                    tt(re[:, :, m:2 * m], re[:, :, 0:m], a, ALU.mult)
                    tt(x, im[:, :, 0:m], b, ALU.mult)
                    tt(im[:, :, m:2 * m], re[:, :, 0:m], b, ALU.mult)
                    link(tt(y, im[:, :, 0:m], a, ALU.mult))
                    tt(re[:, :, m:2 * m], re[:, :, m:2 * m], x, ALU.subtract)
                    return tt(im[:, :, m:2 * m], im[:, :, m:2 * m], y, ALU.add)

                for m in (1, 2, 4, 8, 16, 32):
                    link(double(m))
                pool.wait_ge(ss_ready, 2)
                power(2, 4, rstd_ready)
                link(double(64))
                double(128).then_inc(ftab_ready, 1)
                wait_tile(pool, l, "vs")
                pool.sem_inc(pool_note, 1)
                for k in range(KD):
                    pool.tensor_scalar(memT[:, k, :], memraw[:, k, :], cols[:, C_MEM + k:C_MEM + k + 1], None,
                                       ALU.mult).then_inc(memT_ready, 1)
                for j in range(8):
                    pool.wait_ge(scan_ready, j + 1)
                    gg = g[:, j % 2]
                    f0, f1 = (ftab[:, c, j, :].unsqueeze(1).broadcast_to([P, 2, T]) for c in range(2))
                    tt(tmpp[:, 0:2, :], gg, f0, ALU.mult)
                    link(tt(tmpp[:, 2:4, :], gg, f1, ALU.mult))
                    tt(gg[:, 0, :], tmpp[:, 0, :], tmpp[:, 3, :], ALU.subtract)
                    link(tt(gg[:, 1, :], tmpp[:, 1, :], tmpp[:, 2, :], ALU.add))
                    pool.sem_inc(state_ready, 1)
                pool.wait_ge(ss_ready, 3)
                power(0, 6, rstd_ready)
                pool.wait_ge(ss_ready, 4)
                power(0, 2, rstd_ready)
                pool.wait_ge(ss_ready, 5)
                power(0, 2, rstd_ready)
                with pool.If(l == 0):
                    pool.wait_ge(act_drained, len(DRAINS["act"]))
                    pool.dma_start(lp[:, :], lparams[1]).then_inc(lp_landed, 16)
                    pool.wait_ge(lp_landed, 32)
                with pool.Else():
                    pool.nop()
                pool.wait_ge(arrived, 3 * l + 3)
                pool.sem_inc(pool_note, 1)
                pool.sem_clear(clear_range)
                pool.sem_inc(go, 1)

            pool.dma_start(memraw[:, 0:4, :].rearrange("p k n -> p (k n)"), fgain.broadcast_to([P, D])).then_inc(fg_landed, 16)
            pool.wait_ge(f_dve, 3)
            power(0, 2, f_pool)
            pool.wait_ge(fg_landed, 16)


def constants():
    c = np.zeros((P, CSW), np.float32)

    def put(name, a):
        at, w = CS[name]
        c[:a.shape[0], at:at + w] = a

    p = np.arange(P)
    put("ident", np.eye(P, dtype=np.float32))
    causal = np.zeros((P, 256), np.float32)
    causal[:, 128:] = np.where(p[None, :] <= p[:, None], 0.0, NEG)
    put("cmask", causal)
    pos = np.arange(T, dtype=np.float32)
    inv = (1.0 / (np.float32(10000.0) ** (np.arange(0, ROPE, 2, dtype=np.float32) / np.float32(ROPE)))).astype(np.float32)
    ang = (pos[:, None] * inv[None, :]).astype(np.float32)
    rope = np.concatenate([f(ang).astype(np.float32).reshape(TT, P, 16).transpose(1, 0, 2).reshape(P, 32)
                           for f in (np.cos, np.sin)], axis=1)
    put("rope", rope)
    put("before", (p[:, None] < p[None, :]).astype(np.float32))
    put("ones", np.ones((P, P), np.float32))
    put("iota", np.broadcast_to(np.arange(256, dtype=np.float32), (P, 256)))
    put("iota8", np.broadcast_to(np.arange(8, dtype=np.float32), (P, 8)))
    put("okc", np.stack([(p >= 31), np.ones(P)], axis=1).astype(np.float32))
    put("vcm", (p[:96, None] // 16 == np.arange(NH)[None, :]).astype(np.float32))
    put("half", np.full((P, 4), -0.5, np.float32))
    dist = 255 - np.arange(384)
    exact = BUCKETS // 2
    n = np.maximum(dist, 0)
    nf = np.maximum(n, exact).astype(np.float32)
    large = exact + (np.log(nf / np.float32(exact)) / np.float32(math.log(MAX_DIST / exact)) * np.float32(BUCKETS - exact)).astype(np.int32)
    bucket = np.where(n < exact, n, np.minimum(large, BUCKETS - 1))
    one = np.zeros((33, 512), np.float32)
    one[np.where(dist >= 0, bucket, 32), np.arange(384)] = 1.0
    return c, one


def blocks(w):
    return w.reshape(-1, P, w.shape[-1]).transpose(1, 0, 2)


def pack_weights(a):
    out = np.zeros((CHUNKS, P, SLOT), np.float32)
    c = 0

    def put(x):
        nonlocal c
        x = x.reshape(P, -1)
        out[c, :, :x.shape[1]] = x
        c += 1

    def put_pair(w, n):
        b = blocks(w[:, n * 512:(n + 1) * 512])
        put(b[:, 0:4])
        put(b[:, 4:8])

    def ffn(wg, wu, wd, pieces):
        def gu(i):
            s = slice(i * PIECE, (i + 1) * PIECE)
            b = np.concatenate([blocks(wg[:, s]), blocks(wu[:, s])], axis=2)
            put(b[:, 0:4])
            put(b[:, 4:8])

        def down(i):
            put(blocks(wd[i * PIECE:(i + 1) * PIECE]))

        gu(0)
        for i in range(pieces - 1):
            gu(i + 1)
            down(i)
        down(pieces - 1)

    for l in range(L):
        w = a["w_in"][l]
        kv = 992

        def take(*ranges):
            x = np.concatenate([w[:, s:e] for s, e in ranges], axis=1)
            if x.shape[1] < 256:
                x = np.concatenate([x, np.zeros((D, 256 - x.shape[1]), np.float32)], axis=1)
            put(blocks(x))

        def q(i):
            return 608 + i * 64, 608 + (i + 1) * 64

        take((0, 256))
        take((256, 512))
        take((512, 608), (1760, 1778), (kv + 512, kv + 640))
        take(q(0), q(3), q(1), q(4))
        take(q(2), q(5), (kv + 256, kv + 384))
        take((kv, kv + 256))
        take((kv + 384, kv + 512), (kv + 640, kv + 768))
        wkv = a["xattn_wkv"][l]
        for i in range(XH):
            put(blocks(wkv[:, i * 256:(i + 1) * 256]))
        for n in range(2):
            put_pair(wkv[:, D:], n)
        for n in range(2):
            put_pair(a["w_out"][l], n)
        for i in range(XH):
            put(blocks(a["xattn_wq"][l][:, i * 256:(i + 1) * 256]))
        for n in range(2):
            put_pair(a["xattn_wo"][l], n)
        if l % 2 == 0:
            ffn(a["dense_w_gate"][l // 2], a["dense_w_up"][l // 2], a["dense_w_down"][l // 2], DENSE_PIECES)
        else:
            for e in range(NE):
                ffn(a["moe_w_gate"][l // 2][e], a["moe_w_up"][l // 2][e], a["moe_w_down"][l // 2][e], MOE_PIECES)
    assert c == CHUNKS
    return out


def pack_layer(a, l):
    out = np.zeros((P, LPW), np.float32)

    def put(name, x, off=0):
        at, w = LP[name]
        x = x.reshape(x.shape[0], -1)
        out[:x.shape[0], at + off:at + off + x.shape[1]] = x

    def column(x):
        return x.reshape(-1, P).T

    c = LP["cols"][0]
    for at, name in ((C_MIX, "mix_norm"), (C_OUT, "out_norm"), (C_XN, "xattn_norm"), (C_MEM, "mem_norm"), (C_FFN, "ffn_norm"),
                     (C_ARE, "ssm_a_re"), (C_AIM, "ssm_a_im"), (C_D, "ssm_d"), (C_KVN, "mla_kv_norm")):
        x = column(a[name][l])
        out[:, c + at:c + at + x.shape[1]] = x
    out[:, c + C_LDT:c + C_LDT + 8] = column(np.repeat(a["ssm_log_dt"][l], 64))
    qn = a["mla_q_norm"][l]
    out[:, c + C_QN] = qn[:P]
    out[:64, c + C_QN + 1] = qn[P:]
    for v in range(2):
        out[:, c + C_PE + v * NPAIR:c + C_PE + (v + 1) * NPAIR] = column(a["nsa_cmp_pe"][l, v])
        put("w1", blocks(a["nsa_cmp_w1"][l, v]), v * NPAIR * 64)
        put("w2", a["nsa_cmp_w2"][l, v], v * 64)
    put("glu", blocks(a["ssm_w_glu"][l]))
    uq = a["mla_w_uq"][l].reshape(192, NH, QK)
    uq = np.concatenate([uq[:, :, :NOPE].reshape(192, -1), uq[:, :, NOPE:].reshape(192, -1)], axis=1)
    put("uq", uq[:P])
    put("uq", uq[P:], 576)
    ukv = a["mla_w_ukv"][l].reshape(P, NH, 2, 64)
    put("ukv", ukv[:, :, 0].reshape(P, -1))
    put("ukv", ukv[:, :, 1].reshape(P, -1), 384)
    bt = np.zeros((P, 8, 2, P), np.float32)
    ct = np.zeros((P, 2, 8, 32), np.float32)
    for gi in range(16):
        j, s = gi // 2, (gi % 2) * 64
        r = 16 * (gi % 8)
        o = 16 * (gi % 2)
        for i, (bn, cn) in enumerate((("ssm_b_re", "ssm_c_re"), ("ssm_b_im", "ssm_c_im"))):
            bt[r:r + 16, j, i, s:s + 64] = a[bn][l, gi].T
            ct[s:s + 64, i, j, o:o + 16] = a[cn][l, gi].T
    put("bt", bt)
    put("ct", ct)
    return out


def kernel(**inputs):
    import concourse.bacc as bacc
    from concourse.bass_utils import run_bass_kernel_spmd

    a = {k: np.asarray(v) for k, v in inputs.items()}
    cst, onehot = constants()
    at, w = CS["router"]
    cst[:, at:at + w] = blocks(a["moe_router"][0]).reshape(P, w)
    relb = np.concatenate([a["rel_bias"], np.full((1, NH), NEG / 8, np.float32)], axis=0)
    arrays = {
        "x": np.ascontiguousarray(a["x"][0]), "mem": np.ascontiguousarray(a["mem"][0]),
        "weights": pack_weights(a), "lparams": np.stack([pack_layer(a, l) for l in range(L)]),
        "consts": cst, "onehot": onehot, "relb": relb, "fgain": a["final_norm"][None, :],
    }
    nc = bacc.Bacc("TRN2", target_bir_lowering=False, num_devices=1)
    t = {k: nc.dram_tensor(f"in_{k}", v.shape, F32, kind="ExternalInput").ap() for k, v in arrays.items()}
    out = nc.dram_tensor("out_0", (T, D), F32, kind="ExternalOutput").ap()
    scratch = nc.dram_tensor("skewed_bias", (NH, P, 384), F32, kind="Internal").ap()
    trunk(nc, t["x"], t["mem"], t["weights"], t["lparams"], t["consts"], t["onehot"], t["relb"], t["fgain"], out, scratch)
    r = run_bass_kernel_spmd(nc, [{f"in_{k}": v for k, v in arrays.items()}], core_ids=[0])
    return r.results[0]["out_0"].reshape(1, T, D)
```

```python
import math
from contextlib import ExitStack

import concourse.bass as bass
from concourse import mybir
import numpy as np

ALU = mybir.AluOpType
ACT = mybir.ActivationFunctionType
AX = mybir.AxisListType
F32 = mybir.dt.float32
F32R = mybir.dt.float32r
U32 = mybir.dt.uint32
I32 = mybir.dt.int32

P = 128
D = 1024
KD = D // P
T = 256
TT = T // P
L = 2
NH = 6
HD = 64
NOPE, ROPE = 64, 32
QK = NOPE + ROPE
NCMP = 15
CSTRIDE = 16
NPAIR = 16
XH = 4
FD, FE = 2816, 3584
NE = 8
PIECE = 256
DENSE_PIECES, MOE_PIECES = FD // PIECE, FE // PIECE
EPS = 1e-6
NEG = -1e30
BUCKETS, MAX_DIST = 32, 128

RING = 6
SLOT = 2048
COMMON = 27
DENSE_CHUNKS = 3 * DENSE_PIECES
MOE_CHUNKS = 3 * MOE_PIECES
LAYER_CHUNKS = COMMON + DENSE_CHUNKS
assert LAYER_CHUNKS % RING == 0 and MOE_CHUNKS % RING == 0
CHUNKS = LAYER_CHUNKS + COMMON + NE * MOE_CHUNKS
MOE_FIRST = LAYER_CHUNKS + COMMON

LP = {}
_at = 0
for _n, _w in (("cols", 101), ("glu", 2 * 256), ("uq", 2 * 576), ("ukv", 768), ("w1", 2 * NPAIR * 64), ("w2", 2 * 64),
               ("bt", 2048), ("ct", 2 * 8 * 32)):
    LP[_n] = (_at, _w)
    _at += _w
LPW = _at
C_MIX, C_OUT, C_XN, C_MEM, C_FFN = 0, 8, 16, 24, 32
C_ARE, C_AIM, C_LDT, C_D, C_KVN, C_QN, C_PE = 40, 48, 56, 64, 66, 67, 69
assert C_PE + 2 * NPAIR == LP["cols"][1]
CS = {}
_at = 0
for _n, _w in (("ident", 128), ("cmask", 256), ("rope", 64), ("before", 128), ("ones", 128), ("iota", 256), ("iota8", 8),
               ("okc", 2), ("vcm", 6), ("half", 4), ("router", 64)):
    CS[_n] = (_at, _w)
    _at += _w
CSW = _at

ROT = 5
JOBS = []


def _job(name, eng, chunk=None):
    JOBS.append((name, eng, chunk))


for _i in range(4):
    _job(f"hT{_i}", "act")
for _i, (_n, _e) in enumerate((("u", "act"), ("zA", "act"), ("zB", "act"), ("q0", "dve"), ("q1", "dve"))):
    _job(_n, _e, _i)
_job("ck", "act")
_job("cv", "dve", 5)
_job("vs", "dve", 6)
for _n, _e in (("cqT", "act"), ("ckvT", "act"), ("hid", "dve"), ("qn0", "act"), ("qr0", "dve"), ("qn1", "act"),
               ("qr1", "dve"), ("kn0", "act"), ("kn1", "act"), ("kn2", "act"), ("vm0", "act"), ("vm1", "act"),
               ("kcv", "dve"), ("qT0", "act"), ("qT1", "act"), ("qT2", "act"), ("sc", "dve"), ("pcT", "act"),
               ("oc0", "dve"), ("oc1", "dve")):
    _job(_n, _e)
HEADS = 18
LEAD = 3
SPLIT_FIRST = 15
MEMK = {2: 0, 6: 1, 10: 2, 14: 3}
STATES = {1 + 2 * _i: _i for _i in range(8)}
for _i in range(LEAD):
    _job(f"s{_i}", "dve")
for _i in range(HEADS):
    if _i + LEAD < HEADS:
        _job(f"s{_i + LEAD}", "dve")
    if _i in MEMK:
        _job(f"mk{MEMK[_i]}", "act", 7 + MEMK[_i])
    if _i in STATES:
        _job(f"bu{STATES[_i]}", "dve")
    _job(f"pT{_i}", "act")
_job("mv0_0", "act")
_job("mv0_1", "act", 12)
_job("yr", "dve")
_job("gl", "act")
_job("mv1_0", "act")
_job("mv1_1", "act", 14)
for _i in range(4):
    _job(f"yT{_i}", "dve")
for _i in range(2):
    _job(f"wo{_i}_0", "dve")
    _job(f"wo{_i}_1", "dve", 16 + 2 * _i)
for _i in range(4):
    _job(f"xT{_i}", "dve")
for _i in range(4):
    _job(f"xq{_i}", "act", 19 + _i)
for _i in range(XH):
    _job(f"xs{_i}", "act")
_job("xp0", "dve")
for _i in range(XH):
    if _i + 1 < XH:
        _job(f"xp{_i + 1}", "dve")
    _job(f"xo{_i}", "dve")
for _i in range(2):
    _job(f"xw{_i}_0", "dve")
    _job(f"xw{_i}_1", "dve", 24 + 2 * _i)
for _i in range(4):
    _job(f"fT{_i}", "act")
NAMES = [j[0] for j in JOBS]
assert len(set(NAMES)) == len(NAMES)
DRAINS = {e: [j[0] for j in JOBS if j[1] == e] for e in ("act", "dve")}
PLAIN = [j[0] for j in JOBS if j[2] is None]


def trunk(nc, x, mem, weights, lparams, consts, onehot, relb, fgain, out, scratch):
    with ExitStack() as ctx:
        place = {}

        def sb(name, shape, dt=F32):
            place[name] = (nc.sbuf_base + 31) // 32 * 32
            return ctx.enter_context(nc.sbuf_tensor(name, shape, dt))

        def over(name, shape, of, at=0):
            return nc.alloc_sbuf_tensor_at(name, shape, F32R, offset=place[of] + 4 * at)

        def sem(name):
            return ctx.enter_context(nc.semaphore(name))

        ring = sb("ring", [P, RING, SLOT])
        attn = sb("attn", [P, 3 * SLOT])
        h = sb("h", [P, TT, D])
        row = sb("row", [P, TT, D])
        col = sb("col", [P, KD, T])
        memraw = sb("memraw", [P, KD, T])
        btab = sb("btab", [P, NH, T])
        cst = sb("cst", [P, CSW])
        lp = sb("lp", [P, LPW])
        big = sb("big", [P, 2, 8, T])
        g = sb("g", [P, 2, 2, T])
        ql = sb("ql", [P, 2, T])
        ckvT = sb("ckvT", [P, T])
        qT = attn[0:QK, 0:NH * T].rearrange("p (h n) -> p h n", h=NH)
        kT = attn[0:QK, NH * T:2 * NH * T].rearrange("p (h n) -> p h n", h=NH)
        vm = sb("vm", [P, TT, 384])
        uT = sb("uT", [P, 2, T])
        qz = attn[:, 2 * NH * T:3 * NH * T].rearrange("p (h n) -> p h n", h=NH)
        kslT = sb("kslT", [P, T])
        kwnT = sb("kwnT", [P, T])
        vs = sb("vs", [P, TT, T])
        kc = attn[:, 3 * NH * T:4 * NH * T].rearrange("p (a b n) -> p a b n", a=2, b=3)
        pt = sb("pt", [P, 2, 512])
        xk = sb("xk", [P, KD, T])
        xv = sb("xv", [P, TT, D])
        small = sb("small", [P, 512])
        cp = sb("cp", [P, 2, 8, 32])
        rt = sb("rt", [P, 2, 96])
        kcT = sb("kcT", [P, 16])
        pcs = sb("pcs", [96, T])
        hid = sb("hid", [HD, 2, 32])
        hidr = sb("hidr", [HD, 96])
        vbd = sb("vbd", [96, 384])
        xc = sb("xc", [P, TT, NH, 16])
        pc = sb("pc", [P, TT, NH, 16])
        eight = sb("eight", [P, 16])
        upper = over("upper", [P, 3, SLOT], "attn")
        lower = over("lower", [P, RING, SLOT], "ring")
        colu = over("colu", [P, KD, T], "xv")
        coll = over("coll", [P, KD, T], "xk")
        xeu = over("xeu", [P, KD, P], "xk")
        xel = over("xel", [P, KD, P], "g")
        htu = over("htu", [P, 2, 512], "big", 1024)
        htl = over("htl", [P, 2, 512], "pt")
        colr = over("colr", [P, KD, T], "col")
        xor = over("xor", [P, KD, T], "big", KD * T)
        idx = sb("idx", [P, 8], U32)
        flag = sb("flag", [1, 1], I32)

        def cs(name):
            a, w = CS[name]
            return cst[:, a:a + w]

        def lpv(name):
            a, w = LP[name]
            return lp[:, a:a + w]

        ident = cs("ident")
        cmask = cs("cmask")
        cos2 = cs("rope")[:, 0:32].rearrange("p (t c) -> p t c", t=2)
        sin2 = cs("rope")[:, 32:64].rearrange("p (t c) -> p t c", t=2)
        half = cs("half")
        cols = lpv("cols")
        glu = lpv("glu").rearrange("p (k n) -> p k n", k=2)
        uq = lpv("uq").rearrange("p (k n) -> p k n", k=2)
        ukv = lpv("ukv")
        w1 = lpv("w1").rearrange("p (v m n) -> p v m n", v=2, m=NPAIR)
        w2 = lpv("w2").rearrange("p (v n) -> p v n", v=2)
        bt = lpv("bt").rearrange("p (j c n) -> p j c n", j=8, c=2)
        ct = lpv("ct").rearrange("p (c j n) -> p c j n", c=2, j=8)
        rowf = row[:, :, :].rearrange("p t n -> p (t n)")
        z = rowf[:, 0:704].rearrange("p (t n) -> p t n", t=2)
        krp = rowf[:, 704:896].rearrange("p (t n) -> p t n", t=2)
        qrow = rowf[:, 896:2048].rearrange("p (t h n) -> p t h n", t=2, h=NH)
        prob = kc[:, :, :, :].rearrange("p a b n -> p (a b n)")[:, 0:1536].rearrange("p (b n) -> p b n", b=4)
        ftab = big
        bigf = big[:, :, :, :].rearrange("p a b n -> p (a b n)")
        memT = col
        w1f = lpv("w1")
        tmpd = w1f[:, 0:1024].rearrange("p (a n) -> p a n", a=4)
        tmpdf = w1f[:, 0:1024]
        tmpp = w1f[:, 1024:2048].rearrange("p (a n) -> p a n", a=4)
        kcf = kc[:, :, :, :].rearrange("p a b n -> p (a b n)")
        xprob = kcf.rearrange("p (b n) -> p b n", b=3)
        xkf = xk[:, :, :].rearrange("p k n -> p (k n)")
        xvf = xv[:, :, :].rearrange("p k n -> p (k n)")
        xq = big[:, 0, :, :]
        xo = big[:, 1, :, :]
        ss = small[:, 0:8]
        rstd = small[:, 8:16]
        gates = small[:, 16:52].rearrange("p (t n) -> p t n", t=2)
        mx = small[:, 52:92]
        sums = small[:, 92:132]
        rinv = small[:, 172:212]
        par = small[:, 248:376].rearrange("p (k n) -> p k n", k=16)
        cmx = small[:, 376:388]
        csum = small[:, 388:400]
        xmx = small[:, 404:412]
        xsum = small[:, 412:420]
        xnm = small[:, 420:428]
        xri = small[:, 428:436]
        ssh = small[:, 436:440]

        banks = [ctx.enter_context(nc.psum_tensor(f"bank{i}", [P, 512], F32)) for i in range(8)]
        ob = [banks[5], banks[6]]
        yb = banks[7]

        landed = [sem(f"landed{i}") for i in range(RING)]
        weights_used = sem("weights_used")
        mem_landed = sem("mem_landed")
        x_landed = sem("x_landed")
        cst_landed = sem("cst_landed")
        bias_landed = sem("bias_landed")
        cols_landed = sem("cols_landed")
        lp_landed = sem("lp_landed")
        next_lp_landed = sem("next_lp_landed")
        s_scr = sem("s_scr")
        s_out = sem("s_out")
        arrived = sem("arrived")
        go = sem("go")
        per_layer = []

        def lsem(name):
            s = sem(name)
            per_layer.append(s)
            return s

        mm_done = lsem("mm_done")
        act_drained = lsem("act_drained")
        dve_drained = lsem("dve_drained")
        act_seq = lsem("act_seq")
        dve_seq = lsem("dve_seq")
        pool_seq = lsem("pool_seq")
        pe_note = lsem("pe_note")
        ss_ready = lsem("ss_ready")
        rstd_ready = lsem("rstd_ready")
        z_ready = lsem("z_ready")
        scan_ready = lsem("scan_ready")
        ar1 = lsem("ar1")
        pool_note = lsem("pool_note")
        wt_upper = lsem("wt_upper")
        wt_split = lsem("wt_split")
        tr_upper = lsem("tr_upper")
        row_ready = lsem("row_ready")
        memT_ready = lsem("memT_ready")
        rope_ready = lsem("rope_ready")
        par_ready = lsem("par_ready")
        trig_ready = lsem("trig_ready")
        ftab_ready = lsem("ftab_ready")
        ct_ready = lsem("ct_ready")
        state_ready = lsem("state_ready")
        g_free = lsem("g_free")
        hid_ready = lsem("hid_ready")
        cmp_ready = lsem("cmp_ready")
        cexp_ready = lsem("cexp_ready")
        prob_ready = lsem("prob_ready")
        o_read = lsem("o_read")
        ys_pre = lsem("ys_pre")
        ys_ready = lsem("ys_ready")
        xmax_ready = lsem("xmax_ready")
        xprob_ready = lsem("xprob_ready")
        gu_done = lsem("gu_done")
        upper_done = lsem("upper_done")
        split_done = lsem("split_done")
        units_upper = lsem("units_upper")
        col_up = lsem("col_up")
        col_split = lsem("col_split")
        silu_done = lsem("silu_done")
        hid_done = lsem("hid_done")
        hT_tr = lsem("hT_tr")
        hT_done = lsem("hT_done")
        ffn_added = lsem("ffn_added")
        route = lsem("route")
        route_pe = lsem("route_pe")
        flag_ready = lsem("flag_ready")
        clear_range = range(min(s.num for s in per_layer), max(s.num for s in per_layer) + 1)
        assert len(clear_range) == len(per_layer)

        moe = []
        for i in range(2):
            moe.append({n: sem(f"moe{i}_{n}") for n in (
                "onehot", "gathered", "xe", "oh_t", "oh", "gu", "silu", "hid", "htr", "ht", "down", "y", "scat", "added", "used",
                "upper", "split", "ht_up", "xe_up")})
        flag_again = sem("flag_again")
        final_ready = sem("final_ready")
        p_dve, p_act, p_pool, p_pe = sem("p_dve"), sem("p_act"), sem("p_pool"), sem("p_pe")
        f_dve, f_act, f_pool = sem("f_dve"), sem("f_act"), sem("f_pool")
        fg_landed = sem("fg_landed")
        row_free = sem("row_free")
        landed2 = [sem(f"landed_again{i}") for i in range(RING)]

        def index(name):
            return NAMES.index(name)

        def bank(name):
            return banks[index(name) % ROT]

        def wait_free(eng, name):
            n = index(name) - ROT
            if n < 0:
                return
            old, by, _ = JOBS[n]
            eng.wait_ge(act_drained if by == "act" else dve_drained, DRAINS[by].index(old) + 1)

        def wait_tile(eng, l, name):
            c = JOBS[index(name)][2]
            if c is None:
                eng.wait_ge(mm_done, PLAIN.index(name) + 1)
            else:
                eng.wait_ge(weights_used, l * LAYER_CHUNKS + RING + c + 1)

        def wait_drained(eng, name):
            by = JOBS[index(name)][1]
            eng.wait_ge(act_drained if by == "act" else dve_drained, DRAINS[by].index(name) + 1)

        def kv_group(i):
            return (i % NH) // 3

        def f32(ap):
            return ap.bitcast(F32)

        def split_product(pe, to, x_up, x_lo, w_up, w_lo, start, stop):
            pe.matmul(to, x_up, w_up, start=start, stop=False, skip_group_check=True)
            pe.matmul(to, x_up, w_lo, start=False, stop=False, skip_group_check=True)
            return pe.matmul(to, x_lo, w_up, start=False, stop=stop, skip_group_check=True)

        def layer_chunk_upper(act, l, c):
            act.wait_ge(landed[c % RING], 16 * (LAYER_CHUNKS // RING * l + c // RING + 1))
            if c >= SPLIT_FIRST + 2:
                act.wait_ge(weights_used, l * LAYER_CHUNKS + RING + c - 1)
            act.activation(upper[:, c % 2, :], ring[:, c % RING, :], ACT.Copy).then_inc(wt_upper, 1)

        def layer_chunk_lower(dve, c):
            dve.wait_ge(wt_upper, c - SPLIT_FIRST + 1)
            dve.tensor_tensor(lower[:, c % RING, :], ring[:, c % RING, :], f32(upper[:, c % 2, :]), ALU.subtract).then_inc(wt_split, 1)

        hr = bigf[:, 0:1024].rearrange("p (b t n) -> p b t n", b=2, t=TT)
        gs = bigf[:, 2048:3072].rearrange("p (b t n) -> p b t n", b=2, t=TT)


        def upper_part(act, land, first, c, turns, used, base, done):
            q = first + c
            act.wait_ge(land[q % RING], 16 * (q // RING + 1 + turns))
            if base is not None:
                act.wait_ge(used, base)
            act.activation(upper[:, q % 3, :], ring[:, q % RING, :], ACT.Copy).then_inc(done, 1)

        def lower_part(dve, first, c, up, count, done):
            q = first + c
            dve.wait_ge(up, count)
            dve.tensor_tensor(lower[:, q % RING, :], ring[:, q % RING, :], f32(upper[:, q % 3, :]), ALU.subtract).then_inc(done, 1)

        def dense_pe(pe):
            f0 = COMMON

            def part(i, half, n):
                c = half if i == 0 and n is None else 3 * i - 1 + half
                q = f0 + c
                pe.wait_ge(split_done, c + 1 if n is None else 3 * n + half)
                up, lo = upper[:, q % 3, :], lower[:, q % RING, :]
                for t in range(TT):
                    if half == 0 and n is not None:
                        pe.wait_ge(hid_done, TT * (n - 1) + t + 1)
                    for k in range(4):
                        x = slice(t * P, (t + 1) * P)
                        kk = 4 * half + k
                        ins = split_product(pe, banks[t][:, :], colu[:, kk, x], coll[:, kk, x],
                                            up[:, k * 512:(k + 1) * 512], lo[:, k * 512:(k + 1) * 512],
                                            half == 0 and k == 0, half == 1 and k == 3)
                    if half == 1 and t == 0:
                        ins.then_inc(gu_done, 1)
                ins.then_inc(weights_used, 1)

            def turn(i, n):
                pe.wait_ge(hid_done, TT * n + TT)
                for f in range(2):
                    for t in range(TT):
                        c = f * T + t * P
                        ins = pe.transpose(banks[2][:, c:c + P], hr[:, i % 2, t, f * P:(f + 1) * P], ident)
                ins.then_inc(hT_tr, 1)

            def down(i, n, start=False, last=False):
                q = f0 + (3 * i + 2 if last else 3 * i + 4)
                pe.wait_ge(split_done, 3 * n + (3 if last else 5))
                pe.wait_ge(hT_done, n + 1)
                up, lo = upper[:, q % 3, :], lower[:, q % RING, :]
                for f in range(2):
                    for t in range(TT):
                        x = slice(f * T + t * P, f * T + (t + 1) * P)
                        for nn in range(2):
                            w = slice(f * 1024 + nn * 512, f * 1024 + (nn + 1) * 512)
                            ins = split_product(pe, banks[3 + 2 * t + nn][:, :], htu[:, i % 2, x], htl[:, i % 2, x],
                                                up[:, w], lo[:, w], start and f == 0, last and f == 1)
                ins.then_inc(weights_used, 1)

            def step(i, n, start=False):
                part(i + 1, 0, n + 1)
                turn(i, n)
                part(i + 1, 1, n + 1)
                down(i, n, start)

            pe.wait_ge(col_split, 4)
            part(0, 0, None)
            part(0, 1, None)
            step(0, 0, True)
            step(1, 1)
            with pe.Fori(1, (DENSE_PIECES - 1) // 2) as r:
                step(0, 2 * r)
                step(1, 2 * r + 1)
            n = DENSE_PIECES - 1
            turn(n, n)
            down(n, n, last=True)
            pe.wait_ge(weights_used, RING + LAYER_CHUNKS)

        lg = bigf[:, 3072:3088].rearrange("p (t e) -> p t e", t=TT)
        sel = bigf[:, 3088:3104].rearrange("p (t e) -> p t e", t=TT)
        comb = bigf[:, 3104:3120].rearrange("p (t e) -> p t e", t=TT)
        rank = bigf[:, 3120:3136].rearrange("p (t e) -> p t e", t=TT)
        oh1 = bigf[:, 3136:3152].rearrange("p (t e) -> p t e", t=TT)
        cnt = bigf[:, 3152:3160]
        idf = bigf[:, 3160:3168]
        wd = bigf[:, 3168:3176]
        router = cs("router")
        iota8 = cs("iota8")
        before = cs("before")
        ones = cs("ones")

        def route_on_pe(pe):
            for t in range(TT):
                for k in range(KD):
                    ins = pe.matmul(banks[7][:, t * 8:(t + 1) * 8], col[:, k, t * P:(t + 1) * P], router[:, k * 8:(k + 1) * 8],
                                    start=(k == 0), stop=(k == KD - 1))
            ins.then_inc(route_pe, 1)
            pe.wait_ge(route, 1)
            pe.matmul(banks[6][:, 0:8], before, sel[:, 0, :], start=True, stop=True)
            pe.matmul(banks[6][:, 8:16], before, sel[:, 1, :], start=True, stop=False)
            pe.matmul(banks[6][:, 8:16], ones, sel[:, 0, :], start=False, stop=True)
            pe.matmul(banks[6][:, 16:24], ones, sel[:, 0, :], start=True, stop=False)
            pe.matmul(banks[6][:, 16:24], ones, sel[:, 1, :], start=False, stop=True).then_inc(route_pe, 1)
            pe.wait_ge(route, 2)

        oh = xvf[:, 0:256].rearrange("p (t j) -> p t j", t=TT)
        ohT = xvf[:, 256:512]
        ye = xkf[:, 1024:2048]
        N = MOE_PIECES

        def moe_pe(pe, m, used, first):

            def operands(c, count):
                pe.wait_ge(m["split"], count)
                return upper[:, (first + c) % 3, :], lower[:, (first + c) % RING, :]

            def part(i, half, e, n=None):
                c = half if n is None else 3 * i - 1 + half
                up, lo = operands(c, MOE_CHUNKS * e + (c + 1 if n is None else 3 * n + half))
                if half == 0 and n is not None and not (isinstance(n, int) and n < 2):
                    pe.wait_ge(m["hid"], N * e + n - 1)
                for k in range(4):
                    w = slice(k * 512, (k + 1) * 512)
                    kk = 4 * half + k
                    ins = split_product(pe, banks[i % 2][:, :], xeu[:, kk, :], xel[:, kk, :], up[:, w], lo[:, w],
                                        half == 0 and k == 0, half == 1 and k == 3)
                ins.then_inc(used, 1)

            def turn(i, e, n):
                pe.wait_ge(m["hid"], N * e + n + 1)
                for f in range(2):
                    ins = pe.transpose(banks[2][:, f * P:(f + 1) * P], hr[:, i % 2, 0, f * P:(f + 1) * P], ident)
                ins.then_inc(m["htr"], 1)

            def down(i, e, n, start=False, last=False):
                up, lo = operands(3 * i + 2 if last else 3 * i + 4, MOE_CHUNKS * e + 3 * n + (3 if last else 5))
                pe.wait_ge(m["ht"], N * e + n + 1)
                for f in range(2):
                    x = slice(f * P, (f + 1) * P)
                    for nn in range(2):
                        w = slice(f * 1024 + nn * 512, f * 1024 + (nn + 1) * 512)
                        ins = split_product(pe, banks[3 + nn][:, :], htu[:, i % 2, x], htl[:, i % 2, x], up[:, w], lo[:, w],
                                            start and f == 0, last and f == 1)
                ins.then_inc(used, 1)

            def gather(e):
                pe.wait_ge(m["onehot"], e + 1)
                for k in range(KD):
                    for t in range(TT):
                        ins = pe.matmul(banks[5 + k // 4][:, (k % 4) * P:(k % 4 + 1) * P], row[:, t, k * P:(k + 1) * P], oh[:, t, :],
                                        start=(t == 0), stop=(t == TT - 1))
                ins.then_inc(m["gathered"], 1)

            def turn_onehot(e):
                pe.wait_ge(m["added"], 4 * e + 1)
                for t in range(TT):
                    ins = pe.transpose(banks[7][:, t * P:(t + 1) * P], oh[:, t, :], ident)
                ins.then_inc(m["oh_t"], 1)

            def scatter(e):
                pe.wait_ge(m["y"], e + 1)
                pe.wait_ge(m["oh"], e + 1)
                for t in range(TT):
                    for nn in range(2):
                        q = 2 * t + nn
                        pe.matmul(banks[(5, 6, 7, 2)[q]][:, :], ohT[:, t * P:(t + 1) * P], ye[:, nn * 512:(nn + 1) * 512],
                                  start=True, stop=True).then_inc(m["scat"], 1)

            def step(i, e, n, start=False):
                part(i + 1, 0, e, n + 1)
                turn(i, e, n)
                part(i + 1, 1, e, n + 1)
                down(i, e, n, start)

            def pieces(e, boundary):
                part(1, 0, e, 1)
                turn_onehot(e)
                turn(0, e, 0)
                part(1, 1, e, 1)
                down(0, e, 0, start=True)
                step(1, e, 1)
                with pe.Fori(1, N // 2 - 1) as r:
                    step(0, e, 2 * r)
                    step(1, e, 2 * r + 1)
                step(N - 2, e, N - 2)
                turn(N - 1, e, N - 1)
                if boundary:
                    gather(e + 1)
                down(N - 1, e, N - 1, last=True)

            gather(0)
            pe.wait_ge(m["xe"], 1)
            part(0, 0, 0)
            part(0, 1, 0)
            with pe.Fori(0, NE - 1) as e:
                pieces(e, True)
                pe.wait_ge(m["xe"], e + 2)
                part(0, 0, e + 1)
                part(0, 1, e + 1)
                scatter(e)
            pieces(NE - 1, False)
            scatter(NE - 1)
            pe.wait_ge(m["added"], 4 * NE + 1)

        def dense_act(act, features):

            def up(c, r=0):
                first = c < 3 and isinstance(r, int)
                upper_part(act, landed, COMMON, c, r, weights_used, RING + COMMON if first else RING + COMMON + c - 2 + 6 * r,
                           upper_done)

            def silu(i, n):
                for t in range(TT):
                    if t == 0:
                        act.wait_ge(gu_done, n + 1)
                    else:
                        act.wait_ge(weights_used, RING + COMMON + (2 if isinstance(n, int) and n == 0 else 3 * n + 1))
                    if not (isinstance(n, int) and n == 0):
                        act.wait_ge(hid_done, TT * (n - 1) + t + 1)
                    act.activation(gs[:, i % 2, t, :], banks[t][:, 0:256], ACT.Silu).then_inc(silu_done, 1)

            def copy_units(i, n):
                act.wait_ge(hT_tr, n + 1)
                if not (isinstance(n, int) and n < 2):
                    act.wait_ge(weights_used, RING + COMMON + 3 * n - 1)
                act.activation(htu[:, i % 2, :], banks[2][:, :], ACT.Copy).then_inc(units_upper, 1)

            def step(i, n, r=0, chunks=3):
                copy_units(i, n)
                up(3 * i + 5, r)
                silu(i + 1, n + 1)
                for c in range(1, chunks):
                    up(3 * i + 5 + c, r)

            up(0)
            up(1)
            features()
            up(2)
            silu(0, 0)
            up(3)
            up(4)
            step(0, 0)
            step(1, 1)
            with act.Fori(1, (DENSE_PIECES - 1) // 2 - 1) as r:
                step(0, 2 * r, r)
                step(1, 2 * r + 1, r)
            step(DENSE_PIECES - 3, DENSE_PIECES - 3)
            step(DENSE_PIECES - 2, DENSE_PIECES - 2, chunks=1)
            copy_units(DENSE_PIECES - 1, DENSE_PIECES - 1)

        def moe_act(act, m, used, base, land, first, features):

            def up(c, e, r=0):
                free = base + MOE_CHUNKS * e + c - 2 + 6 * r
                upper_part(act, land, first, c, e * (MOE_CHUNKS // RING) + r, used,
                           base if isinstance(e, int) and isinstance(r, int) and e == 0 and c < 3 else free, m["upper"])

            def silu(i, e, n):
                act.wait_ge(used, base + e * MOE_CHUNKS + (2 if isinstance(n, int) and n == 0 else 3 * n + 1))
                if not (isinstance(n, int) and n < 2):
                    act.wait_ge(m["hid"], N * e + n - 1)
                act.activation(gs[:, i % 2, 0, :], banks[i % 2][:, 0:256], ACT.Silu).then_inc(m["silu"], 1)

            def copy_units(i, e, n):
                act.wait_ge(m["htr"], N * e + n + 1)
                if not (isinstance(n, int) and n < 2):
                    act.wait_ge(used, base + e * MOE_CHUNKS + 3 * n - 1)
                act.activation(htu[:, i % 2, 0:256], banks[2][:, 0:256], ACT.Copy).then_inc(m["ht_up"], 1)

            def copy_onehot(e):
                act.wait_ge(m["oh_t"], e + 1)
                act.activation(ohT, banks[7][:, 0:256], ACT.Copy).then_inc(m["oh"], 1)

            def gathered(e):
                act.wait_ge(m["gathered"], e + 1)
                for k in range(KD):
                    act.activation(xeu[:, k, :], banks[5 + k // 4][:, (k % 4) * P:(k % 4 + 1) * P], ACT.Copy,
                                   scale=cols[:, C_FFN + k:C_FFN + k + 1]).then_inc(m["xe_up"], 1)

            def step(i, e, n, r=0):
                copy_units(i, e, n)
                up(3 * i + 5, e, r)
                silu(i + 1, e, n + 1)
                up(3 * i + 6, e, r)
                up(3 * i + 7, e, r)

            def pieces(e, more):
                copy_units(0, e, 0)
                copy_onehot(e)
                up(5, e)
                silu(1, e, 1)
                up(6, e)
                up(7, e)
                step(1, e, 1)
                with act.Fori(1, N // 2 - 1) as r:
                    step(0, e, 2 * r, r)
                    step(1, e, 2 * r + 1, r)
                copy_units(0, e, N - 2)
                up(3 * N - 1, e)
                silu(1, e, N - 1)
                if more:
                    up(0, e + 1)
                copy_units(1, e, N - 1)
                if more:
                    up(1, e + 1)
                    gathered(e + 1)
                act.wait_ge(used, base + e * MOE_CHUNKS + MOE_CHUNKS)
                for nn in range(2):
                    ins = act.activation(ye[:, nn * 512:(nn + 1) * 512], banks[3 + nn][:, :], ACT.Copy)
                ins.then_inc(m["y"], 1)
                if more:
                    up(2, e + 1)

            up(0, 0)
            up(1, 0)
            features()
            up(2, 0)
            gathered(0)
            silu(0, 0, 0)
            up(3, 0)
            up(4, 0)
            with act.Fori(0, NE - 1) as e:
                pieces(e, True)
                silu(0, e + 1, 0)
                up(3, e + 1)
                up(4, e + 1)
            pieces(NE - 1, False)

        def dense_dve(dve):
            def low(c, n=0):
                lower_part(dve, COMMON, c, upper_done, c + 1 + n, split_done)

            def product(i, n):
                for t in range(TT):
                    dve.wait_ge(silu_done, TT * n + t + 1)
                    if t == 0 and not (isinstance(n, int) and n < 2):
                        dve.wait_ge(hT_tr, n - 1)
                    dve.tensor_tensor(hr[:, i % 2, t, :], gs[:, i % 2, t, :], banks[t][:, 256:512], ALU.mult).then_inc(hid_done, 1)

            def units(i, n):
                dve.wait_ge(units_upper, n + 1)
                dve.tensor_tensor(htl[:, i % 2, :], banks[2][:, :], f32(htu[:, i % 2, :]), ALU.subtract).then_inc(hT_done, 1)

            def step(i, n, r=0, chunks=3):
                units(i, n)
                low(3 * i + 5, 6 * r)
                product(i + 1, n + 1)
                for c in range(1, chunks):
                    low(3 * i + 5 + c, 6 * r)

            low(0)
            low(1)
            for k in range(4):
                x, u, w = (y[:, 2 * k:2 * k + 2, :] for y in (col, colu, coll))
                dve.wait_ge(act_drained, len(DRAINS["act"]) - 3 + k)
                dve.tensor_copy(u, x).then_inc(col_up, 1)
                dve.wait_ge(col_up, k + 1)
                dve.tensor_tensor(w, x, f32(u), ALU.subtract).then_inc(col_split, 1)
            low(2)
            product(0, 0)
            low(3)
            low(4)
            step(0, 0)
            step(1, 1)
            with dve.Fori(1, (DENSE_PIECES - 1) // 2 - 1) as r:
                step(0, 2 * r, r)
                step(1, 2 * r + 1, r)
            step(DENSE_PIECES - 3, DENSE_PIECES - 3)
            step(DENSE_PIECES - 2, DENSE_PIECES - 2, chunks=1)
            units(DENSE_PIECES - 1, DENSE_PIECES - 1)
            dve.wait_ge(weights_used, RING + LAYER_CHUNKS)
            for t in range(TT):
                for n in range(2):
                    hs = h[:, t, n * 512:(n + 1) * 512]
                    dve.tensor_tensor(hs, hs, banks[3 + 2 * t + n][:, :], ALU.add).then_inc(ffn_added, 1)

        def route_on_dve(dve):
            n = [0]

            def link(ins):
                n[0] += 1
                ins.then_inc(ar1, 1)
                dve.wait_ge(ar1, n[0])

            dve.wait_ge(route_pe, 1)
            link(dve.tensor_copy(lg, banks[7][:, 0:16].rearrange("p (t e) -> p t e", t=TT)))
            for t in range(TT):
                for choice in (oh1, sel):
                    link(dve.max(eight[:, 0:8], lg[:, t, :]))
                    link(dve.max_index(idx[:, :], eight[:, 0:8], lg[:, t, :]))
                    if choice is oh1:
                        dve.tensor_copy(wd[:, 4 + t:5 + t], eight[:, 0:1])
                    else:
                        dve.tensor_tensor(wd[:, t:t + 1], eight[:, 0:1], wd[:, 4 + t:5 + t], ALU.subtract)
                    link(dve.tensor_copy(idf, idx[:, :]))
                    link(dve.tensor_scalar(choice[:, t, :], iota8, idf[:, 0:1], None, ALU.is_equal))
                    if choice is oh1:
                        link(dve.scalar_tensor_tensor(lg[:, t, :], oh1[:, t, :], NEG, lg[:, t, :], ALU.mult, ALU.add))
            link(dve.tensor_copy(comb, sel))
            link(dve.tensor_tensor(sel, sel, oh1, ALU.add))
            dve.tensor_copy(eight[:, 8:9], eight[:, 0:1]).then_inc(route, 1)
            dve.wait_ge(route_pe, 2)
            dve.tensor_copy(rank, banks[6][:, 0:16].rearrange("p (t e) -> p t e", t=TT))
            link(dve.tensor_copy(cnt, banks[6][:, 16:24]))
            dve.tensor_copy(eight[:, 9:10], cnt[:, 0:1]).then_inc(route, 1)
            link(dve.tensor_reduce(eight[:, 10:11], cnt, AX.X, ALU.max))
            dve.tensor_scalar(flag[0:1, 0:1], eight[0:1, 10:11], float(P) + 0.5, None, ALU.is_gt).then_inc(flag_ready, 1)
            dve.wait_ge(flag_ready, 1)
            dve.tensor_copy(eight[:, 11:12], eight[:, 10:11]).then_inc(route, 1)
            dve.wait_ge(route, 4)
            link(dve.tensor_scalar(wd[:, 2:4], wd[:, 0:2], 1.0, None, ALU.add))
            link(dve.reciprocal(wd[:, 2:4], wd[:, 2:4]))
            link(dve.tensor_tensor(wd[:, 0:2], wd[:, 0:2], wd[:, 2:4], ALU.mult))
            for t in range(TT):
                link(dve.tensor_scalar(comb[:, t, :], comb[:, t, :], wd[:, t:t + 1], None, ALU.mult))
                link(dve.scalar_tensor_tensor(comb[:, t, :], oh1[:, t, :], wd[:, 2 + t:3 + t], comb[:, t, :], ALU.mult, ALU.add))

        def moe_dve(dve, m, tile, first, routing):
            places = cs("iota")[:, tile * P:(tile + 1) * P]

            def onehot(e):
                for t in range(TT):
                    ins = dve.tensor_scalar(oh[:, t, :], places, rank[:, t, bass.ds(e, 1)], sel[:, t, bass.ds(e, 1)],
                                            ALU.is_equal, ALU.mult)
                ins.then_inc(m["onehot"], 1)

            def gathered(e):
                for k in range(KD):
                    if k % 4 == 0:
                        dve.wait_ge(m["xe_up"], KD * e + k + 4)
                    ins = dve.scalar_tensor_tensor(xel[:, k, :], banks[5 + k // 4][:, (k % 4) * P:(k % 4 + 1) * P],
                                                   cols[:, C_FFN + k:C_FFN + k + 1], f32(xeu[:, k, :]), ALU.mult, ALU.subtract)
                ins.then_inc(m["xe"], 1)

            def low(c, e, n=0):
                lower_part(dve, first, c, m["upper"], MOE_CHUNKS * e + c + 1 + n, m["split"])

            def product(i, e, n):
                dve.wait_ge(m["silu"], N * e + n + 1)
                if not (isinstance(n, int) and n < 2):
                    dve.wait_ge(m["htr"], N * e + n - 1)
                dve.tensor_tensor(hr[:, i % 2, 0, :], gs[:, i % 2, 0, :], banks[i % 2][:, 256:512], ALU.mult).then_inc(m["hid"], 1)

            def units(i, e, n):
                dve.wait_ge(m["ht_up"], N * e + n + 1)
                dve.tensor_tensor(htl[:, i % 2, 0:256], banks[2][:, 0:256], f32(htu[:, i % 2, 0:256]),
                                  ALU.subtract).then_inc(m["ht"], 1)

            def step(i, e, n, r=0):
                units(i, e, n)
                low(3 * i + 5, e, 6 * r)
                product(i + 1, e, n + 1)
                low(3 * i + 6, e, 6 * r)
                low(3 * i + 7, e, 6 * r)

            def next_onehot(e):
                dve.wait_ge(m["oh_t"], e + 1)
                onehot(e + 1)

            def pieces(e, more):
                step(0, e, 0)
                if more:
                    next_onehot(e)
                step(1, e, 1)
                with dve.Fori(1, N // 2 - 1) as r:
                    step(0, e, 2 * r, r)
                    step(1, e, 2 * r + 1, r)
                units(0, e, N - 2)
                low(3 * N - 1, e)
                product(1, e, N - 1)
                if more:
                    low(0, e + 1)
                units(1, e, N - 1)
                if more:
                    low(1, e + 1)
                    gathered(e + 1)
                    low(2, e + 1)

            def add(e):
                for t in range(TT):
                    for nn in range(2):
                        q = 2 * t + nn
                        dve.wait_ge(m["scat"], 4 * e + q + 1)
                        hs = h[:, t, nn * 512:(nn + 1) * 512]
                        dve.scalar_tensor_tensor(hs, banks[(5, 6, 7, 2)[q]][:, :], comb[:, t, bass.ds(e, 1)], hs,
                                                 ALU.mult, ALU.add).then_inc(m["added"], 1)

            dve.sem_inc(m["added"], 1)
            low(0, 0)
            low(1, 0)
            routing()
            onehot(0)
            low(2, 0)
            gathered(0)
            product(0, 0, 0)
            low(3, 0)
            low(4, 0)
            with dve.Fori(0, NE - 1) as e:
                pieces(e, True)
                product(0, e + 1, 0)
                low(3, e + 1)
                add(e)
                low(4, e + 1)
            pieces(NE - 1, False)
            add(NE - 1)
            dve.wait_ge(m["added"], 4 * NE + 1)

        block = ctx.enter_context(nc.Block())

        @block.sync
        def _(sp):
            sp.dma_start(row[:, :, :], mem.rearrange("(t p) n -> p t n", p=P)).then_inc(mem_landed, 16)
            sp.dma_start(cst[:, :], consts).then_inc(cst_landed, 16)
            sp.dma_start(bigf[0:33, 0:512], onehot).then_inc(bias_landed, 16)
            sp.dma_start(bigf[0:33, 512:518], relb).then_inc(bias_landed, 16)
            sp.dma_start(h[:, :, :], x.rearrange("(t p) n -> p t n", p=P)).then_inc(x_landed, 16)
            ncols = LP["cols"][1]
            sp.dma_start(lp[:, 0:ncols], lparams[0][:, 0:ncols]).then_inc(cols_landed, 16)

            def stream(first, count, used, land):
                rounds, rest = divmod(count, RING)
                for s in range(RING):
                    sp.wait_ge(used, s + 1)
                    sp.dma_start(ring[:, s, :], weights[first + s]).then_inc(land[s], 16)
                if land is landed:
                    sp.dma_start(lp[:, ncols:], lparams[0][:, ncols:]).then_inc(lp_landed, 16)
                    sp.wait_ge(p_dve, 4 + NH)
                    sp.dma_start(scratch[:, :, :].rearrange("h p n -> p h n"),
                                 bigf[:, 1408:1408 + NH * 384].rearrange("p (h n) -> p h n", h=NH)).then_inc(s_scr, 16)
                    sp.wait_ge(s_scr, 16)
                    skew = bass.AP(scratch.tensor, 127, [[383, P], [P * 384, NH], [1, T]])
                    sp.dma_start(btab[:, :, :], skew).then_inc(s_scr, 16)
                with sp.Fori(1, rounds) as r:
                    for s in range(RING):
                        sp.wait_ge(used, r * RING + (s + 1))
                        sp.dma_start(ring[:, s, :], weights[first + r * RING + s]).then_inc(land[s], 16)
                for s in range(rest):
                    sp.wait_ge(used, rounds * RING + s + 1)
                    sp.dma_start(ring[:, s, :], weights[first + rounds * RING + s]).then_inc(land[s], 16)

            stream(0, CHUNKS, weights_used, landed)
            sp.wait_ge(flag_again, 1)
            v = sp.value_load(flag[0:1, 0:1], min_val=0, max_val=1)
            with sp.If(v == 1):
                stream(MOE_FIRST, NE * MOE_CHUNKS, moe[1]["used"], landed2)
            with sp.Else():
                sp.nop()
            sp.wait_ge(final_ready, 2)
            sp.dma_start(out.rearrange("(t p) n -> p t n", p=P), row[:, :, :]).then_inc(s_out, 16)
            sp.wait_ge(s_out, 16)
        @block.tensor
        def _(pe):
            mm = pe.matmul

            def finish(name, ins):
                ins.then_inc(mm_done if JOBS[index(name)][2] is None else weights_used, 1)

            def chunk(l, c):
                pe.wait_ge(landed[c % RING], 16 * (LAYER_CHUNKS // RING * l + c // RING + 1))
                return ring[:, c % RING, :]

            def transpose_rows(stage):
                for i in range(4):
                    wait_free(pe, f"{stage}T{i}")
                    b = bank(f"{stage}T{i}")
                    for k in range(2):
                        for t in range(TT):
                            f = (2 * i + k) * P
                            ins = pe.transpose(b[:, (k * TT + t) * P:(k * TT + t + 1) * P], row[:, t, f:f + P], ident)
                    finish(f"{stage}T{i}", ins)

            def features_out(name, l, c, width=2, at=0):
                w = chunk(l, c)
                wait_free(pe, name)
                b = bank(name)
                for m in range(width):
                    for k in range(KD):
                        ins = mm(b[:, m * T:(m + 1) * T], w[:, k * 256 + m * P:k * 256 + (m + 1) * P], col[:, k, :],
                                 start=(k == 0), stop=(k == KD - 1))
                finish(name, ins)

            def tokens_out(stage, l, c0, src):
                for part in range(2):
                    w = chunk(l, c0 + part)
                    for t in range(TT):
                        name = f"{stage}_{t}"
                        if part == 0:
                            wait_free(pe, name)
                        for k in range(4):
                            ins = mm(bank(name)[:, :], src[:, 4 * part + k, t * P:(t + 1) * P], w[:, k * 512:(k + 1) * 512],
                                     start=(part == 0 and k == 0), stop=(part == 1 and k == 3))
                        if part == 1:
                            finish(name, ins)
                        elif t == TT - 1:
                            ins.then_inc(weights_used, 1)

            def split_chunk(c):
                pe.wait_ge(wt_split, c - SPLIT_FIRST + 1)
                return upper[:, c % 2, :], lower[:, c % RING, :]

            def split_features_out(name, c):
                up, lo = split_chunk(c)
                wait_free(pe, name)
                for m in range(2):
                    for k in range(KD):
                        w = slice(k * 256 + m * P, k * 256 + (m + 1) * P)
                        ins = split_product(pe, bank(name)[:, m * T:(m + 1) * T], up[:, w], lo[:, w],
                                            colr[:, k, :], xor[:, k, :], k == 0, k == KD - 1)
                finish(name, ins)

            def split_tokens_out(stage, c0, x_up, x_lo):
                for part in range(2):
                    up, lo = split_chunk(c0 + part)
                    for t in range(TT):
                        name = f"{stage}_{t}"
                        if part == 0:
                            wait_free(pe, name)
                        for k in range(4):
                            x, w, kk = slice(t * P, (t + 1) * P), slice(k * 512, (k + 1) * 512), 4 * part + k
                            ins = split_product(pe, bank(name)[:, :], x_up[:, kk, x], x_lo[:, kk, x], up[:, w], lo[:, w],
                                                part == 0 and k == 0, part == 1 and k == 3)
                        if part == 1:
                            finish(name, ins)
                        elif t == TT - 1:
                            ins.then_inc(weights_used, 1)

            pe.sem_inc(weights_used, RING)
            pe.sem_inc(moe[1]["used"], RING)
            pe.wait_ge(cst_landed, 16)
            pe.wait_ge(p_act, 2)
            for i in range(4):
                for k in range(2):
                    for t in range(TT):
                        f = (2 * i + k) * P
                        ins = pe.transpose(banks[i][:, (k * TT + t) * P:(k * TT + t + 1) * P], row[:, t, f:f + P], ident)
                ins.then_inc(p_pe, 1)
            pe.wait_ge(p_dve, 4)
            for hh in range(NH):
                b = banks[4 + hh % 4]
                if hh >= 4:
                    pe.wait_ge(p_dve, 4 + hh - 3)
                mm(b[:, 0:384], bigf[0:33, 640 + hh * P:640 + (hh + 1) * P], bigf[0:33, 0:384],
                   start=True, stop=True).then_inc(p_pe, 1)
            pe.wait_ge(p_act, 6)
            pe.wait_ge(p_dve, 4 + NH)

            with pe.Fori(0, L) as l:
                pe.wait_ge(row_ready, 2)
                transpose_rows("h")
                wait_drained(pe, "hT3")
                features_out("u", l, 0)
                w = chunk(l, 1)
                wait_free(pe, "zA")
                for t in range(TT):
                    for k in range(KD):
                        ins = mm(bank("zA")[:, t * 256:(t + 1) * 256], col[:, k, t * P:(t + 1) * P], w[:, k * 256:(k + 1) * 256],
                                 start=(k == 0), stop=(k == KD - 1))
                finish("zA", ins)
                w = chunk(l, 2)
                wait_free(pe, "zB")
                for t in range(TT):
                    for k in range(KD):
                        mm(bank("zB")[:, t * 114:(t + 1) * 114], col[:, k, t * P:(t + 1) * P], w[:, k * 256:k * 256 + 114],
                           start=(k == 0), stop=(k == KD - 1))
                for k in range(KD):
                    ins = mm(bank("zB")[:, 228:484], w[:, k * 256 + 114:k * 256 + 242], col[:, k, :],
                             start=(k == 0), stop=(k == KD - 1))
                finish("zB", ins)
                features_out("q0", l, 3)
                features_out("q1", l, 4)
                w = chunk(l, 5)
                for v, name in enumerate(("ck", "cv")):
                    wait_free(pe, name)
                    for k in range(KD):
                        ins = mm(bank(name)[:, 0:T], w[:, k * 256 + v * P:k * 256 + (v + 1) * P], col[:, k, :],
                                 start=(k == 0), stop=(k == KD - 1))
                    finish(name, ins)
                w = chunk(l, 6)
                wait_free(pe, "vs")
                for t in range(TT):
                    for k in range(KD):
                        ins = mm(bank("vs")[:, t * 256:(t + 1) * 256], col[:, k, t * P:(t + 1) * P], w[:, k * 256:(k + 1) * 256],
                                 start=(k == 0), stop=(k == KD - 1))
                finish("vs", ins)

                pe.wait_ge(z_ready, 1)
                wait_free(pe, "cqT")
                b = bank("cqT")
                for t in range(TT):
                    pe.transpose(b[:, t * P:(t + 1) * P], z[:, t, 0:128], ident)
                    ins = pe.transpose(b[0:64, T + t * P:T + (t + 1) * P], z[:, t, 128:192], ident)
                finish("cqT", ins)
                pe.wait_ge(rope_ready, 1)
                wait_free(pe, "ckvT")
                b = bank("ckvT")
                for t in range(TT):
                    pe.transpose(b[:, t * P:(t + 1) * P], z[:, t, 192:320], ident)
                    ins = pe.transpose(b[0:96, T + t * P:T + (t + 1) * P], krp[:, t, :], ident)
                finish("ckvT", ins)
                wait_drained(pe, "ck")
                wait_drained(pe, "cv")
                pe.wait_ge(lp_landed, 16)
                wait_free(pe, "hid")
                b = bank("hid")
                for v in range(2):
                    for m in range(NPAIR):
                        ins = mm(b[0:HD, v * 45:(v + 1) * 45], w1[:, v, m, :], kc[:, v, :, 2 * m:2 * m + 225:CSTRIDE],
                                 start=(m == 0), stop=(m == NPAIR - 1))
                finish("hid", ins)
                wait_drained(pe, "cqT")
                for t in range(TT):
                    for name, a, n in ((f"qn{t}", 0, 384), (f"qr{t}", 384, 192)):
                        wait_free(pe, name)
                        for k in range(2):
                            ins = mm(bank(name)[:, 0:n], ql[:, k, t * P:(t + 1) * P], uq[:, k, a:a + n],
                                     start=(k == 0), stop=(k == 1))
                        finish(name, ins)
                wait_drained(pe, "ckvT")
                for i in range(3):
                    wait_free(pe, f"kn{i}")
                    for hh in range(2):
                        c = (2 * i + hh) * 64
                        ins = mm(bank(f"kn{i}")[0:HD, hh * T:(hh + 1) * T], ukv[:, c:c + 64], ckvT[:, :], start=True, stop=True)
                    finish(f"kn{i}", ins)
                for t in range(TT):
                    wait_free(pe, f"vm{t}")
                    ins = mm(bank(f"vm{t}")[:, 0:384], ckvT[:, t * P:(t + 1) * P], ukv[:, 384:768], start=True, stop=True)
                    finish(f"vm{t}", ins)
                pe.wait_ge(hid_ready, 1)
                wait_free(pe, "kcv")
                b = bank("kcv")
                mm(b[0:64, 0:16], w2[0:HD, 0, :], hid[:, 0, 0:16], start=True, stop=True)
                mm(b[64:128, 0:16], w2[0:HD, 0, :], hid[:, 0, 16:32], start=True, stop=True)
                ins = mm(b[0:96, 16:80], hidr[:, :], w2[0:HD, 1, :], start=True, stop=True)
                finish("kcv", ins)
                wait_drained(pe, "qn1")
                wait_drained(pe, "qr1")
                for i in range(3):
                    wait_free(pe, f"qT{i}")
                    for hh in range(2):
                        for t in range(TT):
                            c = (hh * TT + t) * P
                            ins = pe.transpose(bank(f"qT{i}")[0:QK, c:c + P], qrow[:, t, 2 * i + hh, :], ident)
                    finish(f"qT{i}", ins)
                wait_drained(pe, "kcv")
                wait_free(pe, "sc")
                for t in range(TT):
                    for hh in range(NH):
                        c = (t * NH + hh) * 16
                        ins = mm(bank("sc")[:, c:c + 16], qz[:, hh, t * P:(t + 1) * P], kcT[:, :], start=True, stop=True)
                finish("sc", ins)
                pe.wait_ge(cexp_ready, 1)
                wait_free(pe, "pcT")
                for t in range(TT):
                    ins = pe.transpose(bank("pcT")[0:96, t * P:(t + 1) * P], pc[:, t, :, :].rearrange("p h n -> p (h n)"), ident)
                finish("pcT", ins)
                wait_drained(pe, "pcT")
                for t in range(TT):
                    wait_free(pe, f"oc{t}")
                    ins = mm(bank(f"oc{t}")[:, 0:384], pcs[:, t * P:(t + 1) * P], vbd[:, :], start=True, stop=True)
                    finish(f"oc{t}", ins)

                def scores(i):
                    name = f"s{i}"
                    if i == 0:
                        wait_drained(pe, "qT2")
                        wait_drained(pe, "kn2")
                    if i < NH:
                        q, k = qT[:, i, :], kT[:, i, :]
                    else:
                        q, k = qz[:, i % NH, :], (kslT if i < 2 * NH else kwnT)[:, :]
                    wait_free(pe, name)
                    mm(bank(name)[:, 0:128], q[:, 0:128], k[:, 0:128], start=True, stop=True)
                    finish(name, mm(bank(name)[:, 128:384], q[:, 128:256], k, start=True, stop=True))

                def outputs(i):
                    hh, gi = i % NH, kv_group(i)
                    wait_drained(pe, f"pT{i}")
                    if hh == 0 and i > 0:
                        pe.wait_ge(o_read, TT * (i // NH))
                    if i < NH:
                        v = [vm[:, t, hh * 64:(hh + 1) * 64] for t in range(TT)]
                    else:
                        a = (i // NH - 1) * 128 + gi * 64
                        v = [vs[:, t, a:a + 64] for t in range(TT)]
                    p = pt[:, i % 2, :]
                    mm(ob[0][:, hh * 64:(hh + 1) * 64], p[:, 0:128], v[0], start=True, stop=True)
                    mm(ob[1][:, hh * 64:(hh + 1) * 64], p[:, 128:256], v[0], start=True, stop=False)
                    mm(ob[1][:, hh * 64:(hh + 1) * 64], p[:, 256:384], v[1], start=False, stop=True).then_inc(pe_note, 1)

                def state_inputs(j):
                    name = f"bu{j}"
                    wait_free(pe, name)
                    for c in range(2):
                        ins = mm(bank(name)[:, c * T:(c + 1) * T], bt[:, j, c, :], uT[:, j // 4, :], start=True, stop=True)
                    finish(name, ins)

                def state_outputs(j):
                    pe.wait_ge(state_ready, j + 1)
                    y = yb[32 * (j % 4):32 * (j % 4) + 32, (j // 4) * T:(j // 4 + 1) * T]
                    mm(y, cp[:, 0, j, :], g[:, j % 2, 0, :], start=True, stop=False)
                    mm(y, cp[:, 1, j, :], g[:, j % 2, 1, :], start=False, stop=True).then_inc(g_free, 1)

                for i in range(LEAD):
                    scores(i)
                pe.wait_ge(ct_ready, 1)
                pe.wait_ge(memT_ready, KD)
                for i in range(HEADS):
                    if i + LEAD < HEADS:
                        scores(i + LEAD)
                    if i in MEMK:
                        features_out(f"mk{MEMK[i]}", l, 7 + MEMK[i])
                    if i in STATES:
                        state_inputs(STATES[i])
                    pe.wait_ge(prob_ready, i + 1)
                    wait_free(pe, f"pT{i}")
                    for c in range(3):
                        ins = pe.transpose(bank(f"pT{i}")[:, c * P:(c + 1) * P], prob[:, i % 4, c * P:(c + 1) * P], ident)
                    finish(f"pT{i}", ins)
                    if i > 0:
                        outputs(i - 1)
                    if i in STATES and STATES[i] > 0:
                        state_outputs(STATES[i] - 1)
                outputs(HEADS - 1)
                state_outputs(7)

                tokens_out("mv0", l, 11, memT)
                pe.wait_ge(ys_ready, 1)
                wait_free(pe, "yr")
                for t in range(TT):
                    for k in range(2):
                        ins = pe.transpose(bank("yr")[:, t * T + k * P:t * T + (k + 1) * P], uT[:, k, t * P:(t + 1) * P], ident)
                finish("yr", ins)
                wait_free(pe, "gl")
                for t in range(TT):
                    for k in range(2):
                        ins = mm(bank("gl")[:, t * T:(t + 1) * T], uT[:, k, t * P:(t + 1) * P], glu[:, k, :],
                                 start=(k == 0), stop=(k == 1))
                finish("gl", ins)
                tokens_out("mv1", l, 13, memT)
                pe.wait_ge(row_ready, 4)
                transpose_rows("y")
                wait_drained(pe, "yT3")
                split_tokens_out("wo0", 15, colr, xor)
                split_tokens_out("wo1", 17, colr, xor)

                pe.wait_ge(row_ready, 6)
                transpose_rows("x")
                wait_drained(pe, "xT3")
                for i in range(XH):
                    split_features_out(f"xq{i}", 19 + i)
                for i in range(XH):
                    wait_drained(pe, f"xq{i}")
                    wait_free(pe, f"xs{i}")
                    for t in range(TT):
                        for m in range(2):
                            ins = mm(bank(f"xs{i}")[:, t * T:(t + 1) * T], xq[:, 2 * i + m, t * P:(t + 1) * P], xk[:, 2 * i + m, :],
                                     start=(m == 0), stop=(m == 1))
                    finish(f"xs{i}", ins)
                def turn_probabilities(i):
                    pe.wait_ge(xprob_ready, i + 1)
                    wait_free(pe, f"xp{i}")
                    for kt in range(2):
                        for t in range(TT):
                            c = kt * T + t * P
                            ins = pe.transpose(bank(f"xp{i}")[:, c:c + P], xprob[:, i % 3, t * T + kt * P:t * T + (kt + 1) * P], ident)
                    finish(f"xp{i}", ins)

                turn_probabilities(0)
                for i in range(XH):
                    if i + 1 < XH:
                        turn_probabilities(i + 1)
                    wait_drained(pe, f"xp{i}")
                    wait_free(pe, f"xo{i}")
                    for m in range(2):
                        for kt in range(2):
                            a = i * 256 + m * P
                            ins = mm(bank(f"xo{i}")[:, m * T:(m + 1) * T], xv[:, kt, a:a + P], pt[:, i % 2, kt * T:(kt + 1) * T],
                                     start=(kt == 0), stop=(kt == 1))
                    finish(f"xo{i}", ins)
                wait_drained(pe, "xo3")
                split_tokens_out("xw0", 23, xor, colr)
                split_tokens_out("xw1", 25, xor, colr)

                pe.wait_ge(row_ready, 8)
                transpose_rows("f")
                pe.wait_ge(act_drained, len(DRAINS["act"]))
                pe.wait_ge(dve_drained, len(DRAINS["dve"]))
                with pe.If(l == 0):
                    dense_pe(pe)
                with pe.Else():
                    route_on_pe(pe)
                    moe_pe(pe, moe[0], weights_used, MOE_FIRST)
                pe.drain().then_inc(arrived, 1)
                pe.wait_ge(go, l + 1)

            pe.wait_ge(flag_again, 1)
            v = pe.value_load(flag[0:1, 0:1], min_val=0, max_val=1)
            with pe.If(v == 1):
                moe_pe(pe, moe[1], moe[1]["used"], 0)
            with pe.Else():
                pe.nop()

        @block.scalar
        def _(act):
            A = act.activation
            seq = [0]

            def link(ins):
                seq[0] += 1
                ins.then_inc(act_seq, 1)
                act.wait_ge(act_seq, seq[0])

            def drained(ins):
                ins.then_inc(act_drained, 1)

            def scale_rows(n):
                act.wait_ge(rstd_ready, n)
                A(row[:, 0, :], h[:, 0, :], ACT.Copy, scale=rstd[:, 0:1]).then_inc(row_ready, 1)

            def drain_transposes(l, stage, gain):
                for i in range(4):
                    wait_tile(act, l, f"{stage}T{i}")
                    b = bank(f"{stage}T{i}")
                    for k in range(2):
                        kk = 2 * i + k
                        ins = A(col[:, kk, :], b[:, k * T:(k + 1) * T], ACT.Copy, scale=cols[:, gain + kk:gain + kk + 1])
                    drained(ins)

            def transposes_upper(l, stage, gain):
                for i in range(4):
                    wait_tile(act, l, f"{stage}T{i}")
                    for k in range(2):
                        kk = 2 * i + k
                        ins = A(colr[:, kk, :], bank(f"{stage}T{i}")[:, k * T:(k + 1) * T], ACT.Copy,
                                scale=cols[:, gain + kk:gain + kk + 1])
                    ins.then_inc(tr_upper, 1)

            act.wait_ge(p_pool, 1)
            for t in range(TT):
                A(row[:, t, :], row[:, t, :], ACT.Copy, scale=rstd[:, 6 + t:7 + t]).then_inc(p_act, 1)
            for i in range(4):
                act.wait_ge(p_pe, i + 1)
                if i == 3:
                    act.sem_inc(row_free, 1)
                A(memraw[:, 2 * i:2 * i + 2, :], banks[i][:, :], ACT.Copy).then_inc(p_act, 1)

            with act.Fori(0, L) as l:
                seq[0] = 0
                scale_rows(1)
                act.wait_ge(cols_landed, 16)
                A(par[:, 0, :], cols[:, C_LDT:C_LDT + 8], ACT.Exp).then_inc(trig_ready, 1)
                drain_transposes(l, "h", C_MIX)
                act.wait_ge(par_ready, 1)
                A(par[:, 6, :], par[:, 1, :], ACT.Exp).then_inc(trig_ready, 1)
                A(par[:, 7, :], par[:, 4, :], ACT.Sin).then_inc(trig_ready, 1)
                A(par[:, 8, :], par[:, 5, :], ACT.Sin).then_inc(trig_ready, 1)
                wait_tile(act, l, "u")
                drained(A(uT[:, :, :], bank("u")[:, :], ACT.Copy))
                wait_tile(act, l, "zA")
                drained(A(z[:, :, 0:256], bank("zA")[:, :].rearrange("p (t n) -> p t n", t=2), ACT.Copy))
                wait_tile(act, l, "zB")
                b = bank("zB")[:, 0:228].rearrange("p (t n) -> p t n", t=2)
                A(z[:, :, 256:352], b[:, :, 0:96], ACT.Copy)
                A(gates, b[:, :, 96:114], ACT.Tanh, scale=0.5)
                drained(A(kwnT[:, :], bank("zB")[:, 228:484], ACT.Copy))
                wait_tile(act, l, "ck")
                for gi in range(2):
                    b = bank("ck")[gi * 64:(gi + 1) * 64, 0:T]
                    A(kc[0:64, 0, gi, :], b, ACT.Copy)
                    ins = A(kc[64:128, 0, gi, 0:255], b[:, 1:256], ACT.Copy)
                drained(ins)
                act.wait_ge(rstd_ready, 2)
                for t in range(TT):
                    A(z[:, t, 0:192], z[:, t, 0:192], ACT.Copy, scale=rstd[:, 2 + t:3 + t])
                A(z[:, 0, 192:320], z[:, 0, 192:320], ACT.Copy, scale=rstd[:, 4:5])
                A(z[:, 1, 192:320], z[:, 1, 192:320], ACT.Copy, scale=rstd[:, 5:6]).then_inc(z_ready, 1)
                wait_tile(act, l, "cqT")
                A(ql[:, 0, :], bank("cqT")[:, 0:256], ACT.Copy, scale=cols[:, C_QN:C_QN + 1])
                drained(A(ql[0:64, 1, :], bank("cqT")[0:64, 256:512], ACT.Copy, scale=cols[0:64, C_QN + 1:C_QN + 2]))
                wait_tile(act, l, "ckvT")
                A(ckvT[:, :], bank("ckvT")[:, 0:256], ACT.Copy, scale=cols[:, C_KVN:C_KVN + 1])
                drained(A(kT[64:96, :, :], bank("ckvT")[64:96, 256:512].unsqueeze(1).broadcast_to([32, NH, T]), ACT.Copy))
                for t in range(TT):
                    wait_tile(act, l, f"qn{t}")
                    drained(A(qrow[:, t, :, 0:64], bank(f"qn{t}")[:, 0:384].rearrange("p (h n) -> p h n", h=NH), ACT.Copy))
                for i in range(3):
                    wait_tile(act, l, f"kn{i}")
                    drained(A(kT[0:64, 2 * i:2 * i + 2, :], bank(f"kn{i}")[0:64, :].rearrange("p (h n) -> p h n", h=2), ACT.Copy))
                for t in range(TT):
                    wait_tile(act, l, f"vm{t}")
                    drained(A(vm[:, t, :], bank(f"vm{t}")[:, 0:384], ACT.Copy))
                wait_drained(act, "hid")
                link(A(hid[:, :, :], hid[:, :, :], ACT.Gelu_apprx_tanh))
                A(hidr[:, :].rearrange("p (g r n) -> p g r n", g=2, r=3),
                  hid[:, 1, :].rearrange("p (g n) -> p g n", g=2).unsqueeze(2).broadcast_to([HD, 2, 3, 16]),
                  ACT.Copy).then_inc(hid_ready, 1)
                for i in range(3):
                    wait_tile(act, l, f"qT{i}")
                    drained(A(qT[:, 2 * i:2 * i + 2, :], bank(f"qT{i}")[0:QK, :].rearrange("p (h n) -> p h n", h=2), ACT.Copy))
                act.wait_ge(cmp_ready, 1)
                A(pc[:, :, :, 0:NCMP], pc[:, :, :, 0:NCMP], ACT.Exp, scale=0.125).then_inc(cexp_ready, 1)
                wait_tile(act, l, "pcT")
                drained(A(pcs[:, :], bank("pcT")[0:96, 0:256], ACT.Copy))

                def exponentials(i):
                    wait_drained(act, f"s{i}")
                    p = prob[:, i % 4, :]
                    A(p[:, 0:128], p[:, 0:128], ACT.Exp, bias=mx[:, 2 * i:2 * i + 1], scale=-1.0,
                      accum_out=sums[:, 2 * i:2 * i + 1])
                    A(p[:, 128:384], p[:, 128:384], ACT.Exp, bias=mx[:, 2 * i + 1:2 * i + 2], scale=-1.0,
                      accum_out=sums[:, 2 * i + 1:2 * i + 2]).then_inc(prob_ready, 1)

                for i in range(LEAD):
                    exponentials(i)
                for i in range(HEADS):
                    if i in MEMK:
                        m = MEMK[i]
                        wait_tile(act, l, f"mk{m}")
                        drained(A(xk[:, 2 * m:2 * m + 2, :], bank(f"mk{m}")[:, :], ACT.Copy))
                    wait_tile(act, l, f"pT{i}")
                    if i >= 2:
                        act.wait_ge(pe_note, i - 1)
                    drained(A(pt[:, i % 2, 0:384], bank(f"pT{i}")[:, 0:384], ACT.Copy))
                    if i + LEAD < HEADS:
                        exponentials(i + LEAD)

                def memory_values(m):
                    for t in range(TT):
                        wait_tile(act, l, f"mv{m}_{t}")
                        drained(A(xv[:, t, m * 512:(m + 1) * 512], bank(f"mv{m}_{t}")[:, :], ACT.Copy))

                act.wait_ge(ys_pre, 2)
                A(uT[:, :, :], uT[:, :, :], ACT.Gelu_apprx_tanh).then_inc(ys_ready, 1)
                layer_chunk_upper(act, l, 15)
                layer_chunk_upper(act, l, 16)
                memory_values(0)
                wait_tile(act, l, "gl")
                drained(A(pt[:, 0, :], bank("gl")[:, :], ACT.Tanh, scale=0.5))
                act.wait_ge(rstd_ready, 3)
                for t in range(TT):
                    for s, (a, n) in enumerate(((0, 256), (256, 384), (640, 384))):
                        ins = A(row[:, t, a:a + n], row[:, t, a:a + n], ACT.Copy, scale=rstd[:, 2 * s + t:2 * s + t + 1])
                    ins.then_inc(row_ready, 1)
                memory_values(1)
                transposes_upper(l, "y", C_OUT)
                for c in range(17, 21):
                    layer_chunk_upper(act, l, c)
                scale_rows(4)
                transposes_upper(l, "x", C_XN)
                for i in range(XH):
                    wait_tile(act, l, f"xq{i}")
                    drained(A(xq[:, 2 * i:2 * i + 2, :], bank(f"xq{i}")[:, :], ACT.Copy))
                    if i < 3:
                        layer_chunk_upper(act, l, 21 + i)
                for i in range(XH):
                    act.wait_ge(xmax_ready, i + 1)
                    if i == 3:
                        wait_tile(act, l, "xp0")
                    for t in range(TT):
                        ins = A(xprob[:, i % 3, t * T:(t + 1) * T], bank(f"xs{i}")[:, t * T:(t + 1) * T], ACT.Exp,
                                bias=xnm[:, 2 * i + t:2 * i + t + 1], scale=0.0625, accum_out=xsum[:, 2 * i + t:2 * i + t + 1])
                    drained(ins)
                layer_chunk_upper(act, l, 24)
                for i in range(XH):
                    wait_tile(act, l, f"xo{i}")
                    A(xor[:, 2 * i:2 * i + 2, :], bank(f"xo{i}")[:, :], ACT.Copy).then_inc(tr_upper, 1)
                layer_chunk_upper(act, l, 25)
                layer_chunk_upper(act, l, 26)

                def features():
                    scale_rows(5)
                    drain_transposes(l, "f", C_FFN)

                def features_and_weights():
                    features()
                    act.wait_ge(route, 3)
                    A(wd[:, 0:2], wd[:, 0:2], ACT.Exp).then_inc(route, 1)

                with act.If(l == 0):
                    dense_act(act, features)
                with act.Else():
                    moe_act(act, moe[0], weights_used, RING + MOE_FIRST, landed, MOE_FIRST, features_and_weights)
                act.drain().then_inc(arrived, 1)
                act.wait_ge(go, l + 1)

            act.wait_ge(flag_again, 1)
            v = act.value_load(flag[0:1, 0:1], min_val=0, max_val=1)
            with act.If(v == 1):
                moe_act(act, moe[1], moe[1]["used"], RING, landed2, 0, lambda: None)
            with act.Else():
                act.nop()
            act.wait_ge(f_pool, 1)
            for t in range(TT):
                A(row[:, t, :], h[:, t, :], ACT.Copy, scale=rstd[:, t:t + 1]).then_inc(f_act, 1)

        @block.vector
        def _(dve):
            seq = [0]

            def link(ins):
                seq[0] += 1
                ins.then_inc(dve_seq, 1)
                dve.wait_ge(dve_seq, seq[0])

            def drained(ins):
                ins.then_inc(dve_drained, 1)

            def settled(name):
                dve.wait_ge(dve_drained, DRAINS["dve"].index(name) + 1)

            def tt(out, a, b, op):
                return dve.tensor_tensor(out, a, b, op)

            def squares(src, junk, to):
                return dve.tensor_tensor_reduce(junk, src, src, 1.0, 0.0, ALU.mult, ALU.add, to)

            def mean_eps(a, n, width):
                return dve.tensor_scalar(ss[:, a:a + n], ss[:, a:a + n], 1.0 / width, EPS, ALU.mult, ALU.add)

            def norm_h(junk):
                for t in range(TT):
                    ins = squares(h[:, t, :], junk[:, t * D:(t + 1) * D], ss[:, t:t + 1])
                link(ins)
                mean_eps(0, 2, D).then_inc(ss_ready, 1)

            def scale_rows(n):
                dve.wait_ge(rstd_ready, n)
                dve.tensor_scalar(row[:, 1, :], h[:, 1, :], rstd[:, 1:2], None, ALU.mult).then_inc(row_ready, 1)

            for ap, v in ((ql[64:128, 1, :], 0.0), (hid[:, :, :], 0.0), (pc[:, :, :, :], 0.0),
                          (xc[:, :, :, :], NEG)):
                dve.memset(ap, v)
            dve.wait_ge(mem_landed, 16)
            for t in range(TT):
                ins = squares(row[:, t, :], xvf[:, t * D:(t + 1) * D], ss[:, 6 + t:7 + t])
            ins.then_inc(p_dve, 1)
            dve.wait_ge(p_dve, 1)
            mean_eps(6, 2, D).then_inc(p_dve, 1)
            dve.wait_ge(bias_landed, 32)
            dve.tensor_scalar(bigf[0:33, 512:518], bigf[0:33, 512:518], 8.0, None, ALU.mult).then_inc(p_dve, 1)
            dve.wait_ge(p_dve, 3)
            dve.tensor_copy(bigf[0:33, 640:1408].rearrange("p (h n) -> p h n", h=NH),
                            bigf[0:33, 512:518].unsqueeze(2).broadcast_to([33, NH, P])).then_inc(p_dve, 1)
            for hh in range(NH):
                dve.wait_ge(p_pe, 4 + hh + 1)
                dve.tensor_copy(bigf[:, 1408 + hh * 384:1408 + (hh + 1) * 384], banks[4 + hh % 4][:, 0:384]).then_inc(p_dve, 1)
            dve.wait_ge(x_landed, 16)

            with dve.Fori(0, L) as l:
                seq[0] = 0
                norm_h(xvf)
                dve.wait_ge(row_free, 1)
                scale_rows(1)
                q = [par[:, i, :] for i in range(16)]
                dt_, x1, th, kk, red, ab, mag, sn, cn, abr, abi, den, nr, fr, fi, tmp = q
                lr, li = cols[:, C_ARE:C_ARE + 8], cols[:, C_AIM:C_AIM + 8]
                dve.wait_ge(trig_ready, 1)
                tt(x1, lr, dt_, ALU.mult)
                link(tt(th, li, dt_, ALU.mult))
                magic = 12582912.0
                link(dve.tensor_scalar(kk, th, 1.0 / (2 * math.pi), magic, ALU.mult, ALU.add))
                link(dve.tensor_scalar(kk, kk, -magic, None, ALU.add))
                c1 = 6.28125
                c2 = float(np.float32(np.round((2 * math.pi - c1) * 2 ** 20) / 2 ** 20))
                c3 = 2 * math.pi - c1 - c2
                link(dve.scalar_tensor_tensor(red, kk, -c1, th, ALU.mult, ALU.add))
                link(dve.scalar_tensor_tensor(red, kk, -c2, red, ALU.mult, ALU.add))
                link(dve.scalar_tensor_tensor(red, kk, -c3, red, ALU.mult, ALU.add))
                link(dve.tensor_scalar(red, red, 3.1415925, -3.1415925, ALU.min, ALU.max))
                link(dve.tensor_scalar(ab, red, -1.0, None, ALU.mult))
                link(tt(ab, ab, red, ALU.min))
                dve.tensor_scalar(ab, ab, 1.0, math.pi / 2, ALU.mult, ALU.add).then_inc(par_ready, 1)
                tt(den, lr, lr, ALU.mult)
                link(tt(tmp, li, li, ALU.mult))
                link(tt(den, den, tmp, ALU.add))
                link(dve.reciprocal(den, den))
                dve.wait_ge(trig_ready, 4)
                tt(abr, mag, cn, ALU.mult)
                link(tt(abi, mag, sn, ALU.mult))
                link(dve.tensor_scalar(nr, abr, -1.0, None, ALU.add))
                tt(fr, nr, lr, ALU.mult)
                link(tt(tmp, abi, li, ALU.mult))
                link(tt(fr, fr, tmp, ALU.add))
                link(tt(fr, fr, den, ALU.mult))
                tt(fi, abi, lr, ALU.mult)
                link(tt(tmp, nr, li, ALU.mult))
                link(tt(fi, fi, tmp, ALU.subtract))
                link(tt(fi, fi, den, ALU.mult))
                dve.wait_ge(lp_landed, 16)
                frb, fib = (f.unsqueeze(2).broadcast_to([P, 8, 32]) for f in (fr, fi))
                t0 = pt[:, 0, 0:256].rearrange("p (j n) -> p j n", j=8)
                t1 = pt[:, 1, 0:256].rearrange("p (j n) -> p j n", j=8)
                tt(cp[:, 0], ct[:, 0], frb, ALU.mult)
                tt(t0, ct[:, 1], fib, ALU.mult)
                tt(cp[:, 1], ct[:, 0], fib, ALU.mult)
                link(tt(t1, ct[:, 1], frb, ALU.mult))
                tt(cp[:, 0], cp[:, 0], t0, ALU.subtract)
                dve.scalar_tensor_tensor(cp[:, 1], cp[:, 1], -1.0, t1, ALU.mult, ALU.subtract).then_inc(ct_ready, 1)
                link(dve.memset(kc[:, :, 2, :], 0.0))
                dve.tensor_copy(kc[:, :, 2, 0:32:2], cols[:, C_PE:C_PE + 32].rearrange("p (v m) -> p v m", v=2))

                wait_drained(dve, "zB")
                for t in range(TT):
                    squares(z[:, t, 0:192], pt[:, 0, t * 192:(t + 1) * 192], ss[:, 2 + t:3 + t])
                for t in range(TT):
                    ins = squares(z[:, t, 192:320], pt[:, 1, t * 128:(t + 1) * 128], ss[:, 4 + t:5 + t])
                link(ins)
                mean_eps(2, 2, 192)
                mean_eps(4, 2, 128).then_inc(ss_ready, 1)
                link(dve.tensor_scalar(gates, gates, 1.0, 0.5, ALU.add, ALU.mult))
                dve.memset(krp[:, :, 0:64], 0.0)

                def rotate(out, x1, x2, c, s, shape):
                    n = shape[1]
                    a, b = (rt[:, i, 0:n * 16].rearrange("p (h n) -> p h n", h=n) for i in range(2))
                    tt(a, x1, c, ALU.mult)
                    link(tt(b, x2, s, ALU.mult))
                    link(tt(out[0], a, b, ALU.subtract))
                    tt(a, x2, c, ALU.mult)
                    link(tt(b, x1, s, ALU.mult))
                    return tt(out[1], a, b, ALU.add)

                rotate((krp[:, :, 64:80], krp[:, :, 80:96]), z[:, :, 320:336], z[:, :, 336:352], cos2, sin2,
                       [P, 2, 16]).then_inc(rope_ready, 1)

                dve.memset(qz[64:128, 0:3, :], 0.0)
                dve.memset(qz[0:64, 3:6, :], 0.0)
                wait_tile(dve, l, "q0")
                b = bank("q0")[:, :].rearrange("p (m n) -> p m n", m=2)
                dve.tensor_copy(qz[0:64, 0:2, :], b[0:64])
                drained(dve.tensor_copy(qz[64:128, 3:5, :], b[64:128]))
                wait_tile(dve, l, "q1")
                dve.tensor_copy(qz[0:64, 2, :], bank("q1")[0:64, 0:256])
                dve.tensor_copy(qz[64:128, 5, :], bank("q1")[64:128, 0:256])
                drained(dve.tensor_copy(kslT[:, :], bank("q1")[:, 256:512]))
                wait_tile(dve, l, "cv")
                for gi in range(2):
                    b = bank("cv")[gi * 64:(gi + 1) * 64, 0:T]
                    dve.tensor_copy(kc[0:64, 1, gi, :], b)
                    ins = dve.tensor_copy(kc[64:128, 1, gi, 0:255], b[:, 1:256])
                drained(ins)
                wait_tile(dve, l, "vs")
                drained(dve.tensor_copy(vs[:, :, :], bank("vs")[:, :].rearrange("p (t n) -> p t n", t=2)))
                wait_tile(dve, l, "hid")
                b = bank("hid")
                for v in range(2):
                    ins = dve.tensor_copy(rt[0:64, 0, v:v + 1], b[0:64, v * 45 + 30:v * 45 + 31])
                link(ins)
                for v in range(2):
                    ins = dve.tensor_scalar(hid[:, v, :].rearrange("p (g n) -> p g n", g=2)[:, :, 0:NCMP],
                                            b[0:64, v * 45:v * 45 + 30].rearrange("p (g n) -> p g n", g=2),
                                            rt[0:64, 0, v:v + 1], None, ALU.add)
                drained(ins)
                for t in range(TT):
                    settled(("hid", "qr0")[t])
                    wait_tile(dve, l, f"qr{t}")
                    b = bank(f"qr{t}")[:, 0:192].rearrange("p (h n) -> p h n", h=NH)
                    c, s = (x[:, t, :].unsqueeze(1).broadcast_to([P, NH, 16]) for x in (cos2, sin2))
                    drained(rotate((qrow[:, t, :, 64:80], qrow[:, t, :, 80:96]), b[:, :, 0:16], b[:, :, 16:32], c, s, [P, NH, 16]))
                wait_tile(dve, l, "kcv")
                b = bank("kcv")
                dve.tensor_copy(kcT[:, :], b[:, 0:16])
                drained(tt(vbd[:, :].rearrange("p (h n) -> p h n", h=NH), b[0:96, 16:80].unsqueeze(1).broadcast_to([96, NH, 64]),
                           cs("vcm")[0:96, :].unsqueeze(2).broadcast_to([96, NH, 64]), ALU.mult))
                dve.wait_ge(s_scr, 32)
                wait_tile(dve, l, "sc")
                b = bank("sc")[:, 0:192].rearrange("p (t h n) -> p t h n", t=2, h=NH)
                tt(xc[:, 0, :, 0:7], b[:, 0, :, 0:7], btab[:, :, 159:256:CSTRIDE], ALU.add)
                ins = tt(xc[:, 1, :, 0:NCMP], b[:, 1, :, 0:NCMP], btab[:, :, 31:256:CSTRIDE], ALU.add)
                drained(ins)
                settled("sc")
                cmx3 = cmx.rearrange("p (t h) -> p t h", t=2)
                csum3 = csum.rearrange("p (t h) -> p t h", t=2)
                link(dve.tensor_reduce(cmx3, xc[:, :, :, 0:NCMP], AX.X, ALU.max))
                tt(pc[:, :, :, 0:NCMP], xc[:, :, :, 0:NCMP], cmx3.unsqueeze(3).broadcast_to([P, TT, NH, NCMP]),
                   ALU.subtract).then_inc(cmp_ready, 1)
                dve.wait_ge(cexp_ready, 1)
                link(dve.tensor_reduce(csum3, pc[:, :, :, 0:NCMP], AX.X, ALU.add))
                link(dve.reciprocal(csum, csum))
                link(tt(csum3, csum3, gates[:, :, 0:NH], ALU.mult))
                link(tt(csum3, csum3, cs("okc").unsqueeze(2).broadcast_to([P, TT, NH]), ALU.mult))
                wait_tile(dve, l, "qT2")
                for t in range(TT):
                    wait_tile(dve, l, f"oc{t}")
                    drained(tt(row[:, t, 640:1024].rearrange("p (h n) -> p h n", h=NH),
                               bank(f"oc{t}")[:, 0:384].rearrange("p (h n) -> p h n", h=NH),
                               csum3[:, t, :].unsqueeze(2).broadcast_to([P, NH, 64]), ALU.mult))

                def masked_scores(i):
                    wait_tile(dve, l, f"s{i}")
                    if i >= 4:
                        wait_tile(dve, l, f"pT{i - 4}")
                    b, p = bank(f"s{i}"), prob[:, i % 4, :]
                    m = cmask if i < NH else btab[:, i % NH, :]
                    sc = -float(QK) ** -0.5 if i < NH else -float(HD) ** -0.5
                    dve.tensor_tensor_reduce(p[:, 0:128], b[:, 0:128], m[:, 128:256], sc, 3.0e38, ALU.add, ALU.min,
                                             mx[:, 2 * i:2 * i + 1])
                    drained(dve.tensor_tensor_reduce(p[:, 128:384], b[:, 128:384], m, sc, 3.0e38, ALU.add, ALU.min,
                                                     mx[:, 2 * i + 1:2 * i + 2]))

                def states(j):
                    wait_tile(dve, l, f"bu{j}")
                    if j == 0:
                        dve.wait_ge(ftab_ready, 1)
                    b = bank(f"bu{j}")[:, :].rearrange("p (c n) -> p c n", c=2)
                    f0, f1 = (ftab[:, c, j, :].unsqueeze(1).broadcast_to([P, 2, T]) for c in range(2))
                    if j >= 2:
                        dve.wait_ge(g_free, j - 1)
                    gg = g[:, j % 2]
                    tt(tmpd[:, 0:2, :], b, f0, ALU.mult)
                    drained(tt(tmpd[:, 2:4, :], b, f1, ALU.mult))
                    settled(f"bu{j}")
                    tt(gg[:, 0, :], tmpd[:, 0, :], tmpd[:, 3, :], ALU.add)
                    link(tt(gg[:, 1, :], tmpd[:, 1, :], tmpd[:, 2, :], ALU.subtract))
                    for c in range(2):
                        ins = dve.tensor_tensor_scan(gg[:, c, :], mag[:, j:j + 1].broadcast_to([P, T]), gg[:, c, :], 0.0,
                                                     ALU.mult, ALU.add)
                    ins.then_inc(scan_ready, 1)

                def group_outputs(n):
                    dve.wait_ge(prob_ready, NH * (n + 1))
                    s3 = sums[:, 12 * n:12 * n + 12].rearrange("p (h t) -> p t h", t=2)
                    r3 = rinv[:, 12 * n:12 * n + 12].rearrange("p (t h) -> p t h", t=2)
                    link(dve.reciprocal(r3, s3))
                    if n:
                        link(tt(r3, r3, gates[:, :, n * NH:(n + 1) * NH], ALU.mult))
                    dve.wait_ge(pe_note, NH * (n + 1))
                    for t in range(TT):
                        o = ob[t][:, 0:384].rearrange("p (h n) -> p h n", h=NH)
                        w = r3[:, t, :].unsqueeze(2).broadcast_to([P, NH, 64])
                        a = (256, 640, 640)[n]
                        to = row[:, t, a:a + 384]
                        if n == 0:
                            tt(to.rearrange("p (h n) -> p h n", h=NH), o, w, ALU.mult).then_inc(o_read, 1)
                        else:
                            x = tmpdf[:, t * 512:t * 512 + 384]
                            tt(x.rearrange("p (h n) -> p h n", h=NH), o, w, ALU.mult).then_inc(o_read, 1)
                            dve.wait_ge(o_read, TT * n + t + 1)
                            link(tt(to, to, x, ALU.add))

                for i in range(LEAD):
                    masked_scores(i)
                for i in range(HEADS):
                    if i + LEAD < HEADS:
                        masked_scores(i + LEAD)
                    if i in STATES:
                        states(STATES[i])
                    if i in (NH, 2 * NH):
                        group_outputs(i // NH - 1)
                group_outputs(2)

                dve.wait_ge(g_free, 8)
                for c in range(2):
                    dve.scalar_tensor_tensor(uT[:, c, :], uT[:, c, :], cols[:, C_D + c:C_D + c + 1], yb[:, c * T:(c + 1) * T],
                                             ALU.mult, ALU.add).then_inc(ys_pre, 1)
                layer_chunk_lower(dve, 15)
                layer_chunk_lower(dve, 16)
                wait_tile(dve, l, "yr")
                wait_drained(dve, "gl")
                y3 = row[:, :, 0:256]
                drained(dve.scalar_tensor_tensor(y3, pt[:, 0, :].rearrange("p (t n) -> p t n", t=2), 1.0, bank("yr")[:, :].rearrange("p (t n) -> p t n", t=2),
                                                 ALU.add, ALU.mult))
                settled("yr")
                link(dve.tensor_scalar(y3, y3, 0.5, None, ALU.mult))
                for s, (a, n) in enumerate(((0, 256), (256, 384), (640, 384))):
                    for t in range(TT):
                        ins = squares(row[:, t, a:a + n], w1f[:, t * D + a:t * D + a + n], ss[:, 2 * s + t:2 * s + t + 1])
                link(ins)
                mean_eps(0, 2, 256)
                mean_eps(2, 4, 384).then_inc(ss_ready, 1)

                def transposes_lower(stage, gain, n):
                    for i in range(4):
                        dve.wait_ge(tr_upper, n + i + 1)
                        for k in range(2):
                            kk = 2 * i + k
                            ins = dve.scalar_tensor_tensor(xor[:, kk, :], bank(f"{stage}T{i}")[:, k * T:(k + 1) * T],
                                                           cols[:, gain + kk:gain + kk + 1], f32(colr[:, kk, :]),
                                                           ALU.mult, ALU.subtract)
                        drained(ins)

                def add_to_h(stage, chunks):
                    for n in range(2):
                        for c in chunks[n]:
                            layer_chunk_lower(dve, c)
                        for t in range(TT):
                            wait_tile(dve, l, f"{stage}{n}_{t}")
                            hs = h[:, t, n * 512:(n + 1) * 512]
                            drained(tt(hs, hs, bank(f"{stage}{n}_{t}")[:, :], ALU.add))
                            settled(f"{stage}{n}_{t}")
                            ins = squares(hs, w1f[:, t * D + n * 512:t * D + (n + 1) * 512], ssh[:, 2 * n + t:2 * n + t + 1])
                    link(ins)
                    link(tt(ss[:, 0:2], ssh[:, 0:2], ssh[:, 2:4], ALU.add))
                    mean_eps(0, 2, D).then_inc(ss_ready, 1)

                transposes_lower("y", C_OUT, 0)
                add_to_h("wo", ((17,), (18, 19)))
                scale_rows(4)
                layer_chunk_lower(dve, 20)
                transposes_lower("x", C_XN, 4)
                for c in (21, 22, 23):
                    layer_chunk_lower(dve, c)
                for i in range(XH):
                    wait_tile(dve, l, f"xs{i}")
                    link(dve.tensor_reduce(xmx[:, 2 * i:2 * i + 2], bank(f"xs{i}")[:, :].rearrange("p (t n) -> p t n", t=2),
                                           AX.X, ALU.max))
                    dve.tensor_scalar(xnm[:, 2 * i:2 * i + 2], xmx[:, 2 * i:2 * i + 2], -0.0625, None,
                                      ALU.mult).then_inc(xmax_ready, 1)
                def over_sums(i):
                    wait_drained(dve, f"xs{i}")
                    link(dve.reciprocal(xri[:, 2 * i:2 * i + 2], xsum[:, 2 * i:2 * i + 2]))
                    for t in range(TT):
                        p = xprob[:, i % 3, t * T:(t + 1) * T]
                        ins = dve.tensor_scalar(p, p, xri[:, 2 * i + t:2 * i + t + 1], None, ALU.mult)
                    ins.then_inc(xprob_ready, 1)

                def probabilities_drain(i):
                    wait_tile(dve, l, f"xp{i}")
                    if i >= 2:
                        wait_tile(dve, l, f"xo{i - 2}")
                    drained(dve.tensor_copy(pt[:, i % 2, :], bank(f"xp{i}")[:, :]))

                for i in range(3):
                    over_sums(i)
                probabilities_drain(0)
                over_sums(3)
                for i in range(XH):
                    if i + 1 < XH:
                        probabilities_drain(i + 1)
                    if i == 0:
                        layer_chunk_lower(dve, 24)
                    dve.wait_ge(tr_upper, 8 + i + 1)
                    drained(dve.tensor_tensor(colr[:, 2 * i:2 * i + 2, :].rearrange("p k n -> p (k n)"), bank(f"xo{i}")[:, :],
                                              f32(xor[:, 2 * i:2 * i + 2, :]).rearrange("p k n -> p (k n)"), ALU.subtract))
                add_to_h("xw", ((25,), (26,)))
                scale_rows(5)

                with dve.If(l == 0):
                    dense_dve(dve)
                with dve.Else():
                    moe_dve(dve, moe[0], 0, MOE_FIRST, lambda: route_on_dve(dve))
                dve.drain().then_inc(arrived, 1)
                dve.wait_ge(go, l + 1)

            dve.sem_inc(flag_again, 1)
            v = dve.value_load(flag[0:1, 0:1], min_val=0, max_val=1)
            with dve.If(v == 1):
                moe_dve(dve, moe[1], 1, 0, lambda: None)
            with dve.Else():
                dve.nop()
            for t in range(TT):
                squares(h[:, t, :], bigf[:, t * D:(t + 1) * D], ss[:, t:t + 1]).then_inc(f_dve, 1)
            dve.wait_ge(f_dve, 2)
            mean_eps(0, 2, D).then_inc(f_dve, 1)
            dve.wait_ge(fg_landed, 16)
            fg = memraw[:, 0:4, :].rearrange("p k n -> p (k n)")
            for t in range(TT):
                dve.wait_ge(f_act, t + 1)
                tt(row[:, t, :], row[:, t, :], fg, ALU.mult).then_inc(final_ready, 1)

        @block.gpsimd
        def _(pool):
            seq = [0]

            def link(ins):
                seq[0] += 1
                ins.then_inc(pool_seq, 1)
                pool.wait_ge(pool_seq, seq[0])

            def tt(out, a, b, op):
                return pool.tensor_tensor(out, a, b, op)

            def power(a, n, counter):
                tt(rstd[:, a:a + n], ss[:, a:a + n], half[:, 0:1].broadcast_to([P, n]), ALU.pow).then_inc(counter, 1)

            pool.wait_ge(cst_landed, 16)
            pool.wait_ge(p_dve, 2)
            power(6, 2, p_pool)

            with pool.Fori(0, L) as l:
                seq[0] = 0
                pool.wait_ge(ss_ready, 1)
                power(0, 2, rstd_ready)
                pool.wait_ge(s_scr, 16)
                pool.wait_ge(trig_ready, 4)
                re, im = ftab[:, 0], ftab[:, 1]
                pool.tensor_copy(re[:, :, 0:1], par[:, 8, :].unsqueeze(2))
                link(pool.tensor_copy(im[:, :, 0:1], par[:, 7, :].unsqueeze(2)))

                def double(m):
                    a, b = (f[:, :, m - 1:m].broadcast_to([P, 8, m]) for f in (re, im))
                    x = xkf[:, 0:8 * m].rearrange("p (j n) -> p j n", j=8)
                    y = xkf[:, 1024:1024 + 8 * m].rearrange("p (j n) -> p j n", j=8)
                    tt(re[:, :, m:2 * m], re[:, :, 0:m], a, ALU.mult)
                    tt(x, im[:, :, 0:m], b, ALU.mult)
                    tt(im[:, :, m:2 * m], re[:, :, 0:m], b, ALU.mult)
                    link(tt(y, im[:, :, 0:m], a, ALU.mult))
                    tt(re[:, :, m:2 * m], re[:, :, m:2 * m], x, ALU.subtract)
                    return tt(im[:, :, m:2 * m], im[:, :, m:2 * m], y, ALU.add)

                for m in (1, 2, 4, 8, 16, 32):
                    link(double(m))
                pool.wait_ge(ss_ready, 2)
                power(2, 4, rstd_ready)
                link(double(64))
                double(128).then_inc(ftab_ready, 1)
                wait_tile(pool, l, "vs")
                pool.sem_inc(pool_note, 1)
                for k in range(KD):
                    pool.tensor_scalar(memT[:, k, :], memraw[:, k, :], cols[:, C_MEM + k:C_MEM + k + 1], None,
                                       ALU.mult).then_inc(memT_ready, 1)
                for j in range(8):
                    pool.wait_ge(scan_ready, j + 1)
                    gg = g[:, j % 2]
                    f0, f1 = (ftab[:, c, j, :].unsqueeze(1).broadcast_to([P, 2, T]) for c in range(2))
                    tt(tmpp[:, 0:2, :], gg, f0, ALU.mult)
                    link(tt(tmpp[:, 2:4, :], gg, f1, ALU.mult))
                    tt(gg[:, 0, :], tmpp[:, 0, :], tmpp[:, 3, :], ALU.subtract)
                    link(tt(gg[:, 1, :], tmpp[:, 1, :], tmpp[:, 2, :], ALU.add))
                    pool.sem_inc(state_ready, 1)
                pool.wait_ge(ss_ready, 3)
                power(0, 6, rstd_ready)
                pool.wait_ge(ss_ready, 4)
                power(0, 2, rstd_ready)
                pool.wait_ge(ss_ready, 5)
                power(0, 2, rstd_ready)
                with pool.If(l == 0):
                    pool.wait_ge(act_drained, len(DRAINS["act"]))
                    pool.dma_start(lp[:, :], lparams[1]).then_inc(next_lp_landed, 16)
                    pool.wait_ge(next_lp_landed, 16)
                with pool.Else():
                    pool.nop()
                pool.wait_ge(arrived, 3 * l + 3)
                pool.sem_inc(pool_note, 1)
                pool.sem_clear(clear_range)
                pool.sem_inc(go, 1)

            pool.dma_start(memraw[:, 0:4, :].rearrange("p k n -> p (k n)"), fgain.broadcast_to([P, D])).then_inc(fg_landed, 16)
            pool.wait_ge(f_dve, 3)
            power(0, 2, f_pool)
            pool.wait_ge(fg_landed, 16)


def constants():
    c = np.zeros((P, CSW), np.float32)

    def put(name, a):
        at, w = CS[name]
        c[:a.shape[0], at:at + w] = a

    p = np.arange(P)
    put("ident", np.eye(P, dtype=np.float32))
    causal = np.zeros((P, 256), np.float32)
    causal[:, 128:] = np.where(p[None, :] <= p[:, None], 0.0, NEG)
    put("cmask", causal)
    pos = np.arange(T, dtype=np.float32)
    inv = (1.0 / (np.float32(10000.0) ** (np.arange(0, ROPE, 2, dtype=np.float32) / np.float32(ROPE)))).astype(np.float32)
    ang = (pos[:, None] * inv[None, :]).astype(np.float32)
    rope = np.concatenate([f(ang).astype(np.float32).reshape(TT, P, 16).transpose(1, 0, 2).reshape(P, 32)
                           for f in (np.cos, np.sin)], axis=1)
    put("rope", rope)
    put("before", (p[:, None] < p[None, :]).astype(np.float32))
    put("ones", np.ones((P, P), np.float32))
    put("iota", np.broadcast_to(np.arange(256, dtype=np.float32), (P, 256)))
    put("iota8", np.broadcast_to(np.arange(8, dtype=np.float32), (P, 8)))
    put("okc", np.stack([(p >= 31), np.ones(P)], axis=1).astype(np.float32))
    put("vcm", (p[:96, None] // 16 == np.arange(NH)[None, :]).astype(np.float32))
    put("half", np.full((P, 4), -0.5, np.float32))
    dist = 255 - np.arange(384)
    exact = BUCKETS // 2
    n = np.maximum(dist, 0)
    nf = np.maximum(n, exact).astype(np.float32)
    large = exact + (np.log(nf / np.float32(exact)) / np.float32(math.log(MAX_DIST / exact)) * np.float32(BUCKETS - exact)).astype(np.int32)
    bucket = np.where(n < exact, n, np.minimum(large, BUCKETS - 1))
    one = np.zeros((33, 512), np.float32)
    one[np.where(dist >= 0, bucket, 32), np.arange(384)] = 1.0
    return c, one


def blocks(w):
    return w.reshape(-1, P, w.shape[-1]).transpose(1, 0, 2)


def pack_weights(a):
    out = np.zeros((CHUNKS, P, SLOT), np.float32)
    c = 0

    def put(x):
        nonlocal c
        x = x.reshape(P, -1)
        out[c, :, :x.shape[1]] = x
        c += 1

    def put_pair(w, n):
        b = blocks(w[:, n * 512:(n + 1) * 512])
        put(b[:, 0:4])
        put(b[:, 4:8])

    def ffn(wg, wu, wd, pieces):
        def gu(i):
            s = slice(i * PIECE, (i + 1) * PIECE)
            b = np.concatenate([blocks(wg[:, s]), blocks(wu[:, s])], axis=2)
            put(b[:, 0:4])
            put(b[:, 4:8])

        def down(i):
            put(blocks(wd[i * PIECE:(i + 1) * PIECE]))

        gu(0)
        for i in range(pieces - 1):
            gu(i + 1)
            down(i)
        down(pieces - 1)

    for l in range(L):
        w = a["w_in"][l]
        kv = 992

        def take(*ranges):
            x = np.concatenate([w[:, s:e] for s, e in ranges], axis=1)
            if x.shape[1] < 256:
                x = np.concatenate([x, np.zeros((D, 256 - x.shape[1]), np.float32)], axis=1)
            put(blocks(x))

        def q(i):
            return 608 + i * 64, 608 + (i + 1) * 64

        take((0, 256))
        take((256, 512))
        take((512, 608), (1760, 1778), (kv + 512, kv + 640))
        take(q(0), q(3), q(1), q(4))
        take(q(2), q(5), (kv + 256, kv + 384))
        take((kv, kv + 256))
        take((kv + 384, kv + 512), (kv + 640, kv + 768))
        wkv = a["xattn_wkv"][l]
        for i in range(XH):
            put(blocks(wkv[:, i * 256:(i + 1) * 256]))
        for n in range(2):
            put_pair(wkv[:, D:], n)
        for n in range(2):
            put_pair(a["w_out"][l], n)
        for i in range(XH):
            put(blocks(a["xattn_wq"][l][:, i * 256:(i + 1) * 256]))
        for n in range(2):
            put_pair(a["xattn_wo"][l], n)
        if l % 2 == 0:
            ffn(a["dense_w_gate"][l // 2], a["dense_w_up"][l // 2], a["dense_w_down"][l // 2], DENSE_PIECES)
        else:
            for e in range(NE):
                ffn(a["moe_w_gate"][l // 2][e], a["moe_w_up"][l // 2][e], a["moe_w_down"][l // 2][e], MOE_PIECES)
    assert c == CHUNKS
    return out


def pack_layer(a, l):
    out = np.zeros((P, LPW), np.float32)

    def put(name, x, off=0):
        at, w = LP[name]
        x = x.reshape(x.shape[0], -1)
        out[:x.shape[0], at + off:at + off + x.shape[1]] = x

    def column(x):
        return x.reshape(-1, P).T

    c = LP["cols"][0]
    for at, name in ((C_MIX, "mix_norm"), (C_OUT, "out_norm"), (C_XN, "xattn_norm"), (C_MEM, "mem_norm"), (C_FFN, "ffn_norm"),
                     (C_ARE, "ssm_a_re"), (C_AIM, "ssm_a_im"), (C_D, "ssm_d"), (C_KVN, "mla_kv_norm")):
        x = column(a[name][l])
        out[:, c + at:c + at + x.shape[1]] = x
    out[:, c + C_LDT:c + C_LDT + 8] = column(np.repeat(a["ssm_log_dt"][l], 64))
    qn = a["mla_q_norm"][l]
    out[:, c + C_QN] = qn[:P]
    out[:64, c + C_QN + 1] = qn[P:]
    for v in range(2):
        out[:, c + C_PE + v * NPAIR:c + C_PE + (v + 1) * NPAIR] = column(a["nsa_cmp_pe"][l, v])
        put("w1", blocks(a["nsa_cmp_w1"][l, v]), v * NPAIR * 64)
        put("w2", a["nsa_cmp_w2"][l, v], v * 64)
    put("glu", blocks(a["ssm_w_glu"][l]))
    uq = a["mla_w_uq"][l].reshape(192, NH, QK)
    uq = np.concatenate([uq[:, :, :NOPE].reshape(192, -1), uq[:, :, NOPE:].reshape(192, -1)], axis=1)
    put("uq", uq[:P])
    put("uq", uq[P:], 576)
    ukv = a["mla_w_ukv"][l].reshape(P, NH, 2, 64)
    put("ukv", ukv[:, :, 0].reshape(P, -1))
    put("ukv", ukv[:, :, 1].reshape(P, -1), 384)
    bt = np.zeros((P, 8, 2, P), np.float32)
    ct = np.zeros((P, 2, 8, 32), np.float32)
    for gi in range(16):
        j, s = gi // 2, (gi % 2) * 64
        r = 16 * (gi % 8)
        o = 16 * (gi % 2)
        for i, (bn, cn) in enumerate((("ssm_b_re", "ssm_c_re"), ("ssm_b_im", "ssm_c_im"))):
            bt[r:r + 16, j, i, s:s + 64] = a[bn][l, gi].T
            ct[s:s + 64, i, j, o:o + 16] = a[cn][l, gi].T
    put("bt", bt)
    put("ct", ct)
    return out


def kernel(**inputs):
    import concourse.bacc as bacc
    from concourse.bass_utils import run_bass_kernel_spmd

    a = {k: np.asarray(v) for k, v in inputs.items()}
    cst, onehot = constants()
    at, w = CS["router"]
    cst[:, at:at + w] = blocks(a["moe_router"][0]).reshape(P, w)
    relb = np.concatenate([a["rel_bias"], np.full((1, NH), NEG / 8, np.float32)], axis=0)
    arrays = {
        "x": np.ascontiguousarray(a["x"][0]), "mem": np.ascontiguousarray(a["mem"][0]),
        "weights": pack_weights(a), "lparams": np.stack([pack_layer(a, l) for l in range(L)]),
        "consts": cst, "onehot": onehot, "relb": relb, "fgain": a["final_norm"][None, :],
    }
    nc = bacc.Bacc("TRN2", target_bir_lowering=False, num_devices=1)
    t = {k: nc.dram_tensor(f"in_{k}", v.shape, F32, kind="ExternalInput").ap() for k, v in arrays.items()}
    out = nc.dram_tensor("out_0", (T, D), F32, kind="ExternalOutput").ap()
    scratch = nc.dram_tensor("skewed_bias", (NH, P, 384), F32, kind="Internal").ap()
    trunk(nc, t["x"], t["mem"], t["weights"], t["lparams"], t["consts"], t["onehot"], t["relb"], t["fgain"], out, scratch)
    r = run_bass_kernel_spmd(nc, [{f"in_{k}": v for k, v in arrays.items()}], core_ids=[0])
    return r.results[0]["out_0"].reshape(1, T, D)
```
